# Optimizing a Trainium2 kernel written in Bass

```python
import math
import jax, jax.numpy as jnp
from jax import lax
import numpy as np

D_MODEL = 1024
BATCH = 1
SEQ = 256
DEPTH = 1

SSM_WIDTH = D_MODEL // 2
SSM_GROUP = 16
SSM_GROUPS = SSM_WIDTH // SSM_GROUP
SSM_STATE = 64
ATTN_HEAD_DIM = 64
ATTN_HEADS = D_MODEL // (2 * ATTN_HEAD_DIM)
ATTN_WIDTH = ATTN_HEADS * 2 * ATTN_HEAD_DIM
Q_BLOCK = 128
IN_WIDTH = SSM_WIDTH + 3 * ATTN_WIDTH + 2 * D_MODEL
N_EXPERTS = 32
TOP_K = 4
D_FF = D_MODEL
SWIGLU_ALPHA = 1.702
SWIGLU_LIMIT = 7.0
MOE_BLOCK = 256
NORM_EPS = 1e-5

kernel_name = "hybrid_s5_diffattn_moe_block"

def rms_norm(x, gain, eps=NORM_EPS):
    xf = x.astype(jnp.float32)
    y = xf * lax.rsqrt(jnp.mean(xf * xf, axis=-1, keepdims=True) + eps)
    return (y * gain.astype(jnp.float32)).astype(x.dtype)

def _complex_linear_combine(e1, e2):
    a1r, a1i, b1r, b1i = e1
    a2r, a2i, b2r, b2i = e2
    ar = a1r * a2r - a1i * a2i
    ai = a1r * a2i + a1i * a2r
    br = a2r * b1r - a2i * b1i + b2r
    bi = a2r * b1i + a2i * b1r + b2i
    return (ar, ai, br, bi)

def s5_ssm(u, lambda_re, lambda_im, log_dt, b_re, b_im, c_re, c_im, d_skip):
    bsz, seq, _ = u.shape
    uf = u.astype(jnp.float32).reshape(bsz, seq, SSM_GROUPS, SSM_GROUP)
    dt = jnp.exp(log_dt.astype(jnp.float32))[:, None]
    lr = jnp.minimum(lambda_re.astype(jnp.float32), -1e-4)
    li = lambda_im.astype(jnp.float32)
    mag = jnp.exp(lr * dt)
    abar_re = mag * jnp.cos(li * dt)
    abar_im = mag * jnp.sin(li * dt)
    den = lr * lr + li * li
    nr = abar_re - 1.0
    coef_re = (nr * lr + abar_im * li) / den
    coef_im = (abar_im * lr - nr * li) / den
    br = b_re.astype(jnp.float32)
    bi = b_im.astype(jnp.float32)
    bbar_re = coef_re[..., None] * br - coef_im[..., None] * bi
    bbar_im = coef_re[..., None] * bi + coef_im[..., None] * br
    bu_re = jnp.einsum('bsgh,gph->bsgp', uf, bbar_re)
    bu_im = jnp.einsum('bsgh,gph->bsgp', uf, bbar_im)
    a_re = jnp.broadcast_to(abar_re, bu_re.shape)
    a_im = jnp.broadcast_to(abar_im, bu_im.shape)
    _, _, x_re, x_im = lax.associative_scan(
        _complex_linear_combine, (a_re, a_im, bu_re, bu_im), axis=1)
    y = (jnp.einsum('bsgp,ghp->bsgh', x_re, c_re.astype(jnp.float32))
         - jnp.einsum('bsgp,ghp->bsgh', x_im, c_im.astype(jnp.float32))
         + d_skip.astype(jnp.float32) * uf)
    return y.reshape(bsz, seq, SSM_WIDTH)

def diff_attention(q, k, v, q_gain, k_gain, lq1, lk1, lq2, lk2, subln_gain, lambda_init):
    bsz, seq, _ = q.shape
    q = rms_norm(q.reshape(bsz, seq, ATTN_HEADS, 2, ATTN_HEAD_DIM), q_gain)
    k = rms_norm(k.reshape(bsz, seq, ATTN_HEADS, 2, ATTN_HEAD_DIM), k_gain)
    q = q.transpose(0, 3, 2, 1, 4)
    k = k.transpose(0, 3, 2, 1, 4)
    v = v.reshape(bsz, seq, ATTN_HEADS, 2 * ATTN_HEAD_DIM).transpose(0, 2, 1, 3)
    lam = (jnp.exp(jnp.sum(lq1.astype(jnp.float32) * lk1.astype(jnp.float32)))
           - jnp.exp(jnp.sum(lq2.astype(jnp.float32) * lk2.astype(jnp.float32)))
           + lambda_init)
    scale = 1.0 / math.sqrt(ATTN_HEAD_DIM)
    outs = []
    for i in range(seq // Q_BLOCK):
        q0 = i * Q_BLOCK
        kend = q0 + Q_BLOCK
        s = jnp.einsum('bmhqd,bmhkd->bmhqk', q[:, :, :, q0:kend], k[:, :, :, :kend]).astype(jnp.float32) * scale
        mask = jnp.arange(kend)[None, :] <= (q0 + jnp.arange(Q_BLOCK))[:, None]
        p = jax.nn.softmax(jnp.where(mask, s, -jnp.inf), axis=-1)
        a = p[:, 0] - lam * p[:, 1]
        outs.append(jnp.einsum('bhqk,bhkv->bhqv', a.astype(v.dtype), v[:, :, :kend]))
    o = jnp.concatenate(outs, axis=2)
    o = rms_norm(o, subln_gain) * (1.0 - lambda_init)
    return o.transpose(0, 2, 1, 3).reshape(bsz, seq, ATTN_WIDTH)

def clamped_swiglu_expert(xb, w1, b1, w2, b2):
    h = xb @ w1 + b1
    gate = jnp.minimum(h[..., ::2], SWIGLU_LIMIT)
    up = jnp.clip(h[..., 1::2], -SWIGLU_LIMIT, SWIGLU_LIMIT)
    glu = gate * jax.nn.sigmoid(SWIGLU_ALPHA * gate)
    return ((up + 1.0) * glu) @ w2 + b2

def moe_ffn(h, w_router, b_router, w1, b1, w2, b2):
    bsz, seq, d = h.shape
    n_tok = bsz * seq
    xt = h.reshape(n_tok, d)
    logits = (xt @ w_router + b_router).astype(jnp.float32)
    top_vals, top_idx = lax.top_k(logits, TOP_K)
    gates = jax.nn.softmax(top_vals, axis=-1)
    n_pairs = n_tok * TOP_K
    e_flat = top_idx.reshape(-1).astype(jnp.int32)
    tok_flat = jnp.arange(n_pairs, dtype=jnp.int32) // TOP_K
    g_flat = gates.reshape(-1)
    order = jnp.argsort(e_flat)
    e_sorted = e_flat[order]
    counts = jnp.bincount(e_flat, length=N_EXPERTS)
    padded = (counts + MOE_BLOCK - 1) // MOE_BLOCK * MOE_BLOCK
    pad_end = jnp.cumsum(padded)
    pad_start = pad_end - padded
    grp_start = jnp.cumsum(counts) - counts
    dest = pad_start[e_sorted] + (jnp.arange(n_pairs, dtype=jnp.int32) - grp_start[e_sorted])
    n_slots = n_pairs + N_EXPERTS * MOE_BLOCK
    n_blocks = n_slots // MOE_BLOCK
    slot_tok = jnp.full((n_slots,), n_tok, jnp.int32).at[dest].set(tok_flat[order])
    slot_gate = jnp.zeros((n_slots,), jnp.float32).at[dest].set(g_flat[order])
    block_exp = jnp.minimum(
        jnp.searchsorted(pad_end, jnp.arange(n_blocks) * MOE_BLOCK, side='right'), N_EXPERTS - 1)
    x_pad = jnp.concatenate([xt, jnp.zeros((1, d), xt.dtype)], axis=0)
    xb = x_pad[slot_tok].reshape(n_blocks, MOE_BLOCK, d)

    def expert_block(args):
        xblk, e = args
        return clamped_swiglu_expert(xblk, w1[e], b1[e], w2[e], b2[e])

    yb = lax.map(expert_block, (xb, block_exp))
    y = yb.reshape(n_slots, d).astype(jnp.float32) * slot_gate[:, None]
    out = jax.ops.segment_sum(y, slot_tok, num_segments=n_tok + 1)[:n_tok]
    return out.reshape(bsz, seq, d).astype(h.dtype)

def setup_inputs(seed: int = 0) -> dict:
    key = jax.random.key(seed)
    ks = jax.random.split(key, 32)
    L, D, G, H, P = DEPTH, D_MODEL, SSM_GROUPS, SSM_GROUP, SSM_STATE
    nrm = lambda k, shape, s: jax.random.normal(k, shape, jnp.float32) * s
    lam_im0 = jnp.pi * jnp.arange(P, dtype=jnp.float32)
    return {
        "x": nrm(ks[0], (BATCH, SEQ, D), 1.0),
        "norm1_gain": 1.0 + nrm(ks[1], (L, D), 0.01),
        "w_in": nrm(ks[2], (L, D, IN_WIDTH), D ** -0.5),
        "lambda_re": -0.5 + nrm(ks[3], (L, G, P), 0.01),
        "lambda_im": lam_im0 + nrm(ks[4], (L, G, P), 0.01),
        "log_dt": jax.random.uniform(ks[5], (L, G), jnp.float32, math.log(1e-3), math.log(1e-1)),
        "ssm_b_re": nrm(ks[6], (L, G, P, H), (2 * H) ** -0.5),
        "ssm_b_im": nrm(ks[7], (L, G, P, H), (2 * H) ** -0.5),
        "ssm_c_re": nrm(ks[8], (L, G, H, P), P ** -0.5),
        "ssm_c_im": nrm(ks[9], (L, G, H, P), P ** -0.5),
        "ssm_d": nrm(ks[10], (L, G, H), 1.0),
        "w_glu": nrm(ks[11], (L, SSM_WIDTH, SSM_WIDTH), SSM_WIDTH ** -0.5),
        "b_glu": nrm(ks[12], (L, SSM_WIDTH), 0.01),
        "q_norm_gain": 1.0 + nrm(ks[13], (L, ATTN_HEAD_DIM), 0.01),
        "k_norm_gain": 1.0 + nrm(ks[14], (L, ATTN_HEAD_DIM), 0.01),
        "lambda_q1": nrm(ks[15], (L, ATTN_HEAD_DIM), 0.1),
        "lambda_k1": nrm(ks[16], (L, ATTN_HEAD_DIM), 0.1),
        "lambda_q2": nrm(ks[17], (L, ATTN_HEAD_DIM), 0.1),
        "lambda_k2": nrm(ks[18], (L, ATTN_HEAD_DIM), 0.1),
        "subln_gain": 1.0 + nrm(ks[19], (L, 2 * ATTN_HEAD_DIM), 0.01),
        "w_proj_ssm": nrm(ks[20], (L, SSM_WIDTH, D), SSM_WIDTH ** -0.5),
        "w_proj_attn": nrm(ks[21], (L, ATTN_WIDTH, D), ATTN_WIDTH ** -0.5),
        "w_out": nrm(ks[22], (L, D, D), D ** -0.5),
        "norm2_gain": 1.0 + nrm(ks[23], (L, D), 0.01),
        "w_router": nrm(ks[24], (L, D, N_EXPERTS), D ** -0.5),
        "b_router": nrm(ks[25], (L, N_EXPERTS), 0.01),
        "w_exp1": nrm(ks[26], (L, N_EXPERTS, D, 2 * D_FF), D ** -0.5),
        "b_exp1": nrm(ks[27], (L, N_EXPERTS, 2 * D_FF), 0.01),
        "w_exp2": nrm(ks[28], (L, N_EXPERTS, D_FF, D), D_FF ** -0.5),
        "b_exp2": nrm(ks[29], (L, N_EXPERTS, D), 0.01),
    }

def reference(x, norm1_gain, w_in, lambda_re, lambda_im, log_dt, ssm_b_re, ssm_b_im, ssm_c_re,
              ssm_c_im, ssm_d, w_glu, b_glu, q_norm_gain, k_norm_gain, lambda_q1, lambda_k1,
              lambda_q2, lambda_k2, subln_gain, w_proj_ssm, w_proj_attn, w_out, norm2_gain,
              w_router, b_router, w_exp1, b_exp1, w_exp2, b_exp2):
    splits = np.cumsum([SSM_WIDTH, ATTN_WIDTH, ATTN_WIDTH, ATTN_WIDTH, D_MODEL]).tolist()
    for l in range(DEPTH):
        lambda_init = 0.8 - 0.6 * math.exp(-0.3 * l)
        h = rms_norm(x, norm1_gain[l])
        proj = h @ w_in[l]
        u_ssm, q, k, v, g_ssm, g_attn = jnp.split(proj, splits, axis=-1)
        y = s5_ssm(u_ssm, lambda_re[l], lambda_im[l], log_dt[l], ssm_b_re[l], ssm_b_im[l],
                   ssm_c_re[l], ssm_c_im[l], ssm_d[l])
        z = jax.nn.gelu(y)
        ssm_out = (z * jax.nn.sigmoid(z @ w_glu[l].astype(jnp.float32) + b_glu[l])).astype(x.dtype)
        attn_out = diff_attention(q, k, v, q_norm_gain[l], k_norm_gain[l], lambda_q1[l], lambda_k1[l],
                                  lambda_q2[l], lambda_k2[l], subln_gain[l], lambda_init)
        merged = (jax.nn.sigmoid(g_ssm) * (ssm_out @ w_proj_ssm[l])
                  + jax.nn.sigmoid(g_attn) * (attn_out @ w_proj_attn[l]))
        x = x + merged @ w_out[l]
        h2 = rms_norm(x, norm2_gain[l])
        x = x + moe_ffn(h2, w_router[l], b_router[l], w_exp1[l], b_exp1[l], w_exp2[l], b_exp2[l])
    return x


_drawn_inputs = setup_inputs


def setup_inputs(seed=0):
    import zlib

    import numpy as np

    out = dict(_drawn_inputs(seed))
    spreads = {}
    factors = {'lambda_re': 200.0,
     'b_glu': 75.297,
     'k_norm_gain': 3.075,
     'subln_gain': 8.316,
     'b_router': 2.964,
     'b_exp1': 8.0,
     'b_exp2': 50.081,
     'lambda_im': 31.248,
     'log_dt': 31.64,
     'ssm_b_re': 36.232,
     'ssm_b_im': 46.528,
     'ssm_c_re': 30.52,
     'ssm_c_im': 42.376,
     'norm2_gain': 3.179}
    for name, (base, spread) in spreads.items():
        noise = np.random.default_rng([zlib.crc32(name.encode()), seed]).standard_normal(out[name].shape)
        drawn = base * np.exp(spread * noise) if base else spread * noise
        out[name] = __import__('jax').numpy.asarray(drawn.astype(out[name].dtype))
    for name, factor in factors.items():
        out[name] = (out[name] * factor).astype(out[name].dtype)
    return out
```

```python
import math
from contextlib import ExitStack

import concourse.bass as bass
from concourse import mybir

ALU = mybir.AluOpType
ACT = mybir.ActivationFunctionType
AX = mybir.AxisListType
F32 = mybir.dt.float32
I32 = mybir.dt.int32

P = 128
D = 1024
S = 256
TT = S // P
KT = D // P
SW = 512
CT = SW // P
NST = 16
HEADS = 8
E = 32
FF = 1024
SLOT = 64
N = 512
EPS = 1e-5
LAMBDA_INIT = 0.8 - 0.6 * math.exp(-0.3 * 0)
SCALE = 0.125
MASKED = -1e30
MAGIC = 1.5 * 2.0 ** 23
LOG2E = 1.4426950408889634
LN2_HI, LN2_LO = 0.693359375, -2.12194440e-4
INV_2PI = 0.15915494309189535
TWO_PI_1 = 6.28125
TWO_PI_2 = 0.0019350051879882812
TWO_PI_3 = 2 * math.pi - TWO_PI_1 - TWO_PI_2
MAX_EXTRA = 16
W1P, W2P = 8, 4

LRE, LIM, LDT, G1, BG, DS, SG, QG, KG, G2 = 0, 32, 64, 96, 104, 108, 112, 113, 114, 115

P_GLU, P_PSSM, P_PATT, P_WOUT, N_PIECES = 22, 23, 25, 29, 33
SSM_AT = {4: [0], 5: [1], 6: [2], 7: [3], 8: [4], 9: [5], 10: [6, 7], 11: [8, 9], 12: [10, 11, 12], 13: [13, 14, 15]}


def hybrid_block(nc, t, out):
    x_d, w_in_d = t["x"], t["w_in"]
    ctx = ExitStack()
    with ctx:
        def sb(name, shape, dt=F32):
            return ctx.enter_context(nc.sbuf_tensor(name, shape, dt))

        def sem(name):
            return ctx.enter_context(nc.semaphore(name))

        bank01 = ctx.enter_context(nc.psum_tensor("bank01", [P, 2, N], F32))
        bank23 = ctx.enter_context(nc.psum_tensor("bank23", [P, 2, N], F32))
        bank = [bank01[:, 0, :], bank01[:, 1, :], bank23[:, 0, :], bank23[:, 1, :]]
        t_bank = ctx.enter_context(nc.psum_tensor("t_bank", [P, N], F32))
        y_bank = ctx.enter_context(nc.psum_tensor("y_bank", [P, N], F32))
        pair = ctx.enter_context(nc.psum_tensor("pair", [P, 2, N], F32))

        ring = sb("ring", [P, 12, 2048])
        stream = sb("stream", [P, 4, 2048])
        x_acc = sb("x_acc", [P, TT, D])
        hT = sb("hT", [P, KT, S])
        uu = sb("uu", [P, 2048])
        qs = sb("qs", [P, 2048])
        zT = sb("zT", [P, CT, S])
        sg = sb("sg", [P, 2, TT, D])
        tmp = sb("tmp", [P, 3, 2, S])
        ident = sb("ident", [P, P])
        ones = sb("ones", [P, P])
        before = sb("before", [P, P])
        causal = sb("causal", [P, 3, P])
        iota = sb("iota", [P, 5 * SLOT])
        prow = sb("prow", [P, P])
        pcol = sb("pcol", [P, P])
        bT = sb("bT", [P, CT, 2, P])
        cT = sb("cT", [P, 2, NST, 32])
        lq = sb("lq", [P, 4, 64])
        w_r = sb("w_r", [P, KT, E])
        small = sb("small", [P, 26, NST])
        stat = sb("stat", [P, 160])
        ldt2 = sb("ldt2", [P, 2])
        route = sb("route", [P, 7, TT, E])
        gateT = sb("gateT", [E, S])
        table = sb("table", [1, 2 + 2 * MAX_EXTRA], I32)

        v_tok = ring[:, 2, :].rearrange("p (t n) -> p t n", t=TT)
        o_tok = ring[:, 3, :].rearrange("p (t n) -> p t n", t=TT)
        att = ring[:, 4:6, :].rearrange("p a n -> p (a n)")
        masked = att[:, 0:768].rearrange("p (m n) -> p m n", m=2)
        probs = att[:, 768:1536].rearrange("p (m n) -> p m n", m=2)
        a_mix = att[:, 1536:1920]
        aT = att[:, 1920:2304].rearrange("p (b n) -> p b n", b=3)
        o_sq = att[:, 2304:2560].rearrange("p (t n) -> p t n", t=TT)
        b_raw = att[:, 0:1024].rearrange("p (r j c) -> p r j c", r=2, j=NST)
        c_raw = att[:, 1024:2048].rearrange("p (r c n) -> p r c n", r=2, c=CT)
        glu_a = qs[:, 0:1024]
        glu_g = qs[:, 1024:2048]
        x_state = att[:, 3072:4096].rearrange("p (b r n) -> p b r n", b=2, r=2)
        qT = ring[:, 6, :].rearrange("p (h n) -> p h n", h=HEADS)
        kT = ring[:, 7, :].rearrange("p (h n) -> p h n", h=HEADS)
        turn = ring[:, 8:12, :].rearrange("p a n -> p (a n)").rearrange("p (j r n) -> p j r n", j=NST, r=2)
        u_tok = uu[:, 0:1024].rearrange("p (t n) -> p t n", t=TT)
        yT = uu[:, 0:1024].rearrange("p (c n) -> p c n", c=CT)
        uT = uu[:, 1024:2048].rearrange("p (c n) -> p c n", c=CT)
        merged = uu[:, :].rearrange("p (t n) -> p t n", t=TT)
        qn = qs[:, 0:1024].rearrange("p (t n) -> p t n", t=TT)
        sq = qs[:, 1024:2048].rearrange("p (t n) -> p t n", t=TT)
        oT = qs[:, :].rearrange("p (h n) -> p h n", h=HEADS)
        h2 = qs[:, :].rearrange("p (t n) -> p t n", t=TT)
        sgf = sg[:, :, :, :].rearrange("p a t n -> p (a t n)")
        h_tok = sgf[:, 0:2048].rearrange("p (t n) -> p t n", t=TT)
        sq_x = sgf[:, 2048:4096].rearrange("p (t n) -> p t n", t=TT)
        turn_t = sgf[:, 0:4096].rearrange("p (a j n) -> p a j n", a=2, j=NST)
        glu_t = sgf[:, 0:1024]
        xT = sgf[:, 0:512].rearrange("p (k n) -> p k n", k=KT)
        g_act = sgf[:, 512:1024]
        u_act = sgf[:, 1024:1536]
        s_act = sgf[:, 1536:2048]
        actT = sgf[:, 2048:2560].rearrange("p (j n) -> p j n", j=4)
        y_sb = sgf[:, 2560:3072]
        sel = sgf[:, 3072:3200].rearrange("p (t n) -> p t n", t=TT)
        sel_g = sgf[:, 3200:3456].rearrange("p (t n) -> p t n", t=TT)
        put = sgf[:, 3456:3712]
        b2_sb = tmp[0:E, 0:2, :, :].rearrange("p a b n -> p (a b n)")
        b1_row = stream[0:1, 0, :]
        big = stream[0:1, 1, 0:MAX_EXTRA * 96].rearrange("p (a b) -> p a b", a=MAX_EXTRA)
        flag = stream[0:1, 2, 0:96]
        flag_e = stream[0:1, 2, 96:192]
        flag_b = stream[0:1, 2, 192:288]
        flag_pos = stream[0:1, 2, 288:384]
        table_f = stream[0:1, 2, 384:384 + 2 + 2 * MAX_EXTRA]

        x_in = sem("x_in")
        prow_in = sem("prow_in")
        bc_in = sem("bc_in")
        misc_in = sem("misc_in")
        b2_in = sem("b2_in")
        piece_in = [sem(f"piece_in{i}") for i in range(4)]
        w1_in = [sem(f"w1_in{i}") for i in range(W1P)]
        w2_in = [sem(f"w2_in{i}") for i in range(W2P)]
        b1_in = sem("b1_in")
        out_in = sem("out_in")
        zeroed = sem("zeroed")
        consts = sem("consts")
        pool_step = sem("pool_step")
        turns_ready = sem("turns_ready")
        dve_step = sem("dve_step")
        act_step = sem("act_step")
        prow_ready = sem("prow_ready")
        x_sq = sem("x_sq")
        h_ready = sem("h_ready")
        pcol_ps = sem("pcol_ps")
        pcol_ready = sem("pcol_ready")
        hT_ps = sem("hT_ps")
        hT_dve = sem("hT_dve")
        hT_act = sem("hT_act")
        b_ps = sem("b_ps")
        c_ps = sem("c_ps")
        bT_ready = sem("bT_ready")
        cT_ready = sem("cT_ready")
        sin_in = sem("sin_in")
        sin_ready = sem("sin_ready")
        turn_base = sem("turn_base")
        piece_used = sem("piece_used")
        chunk_read = sem("chunk_read")
        qk_sq = sem("qk_sq")
        qk_ss = sem("qk_ss")
        qk_std = sem("qk_std")
        qk_n = sem("qk_n")
        t_ps = sem("t_ps")
        t_read = sem("t_read")
        bu_ps = sem("bu_ps")
        bu_read = sem("bu_read")
        xs_ready = sem("xs_ready")
        y_ps = sem("y_ps")
        y_read = sem("y_read")
        s_ps = sem("s_ps")
        s_read = sem("s_read")
        nmax = sem("nmax")
        p_ready = sem("p_ready")
        a_ready = sem("a_ready")
        aT_ps = sem("aT_ps")
        aT_ready = sem("aT_ready")
        o_ps = sem("o_ps")
        o_read = sem("o_read")
        o_std = sem("o_std")
        o_norm = sem("o_norm")
        oT_ps = sem("oT_ps")
        oT_ready = sem("oT_ready")
        gel_in = sem("gel_in")
        gel_sig = sem("gel_sig")
        z_ready = sem("z_ready")
        glu_ps = sem("glu_ps")
        glu_sig = sem("glu_sig")
        sout_ready = sem("sout_ready")
        gates_sig = sem("gates_sig")
        merged_s = sem("merged_s")
        mT_ps = sem("mT_ps")
        mT_ready = sem("mT_ready")
        x1_ready = sem("x1_ready")
        x1_std = sem("x1_std")
        x1_sq = sem("x1_sq")
        h2_ready = sem("h2_ready")
        h2T_ps = sem("h2T_ps")
        h2T_ready = sem("h2T_ready")
        logit_ps = sem("logit_ps")
        top_ready = sem("top_ready")
        gexp = sem("gexp")
        picked = sem("picked")
        rank_ps = sem("rank_ps")
        gates_ready = sem("gates_ready")
        gT_ps = sem("gT_ps")
        gT_ready = sem("gT_ready")
        bias2_ps = sem("bias2_ps")
        table_ready = sem("table_ready")
        w1_used = sem("w1_used")
        w2_used = sem("w2_used")
        sel_ready = sem("sel_ready")
        selg_ready = sem("selg_ready")
        xg_ps = sem("xg_ps")
        xT_ready = sem("xT_ready")
        hid_ps = sem("hid_ps")
        g_ready = sem("g_ready")
        hid_read = sem("hid_read")
        um_ready = sem("um_ready")
        sig_ready = sem("sig_ready")
        act_ready = sem("act_ready")
        actT_ps = sem("actT_ps")
        actT_ready = sem("actT_ready")
        put_ps = sem("put_ps")
        put_ready = sem("put_ready")
        y_ready = sem("y_ready")
        comb_ps = sem("comb_ps")
        added = sem("added")

        ps_xg, ps_act, ps_y, ps_put = bank[2], bank[3], t_bank, y_bank

        def col(a, n=1):
            return stat[:, a:a + n]
        x_ss, x_std, x_rs = col(0, 2), col(2, 2), col(4, 2)
        n_ss, n_std, n_rs = col(6, 16), col(22, 16), col(38, 16)
        lam_sum, lam_exp, neg_lam = col(54, 2), col(56, 2), col(58)
        s_max, n_bias, p_sum, p_rs = col(60, 4), col(64, 4), col(68, 4), col(72, 4)
        p_c1 = col(76, 2)
        o_ss, o_rs = col(80, 16), col(96, 16)
        top8 = stat[:, 112:128].rearrange("p (t n) -> p t n", t=TT)
        neg_top, over, need, g_sum, g_rs = col(128, 2), col(130, 2), col(132, 2), col(134, 2), col(136, 2)
        sub_gain, half_pi, eps = col(157), col(158), col(159)
        names = ["ldt", "lr", "li", "k", "r", "q", "pw", "dt", "a", "em1", "mag", "th", "thk", "thr", "sh", "ch",
                 "cos", "sin", "vers", "nr", "ai", "den", "t1", "t2", "cr", "ci"]
        sm = {n: small[:, i, :] for i, n in enumerate(names)}

        block = ctx.enter_context(nc.Block())

        def stream_source(i):
            def cut(w, kh, n):
                return w[512 * kh:512 * kh + 512, N * n:N * n + N].rearrange("(k p) n -> p k n", p=P)
            if i < P_GLU:
                return cut(w_in_d[0], i % 2, i // 2)
            if i == P_GLU:
                return cut(t["w_glu"][0], 0, 0)
            if i < P_PATT:
                return cut(t["w_proj_ssm"][0], 0, i - P_PSSM)
            if i < P_WOUT:
                return cut(t["w_proj_attn"][0], (i - P_PATT) % 2, (i - P_PATT) // 2)
            return cut(t["w_out"][0], (i - P_WOUT) % 2, (i - P_WOUT) // 2)

        def w1_source(e, k):
            return t["w_exp1"][0, bass.ds(e, 1), P * k:P * k + P, :].rearrange("e p n -> p (e n)")

        def w2_source(e, m):
            return t["w_exp2"][0, bass.ds(e, 1), 2 * P * m:2 * P * m + 2 * P, :].rearrange("e (k p) n -> p (e k) n", p=P)

        def ring_w2(m):
            return ring[:, W1P + m, :].rearrange("p (k n) -> p k n", k=2)

        @block.sync
        def _(sp):
            sp.dma_start(x_acc[:, :, :], x_d[0].rearrange("(t p) n -> p t n", p=P)).then_inc(x_in, 16)

            def stream_piece(i):
                if i >= 4:
                    sp.wait_ge(piece_used, i - 3)
                sp.dma_start(stream[:, i % 4, :].rearrange("p (k n) -> p k n", k=4),
                             stream_source(i)).then_inc(piece_in[i % 4], 16)

            for i in range(6):
                stream_piece(i)
            for k in range(2):
                sp.dma_start(ring[:, k, :], w1_source(0, k)).then_inc(w1_in[k], 16)
            for i in range(6, 18):
                stream_piece(i)
            sp.wait_ge(xs_ready, NST)
            for m in range(W2P):
                sp.dma_start(ring_w2(m), w2_source(0, m)).then_inc(w2_in[m], 16)
            sp.dma_start(b2_sb, t["b_exp2"][0]).then_inc(b2_in, 16)
            for i in range(18, P_PATT):
                stream_piece(i)
            sp.wait_ge(oT_ps, 4)
            for k in range(2, W1P):
                sp.dma_start(ring[:, k, :], w1_source(0, k)).then_inc(w1_in[k], 16)
            for i in range(P_PATT, N_PIECES):
                stream_piece(i)
            sp.wait_ge(piece_used, N_PIECES)
            sp.dma_start(b1_row, t["b_exp1"][0, 0:1, :]).then_inc(b1_in, 16)

            def load_block(i, e):
                for k in range(W1P):
                    sp.wait_ge(w1_used, (i - 1) * W1P + k + 1)
                    sp.dma_start(ring[:, k, :], w1_source(e, k)).then_inc(w1_in[k], 16)
                sp.wait_ge(hid_ps, i)
                sp.dma_start(b1_row, t["b_exp1"][0, bass.ds(e, 1), :]).then_inc(b1_in, 16)
                for m in range(W2P):
                    sp.wait_ge(w2_used, (i - 1) * W2P + m + 1)
                    sp.dma_start(ring_w2(m), w2_source(e, m)).then_inc(w2_in[m], 16)

            with sp.Fori(1, E) as e:
                load_block(e, e)
            sp.wait_ge(table_ready, 1)
            extra = sp.value_load(table[0:1, 0:1], min_val=0, max_val=MAX_EXTRA)
            with sp.If(extra > 0):
                with sp.Fori(0, extra) as j:
                    e = sp.value_load(table[0:1, bass.ds(j + 2, 1)], min_val=0, max_val=E - 1)
                    load_block(j + E, e)
            sp.wait_ge(added, (extra + E + 1) * 2)
            sp.dma_start(out[0].rearrange("(t p) n -> p t n", p=P), x_acc[:, :, :]).then_inc(out_in, 16)
            sp.wait_ge(out_in, 16)

        @block.gpsimd
        def _(pool):
            n_step = [0]

            def step(ins):
                n_step[0] += 1
                ins.then_inc(pool_step, 1)
                pool.wait_ge(pool_step, n_step[0])

            nc.gpsimd.memset(prow[:, :], 0.0).then_inc(zeroed, 1)
            nc.gpsimd.memset(att[:, 0:2048], 0.0).then_inc(zeroed, 1)
            step(nc.gpsimd.memset(ones[:, :], 1.0))
            step(nc.gpsimd.memset(ident[:, :], 0.0))
            nc.gpsimd.affine_select(out=ident[:, :], in_=ident[:, :], compare_op=ALU.not_equal, fill=1.0, base=0,
                                    pattern=[[-1, P]], channel_multiplier=1).then_inc(consts, 1)
            nc.gpsimd.affine_select(out=before[:, :], in_=ones[:, :], compare_op=ALU.is_gt, fill=0.0, base=0,
                                    pattern=[[1, P]], channel_multiplier=-1).then_inc(consts, 1)
            step(nc.gpsimd.memset(causal[:, :, :], 0.0))
            for b in (0, 2):
                nc.gpsimd.affine_select(out=causal[:, b, :], in_=causal[:, b, :], compare_op=ALU.is_ge, fill=MASKED,
                                        base=0, pattern=[[-1, P]], channel_multiplier=1).then_inc(consts, 1)
            nc.gpsimd.iota(iota[:, :], pattern=[[1, 5 * SLOT]], base=0, channel_multiplier=0,
                           allow_small_or_imprecise_dtypes=True).then_inc(consts, 1)
            pool.wait_ge(turn_base, 1)
            for half in range(2):
                js = slice(8 * half, 8 * half + 8)
                for n, pr, pi in ((64, "t1", "t2"), (128, "th", "thk")):
                    def wide(name):
                        return sm[name][:, js].unsqueeze(2).to_broadcast([P, 8, n])
                    c0, s0 = turn[:, js, 0, 0:n], turn[:, js, 1, 0:n]
                    a, b = turn_t[:, 0, js, 0:n], turn_t[:, 1, js, 0:n]
                    step(nc.gpsimd.tensor_tensor(a, c0, wide(pr), ALU.mult))
                    step(nc.gpsimd.tensor_tensor(b, s0, wide(pi), ALU.mult))
                    step(nc.gpsimd.tensor_tensor(turn[:, js, 0, n:2 * n], a, b, ALU.subtract))
                    step(nc.gpsimd.tensor_tensor(a, c0, wide(pi), ALU.mult))
                    step(nc.gpsimd.tensor_tensor(b, s0, wide(pr), ALU.mult))
                    if n == 64:
                        step(nc.gpsimd.tensor_tensor(turn[:, js, 1, n:2 * n], a, b, ALU.add))
                    else:
                        nc.gpsimd.tensor_tensor(turn[:, js, 1, n:2 * n], a, b, ALU.add).then_inc(turns_ready, 1)

        @block.scalar
        def _(act):
            act.wait_ge(zeroed, 2)
            half = t["lambda_re"][0].rearrange("(j g) p -> j (g p)", g=2)
            act.dma_start(prow[LRE:LRE + NST, :], half).then_inc(prow_in, 16)
            act.dma_start(prow[LIM:LIM + NST, :], t["lambda_im"][0].rearrange("(j g) p -> j (g p)", g=2)).then_inc(prow_in, 16)
            act.dma_start(ldt2[LDT:LDT + NST, :], t["log_dt"][0].rearrange("(j g) -> j g", g=2)).then_inc(prow_in, 16)
            act.dma_start(prow[G1:G1 + KT, :], t["norm1_gain"][0].rearrange("(k p) -> k p", p=P)).then_inc(prow_in, 16)
            act.dma_start(prow[BG:BG + CT, :], t["b_glu"][0].rearrange("(k p) -> k p", p=P)).then_inc(prow_in, 16)
            act.dma_start(prow[DS:DS + CT, :], t["ssm_d"][0].rearrange("(c g) h -> c (g h)", c=CT)).then_inc(prow_in, 16)
            act.dma_start(prow[SG:SG + 1, :], t["subln_gain"]).then_inc(prow_in, 16)
            for r, name in ((QG, "q_norm_gain"), (KG, "k_norm_gain")):
                for m in range(2):
                    act.dma_start(prow[r:r + 1, 64 * m:64 * m + 64], t[name]).then_inc(prow_in, 16)
            act.dma_start(prow[G2:G2 + KT, :], t["norm2_gain"][0].rearrange("(k p) -> k p", p=P)).then_inc(prow_in, 16)
            for r, name in enumerate(("ssm_b_re", "ssm_b_im")):
                src = t[name][0].rearrange("(j g) p h -> g p j h", g=2)
                for g in range(2):
                    act.dma_start(b_raw[64 * g:64 * g + 64, r, :, 16 * g:16 * g + 16], src[g]).then_inc(bc_in, 16)
            for r, name in enumerate(("ssm_c_re", "ssm_c_im")):
                src = t[name][0].rearrange("(c b) h p -> b h c p", c=CT)
                for b in range(8):
                    g = b % 2
                    act.dma_start(c_raw[16 * b:16 * b + 16, r, :, 64 * g:64 * g + 64], src[b]).then_inc(bc_in, 16)
            for i, name in enumerate(("lambda_q1", "lambda_k1", "lambda_q2", "lambda_k2")):
                act.dma_start(lq[:, i, :], t[name][0].partition_broadcast(P)).then_inc(misc_in, 16)
            act.dma_start(w_r[:, :, :], t["w_router"][0].rearrange("(k p) e -> p k e", p=P)).then_inc(misc_in, 16)
            act.dma_start(route[:, 6, 0, :], t["b_router"][0].partition_broadcast(P)).then_inc(misc_in, 16)

            act.wait_ge(x_in, 16)
            for tt in range(TT):
                nc.scalar.activation(sq_x[:, tt, :], x_acc[:, tt, :], ACT.Square,
                                     accum_out=x_ss[:, tt:tt + 1]).then_inc(act_step, 1)
            act.wait_ge(act_step, 2)
            act.wait_ge(dve_step, 2)
            nc.scalar.activation(x_std, x_ss, ACT.Sqrt, bias=eps, scale=1.0 / D).then_inc(x_sq, 1)
            for b in (1, 3):
                act.wait_ge(pcol_ready, 1)
                act.wait_ge(hT_ps, b + 1)
                for k in (2 * b, 2 * b + 1):
                    nc.scalar.activation(hT[:, k, :], bank[b][:, 256 * (k % 2):256 * (k % 2) + 256], ACT.Identity,
                                         scale=pcol[:, G1 + k:G1 + k + 1]).then_inc(hT_act, 1)
            act.wait_ge(b_ps, 2)
            for r in range(2):
                nc.scalar.copy(bT[:, :, r, :], pair[:, r, :].rearrange("p (c n) -> p c n", c=CT)).then_inc(bT_ready, 1)
            act.wait_ge(sin_in, 1)
            nc.scalar.activation(sm["sh"], sm["thr"], ACT.Sin, scale=0.5).then_inc(sin_ready, 1)
            nc.scalar.activation(sm["ch"], sm["thr"], ACT.Sin, scale=0.5, bias=half_pi).then_inc(sin_ready, 1)

            def copy_t(dst, ps, gain=None, view=None):
                if gain is None:
                    nc.scalar.copy(dst, ps).then_inc(t_read, 1)
                else:
                    nc.scalar.activation(dst, ps, ACT.Identity, scale=gain).then_inc(t_read, 1)

            for c in range(7):
                act.wait_ge(piece_used, 2 * c + 2)
                b = 2 * (c % 2)
                if c == 0:
                    for tt in range(TT):
                        nc.scalar.copy(u_tok[:, tt, :], bank[b + tt][:, :]).then_inc(chunk_read, 1)
                    act.wait_ge(t_ps, 1)
                    copy_t(uT[:, 0:2, :], t_bank[:, :].rearrange("p (c n) -> p c n", c=2))
                    act.wait_ge(t_ps, 2)
                    copy_t(uT[:, 2:4, :], y_bank[:, :].rearrange("p (c n) -> p c n", c=2))
                elif c < 5:
                    if c >= 2:
                        act.wait_ge(qk_ss, c - 1)
                    for tt in range(TT):
                        nc.scalar.activation(sq[:, tt, :], bank[b + tt][:, :], ACT.Square).then_inc(qk_sq, 1)
                    act.wait_ge(qk_ss, c)
                    nc.scalar.activation(n_std, n_ss, ACT.Sqrt, bias=eps,
                                         scale=1.0 / 64).then_inc(qk_std, 1)
                    dst, gain = (qT, QG) if c < 3 else (kT, KG)
                    for r in range(2):
                        h = 4 * ((c - 1) % 2) + 2 * r
                        act.wait_ge(t_ps, 2 * c + r + 1)
                        copy_t(dst[:, h:h + 2, :], t_bank[:, :].rearrange("p (h n) -> p h n", h=2), pcol[:, gain:gain + 1])
                else:
                    for tt in range(TT):
                        nc.scalar.copy(v_tok[:, tt, N * (c - 5):N * (c - 5) + N], bank[b + tt][:, :]).then_inc(chunk_read, 1)

            act.wait_ge(nmax, 1)
            nc.scalar.activation(lam_exp, lam_sum, ACT.Exp).then_inc(act_step, 1)

            for h in range(HEADS):
                act.wait_ge(nmax, h + 2)
                for m in range(2):
                    for qt in range(2):
                        cs = slice(0, 128) if qt == 0 else slice(128, 384)
                        i = 2 * m + qt
                        nc.scalar.activation(probs[:, m, cs], masked[:, m, cs], ACT.Exp, bias=n_bias[:, i:i + 1],
                                             scale=SCALE, accum_out=p_sum[:, i:i + 1]).then_inc(p_ready, 1)
                if h % 2:
                    c = 7 + h // 2
                    g = h // 2
                    act.wait_ge(piece_used, 2 * c + 2)
                    if h == 1:
                        act.wait_ge(turns_ready, 2)
                    for tt in range(TT):
                        nc.scalar.copy(sg[:, g // 2, tt, N * (g % 2):N * (g % 2) + N],
                                       bank[2 * (c % 2) + tt][:, :]).then_inc(chunk_read, 1)
                act.wait_ge(aT_ps, h + 1)
                nc.scalar.copy(aT, t_bank[:, 0:384].rearrange("p (b n) -> p b n", b=3)).then_inc(aT_ready, 1)
                act.wait_ge(o_ps, h + 1)
                for qt in range(2):
                    ps = y_bank[:, 128 * qt:128 * qt + 128]
                    nc.scalar.activation(o_sq[:, qt, :], ps, ACT.Square,
                                         accum_out=o_ss[:, 8 * qt + h:8 * qt + h + 1]).then_inc(o_read, 1)
                    nc.scalar.copy(o_tok[:, qt, 128 * h:128 * h + 128], ps).then_inc(o_read, 1)
            act.wait_ge(o_read, 4 * HEADS)
            nc.scalar.activation(o_rs, o_ss, ACT.Sqrt, bias=eps, scale=1.0 / P).then_inc(o_std, 1)
            act.wait_ge(gel_in, 1)
            nc.scalar.activation(glu_g, glu_a, ACT.Sigmoid, scale=2 * 0.7978845608028654).then_inc(gel_sig, 1)
            act.wait_ge(chunk_read, 12)
            nc.scalar.activation(sgf[:, :], sgf[:, :], ACT.Sigmoid).then_inc(gates_sig, 1)
            for ct in range(CT):
                if ct < 2:
                    act.wait_ge(glu_ps, 1)
                else:
                    act.wait_ge(piece_used, P_GLU + 1)
                nc.scalar.activation(glu_g[:, S * ct:S * ct + S], pair[:, ct // 2, S * (ct % 2):S * (ct % 2) + S], ACT.Sigmoid,
                                     bias=pcol[:, BG + ct:BG + ct + 1]).then_inc(glu_sig, 1)
            act.wait_ge(sout_ready, 1)
            for b in range(4):
                act.wait_ge(oT_ps, b + 1)
                nc.scalar.activation(oT[:, 2 * b:2 * b + 2, :], bank[b][:, :].rearrange("p (h n) -> p h n", h=2), ACT.Identity,
                                     scale=sub_gain).then_inc(oT_ready, 1)
            for b in range(4):
                act.wait_ge(mT_ps, b + 1)
                nc.scalar.copy(hT[:, 2 * b:2 * b + 2, :],
                               bank[b][:, :].rearrange("p (h n) -> p h n", h=2)).then_inc(mT_ready, 1)
            for tt in range(TT):
                act.wait_ge(x1_ready, 4)
                nc.scalar.activation(sg[:, 0, tt, :], x_acc[:, tt, :], ACT.Square,
                                     accum_out=x_ss[:, tt:tt + 1]).then_inc(x1_sq, 1)
            act.wait_ge(x1_sq, 2)
            nc.scalar.activation(x_std, x_ss, ACT.Sqrt, bias=eps, scale=1.0 / D).then_inc(x1_std, 1)
            for b in range(4):
                act.wait_ge(h2T_ps, b + 1)
                for k in (2 * b, 2 * b + 1):
                    nc.scalar.activation(hT[:, k, :], bank[b][:, S * (k % 2):S * (k % 2) + S], ACT.Identity,
                                         scale=pcol[:, G2 + k:G2 + k + 1]).then_inc(h2T_ready, 1)
            for tt in range(TT):
                act.wait_ge(top_ready, tt + 1)
                nc.scalar.activation(route[:, 1, tt, :], route[:, 0, tt, :], ACT.Exp,
                                     bias=neg_top[:, tt:tt + 1]).then_inc(gexp, 1)
            act.wait_ge(gT_ps, 1)
            nc.scalar.copy(gateT[:, :], t_bank[0:E, 0:S]).then_inc(gT_ready, 1)

            def block_work(i):
                act.wait_ge(g_ready, i + 1)
                nc.scalar.activation(s_act, g_act, ACT.Sigmoid, scale=1.702).then_inc(sig_ready, 1)
                act.wait_ge(actT_ps, i + 1)
                nc.scalar.copy(actT, ps_act[:, :].rearrange("p (j n) -> p j n", j=4)).then_inc(actT_ready, 1)
                act.wait_ge(put_ps, i + 1)
                nc.scalar.copy(put, ps_put[:, 0:S]).then_inc(put_ready, 1)
                act.wait_ge(w2_used, (i + 1) * W2P)
                nc.scalar.copy(y_sb, ps_y[:, :]).then_inc(y_ready, 1)

            block_work(0)
            with act.Fori(1, E) as i:
                block_work(i)
            act.wait_ge(table_ready, 1)
            extra = act.value_load(table[0:1, 0:1], min_val=0, max_val=MAX_EXTRA)
            with act.If(extra > 0):
                with act.Fori(0, extra) as j:
                    block_work(j + E)

        @block.vector
        def _(dve):
            V = nc.vector
            n_step = [0]

            def mark(ins):
                n_step[0] += 1
                ins.then_inc(dve_step, 1)

            def sync():
                dve.wait_ge(dve_step, n_step[0])

            def step(ins):
                mark(ins)
                sync()

            def mul(out, a, b):
                return V.tensor_tensor(out, a, b, ALU.mult)

            mark(V.memset(half_pi, math.pi / 2))
            step(V.memset(eps, EPS))
            dve.wait_ge(x_sq, 1)
            step(V.reciprocal(x_rs, x_std))
            for tt in range(TT):
                V.tensor_scalar(h_tok[:, tt, :], x_acc[:, tt, :], x_rs[:, tt:tt + 1], None, ALU.mult).then_inc(h_ready, 1)
            dve.wait_ge(prow_in, 16 * 12)
            V.tensor_copy(prow[LDT:LDT + NST, :].rearrange("j (g p) -> j g p", g=2),
                          ldt2[LDT:LDT + NST, :].unsqueeze(2).to_broadcast([NST, 2, 64])).then_inc(prow_ready, 1)
            dve.wait_ge(pcol_ps, 1)
            V.tensor_copy(pcol[:, :], t_bank[:, 0:P]).then_inc(pcol_ready, 1)
            dve.wait_ge(pcol_ready, 1)
            step(V.tensor_scalar(sub_gain, pcol[:, SG:SG + 1], 1.0 - LAMBDA_INIT, None, ALU.mult))
            for b in (0, 2):
                dve.wait_ge(hT_ps, b + 1)
                for k in (2 * b, 2 * b + 1):
                    V.tensor_scalar(hT[:, k, :], bank[b][:, S * (k % 2):S * (k % 2) + S], pcol[:, G1 + k:G1 + k + 1], None,
                                    ALU.mult).then_inc(hT_dve, 1)

            def exponential(x):
                step(V.tensor_scalar(sm[x], sm[x], -100.0, 88.0, ALU.max, ALU.min))
                step(V.tensor_scalar(sm["k"], sm[x], LOG2E, MAGIC, ALU.mult, ALU.add))
                step(V.tensor_scalar(sm["k"], sm["k"], MAGIC, -127.0, ALU.subtract, ALU.max))
                step(V.scalar_tensor_tensor(sm["r"], sm["k"], -LN2_HI, sm[x], ALU.mult, ALU.add))
                step(V.scalar_tensor_tensor(sm["r"], sm["k"], -LN2_LO, sm["r"], ALU.mult, ALU.add))
                mark(V.tensor_scalar(sm["pw"].bitcast(I32), sm["k"], 127.0, 2.0 ** 23, ALU.add, ALU.mult))
                step(V.tensor_scalar(sm["q"], sm["r"], 1.0 / 8, 1.0, ALU.mult, ALU.add))
                for n in (7, 6, 5, 4, 3, 2):
                    step(mul(sm["q"], sm["q"], sm["r"]))
                    step(V.tensor_scalar(sm["q"], sm["q"], 1.0 / n, 1.0, ALU.mult, ALU.add))
                step(mul(sm["q"], sm["q"], sm["r"]))

            step(V.tensor_copy(sm["ldt"], pcol[:, LDT:LDT + NST]))
            exponential("ldt")
            step(V.scalar_tensor_tensor(sm["dt"], sm["q"], 1.0, sm["pw"], ALU.add, ALU.mult))
            mark(V.tensor_scalar(sm["lr"], pcol[:, LRE:LRE + NST], -1e-4, None, ALU.min))
            mark(V.tensor_copy(sm["li"], pcol[:, LIM:LIM + NST]))
            step(mul(sm["th"], pcol[:, LIM:LIM + NST], sm["dt"]))
            step(V.tensor_scalar(sm["thk"], sm["th"], INV_2PI, MAGIC, ALU.mult, ALU.add))
            step(V.tensor_scalar(sm["thk"], sm["thk"], MAGIC, None, ALU.subtract))
            step(V.scalar_tensor_tensor(sm["thr"], sm["thk"], -TWO_PI_1, sm["th"], ALU.mult, ALU.add))
            step(V.scalar_tensor_tensor(sm["thr"], sm["thk"], -TWO_PI_2, sm["thr"], ALU.mult, ALU.add))
            step(V.scalar_tensor_tensor(sm["thr"], sm["thk"], -TWO_PI_3, sm["thr"], ALU.mult, ALU.add))
            V.tensor_scalar(sm["thr"], sm["thr"], -3.14159, 3.14159, ALU.max, ALU.min).then_inc(sin_in, 1)
            step(mul(sm["a"], sm["lr"], sm["dt"]))
            exponential("a")
            mark(V.scalar_tensor_tensor(sm["mag"], sm["q"], 1.0, sm["pw"], ALU.add, ALU.mult))
            mark(V.tensor_scalar(sm["t2"], sm["pw"], 1.0, None, ALU.subtract))
            step(mul(sm["t1"], sm["q"], sm["pw"]))
            step(V.tensor_tensor(sm["em1"], sm["t1"], sm["t2"], ALU.add))
            dve.wait_ge(sin_ready, 2)
            mark(V.scalar_tensor_tensor(sm["sin"], sm["sh"], 2.0, sm["ch"], ALU.mult, ALU.mult))
            step(V.scalar_tensor_tensor(sm["vers"], sm["sh"], 2.0, sm["sh"], ALU.mult, ALU.mult))
            step(V.tensor_scalar(sm["cos"], sm["vers"], -1.0, 1.0, ALU.mult, ALU.add))
            mark(mul(sm["ai"], sm["mag"], sm["sin"]))
            step(mul(sm["nr"], sm["em1"], sm["cos"]))
            step(V.tensor_tensor(sm["nr"], sm["nr"], sm["vers"], ALU.subtract))
            mark(mul(sm["t1"], sm["lr"], sm["lr"]))
            step(mul(sm["t2"], sm["li"], sm["li"]))
            step(V.tensor_tensor(sm["den"], sm["t1"], sm["t2"], ALU.add))
            step(V.reciprocal(sm["den"], sm["den"]))
            mark(mul(sm["t1"], sm["nr"], sm["lr"]))
            step(mul(sm["t2"], sm["ai"], sm["li"]))
            step(V.tensor_tensor(sm["t1"], sm["t1"], sm["t2"], ALU.add))
            step(mul(sm["cr"], sm["t1"], sm["den"]))
            mark(mul(sm["t1"], sm["ai"], sm["lr"]))
            step(mul(sm["t2"], sm["nr"], sm["li"]))
            step(V.tensor_tensor(sm["t1"], sm["t1"], sm["t2"], ALU.subtract))
            step(mul(sm["ci"], sm["t1"], sm["den"]))
            powers = {1: ("cos", "sin"), 2: ("ldt", "q"), 4: ("k", "r"), 8: ("a", "em1"), 16: ("nr", "ai"),
                      32: ("sh", "ch"), 64: ("t1", "t2"), 128: ("th", "thk")}
            for n in (1, 2, 4, 8, 16, 32, 64):
                (pr, pi), (qr, qi) = powers[n], powers[2 * n]
                mark(mul(sm["den"], sm[pr], sm[pr]))
                mark(mul(sm["dt"], sm[pi], sm[pi]))
                step(V.scalar_tensor_tensor(sm[qi], sm[pr], 2.0, sm[pi], ALU.mult, ALU.mult))
                step(V.tensor_tensor(sm[qr], sm["den"], sm["dt"], ALU.subtract))
            dve.wait_ge(hT_ps, 4)
            mark(V.memset(turn[:, :, 0, 0:1], 1.0))
            step(V.memset(turn[:, :, 1, 0:1], 0.0))
            for n in (1, 2, 4, 8, 16, 32):
                def wide(name):
                    return sm[name].unsqueeze(2).to_broadcast([P, NST, n])
                pr, pi = powers[n]
                c0, s0 = turn[:, :, 0, 0:n], turn[:, :, 1, 0:n]
                c1, s1 = turn[:, :, 0, n:2 * n], turn[:, :, 1, n:2 * n]
                a, b = turn_t[:, 0, :, 0:n], turn_t[:, 1, :, 0:n]
                mark(mul(a, c0, wide(pr)))
                mark(mul(b, s0, wide(pi)))
                mark(mul(c1, c0, wide(pi)))
                step(mul(s1, s0, wide(pr)))
                step(V.tensor_tensor(s1, s1, c1, ALU.add))
                ins = V.tensor_tensor(c1, a, b, ALU.subtract)
                if n < 32:
                    step(ins)
                else:
                    ins.then_inc(turn_base, 1)
            dve.wait_ge(c_ps, 2)
            cre = t_bank[:, :].rearrange("p (j n) -> p j n", j=NST)
            cim = y_bank[:, :].rearrange("p (j n) -> p j n", j=NST)
            w = [tmp[:, i, :, :].rearrange("p a n -> p (a n)").rearrange("p (j n) -> p j n", j=NST) for i in range(3)]
            cr_w = sm["cr"].unsqueeze(2).to_broadcast([P, NST, 32])
            ci_w = sm["ci"].unsqueeze(2).to_broadcast([P, NST, 32])
            mark(mul(w[0], cre, cr_w))
            mark(mul(w[1], cim, ci_w))
            step(mul(w[2], cre, ci_w))
            V.tensor_tensor(cT[:, 0, :, :], w[0], w[1], ALU.subtract).then_inc(cT_ready, 1)
            dve.wait_ge(cT_ready, 1)
            step(mul(w[0], cim, cr_w))
            V.scalar_tensor_tensor(cT[:, 1, :, :], w[2], -1.0, w[0], ALU.mult, ALU.subtract).then_inc(cT_ready, 1)
            dve.wait_ge(cT_ready, 2)
            dve.wait_ge(misc_in, 16 * 6)
            for i in range(2):
                mark(V.tensor_tensor_reduce(out=tmp[:, 0, i, 0:64], in0=lq[:, 2 * i, :], in1=lq[:, 2 * i + 1, :], scale=1.0,
                                            scalar=0.0, op0=ALU.mult, op1=ALU.add, accum_out=lam_sum[:, i:i + 1]))
            sync()

            def state_tile(j):
                if j == 0:
                    dve.wait_ge(turns_ready, 1)
                if j == 8:
                    dve.wait_ge(turns_ready, 2)
                rot = turn[:, j, :, :]
                src = pair[:, j % 2, :].rearrange("p (r n) -> p r n", r=2)
                a, b, v = tmp[:, 0, :, :], tmp[:, 1, :, :], tmp[:, 2, :, :]
                decay = sm["mag"][:, j:j + 1].to_broadcast([P, S])
                dve.wait_ge(bu_ps, j + 1)
                mark(mul(a, rot, src))
                mul(b, rot, src[:, ::-1, :]).then_inc(bu_read, 1)
                dve.wait_ge(bu_read, j + 1)
                sync()
                mark(V.tensor_tensor(v[:, 0, :], a[:, 0, :], a[:, 1, :], ALU.add))
                mark(V.tensor_tensor(v[:, 1, :], b[:, 0, :], b[:, 1, :], ALU.subtract))
                sync()
                for r in range(2):
                    mark(V.tensor_tensor_scan(a[:, r, :], decay, v[:, r, :], 0.0, ALU.mult, ALU.add))
                sync()
                mark(mul(b, rot, a))
                mark(mul(v, rot, a[:, ::-1, :]))
                sync()
                if j >= 2:
                    dve.wait_ge(y_ps, j - 1)
                mark(V.tensor_tensor(x_state[:, j % 2, 0, :], b[:, 0, :], b[:, 1, :], ALU.subtract))
                V.tensor_tensor(x_state[:, j % 2, 1, :], v[:, 0, :], v[:, 1, :], ALU.add).then_inc(xs_ready, 1)
                dve.wait_ge(xs_ready, j + 1)
                sync()

            def ssm_out(ct):
                dve.wait_ge(y_ps, 4 * ct + 4)
                if ct == 0:
                    dve.wait_ge(t_read, 2)
                V.scalar_tensor_tensor(yT[:, ct, :], uT[:, ct, :], pcol[:, DS + ct:DS + ct + 1],
                                       y_bank[:, S * (ct % 2):S * (ct % 2) + S], ALU.mult, ALU.add).then_inc(y_read, 1)

            def norm_qk(c):
                dve.wait_ge(qk_sq, 2 * c)
                V.tensor_reduce(n_ss, sq.rearrange("p t (g d) -> p (t g) d", d=64), AX.X, ALU.add).then_inc(qk_ss, 1)
                dve.wait_ge(qk_std, c)
                step(V.reciprocal(n_rs, n_std))
                if c >= 2:
                    dve.wait_ge(t_ps, 2 * c)
                for tt in range(TT):
                    mul(qn[:, tt, :].rearrange("p (g d) -> p g d", d=64),
                        bank[2 * (c % 2) + tt].rearrange("p (g d) -> p g d", d=64),
                        n_rs[:, 8 * tt:8 * tt + 8].unsqueeze(2).to_broadcast([P, 8, 64])).then_inc(qk_n, 1)

            y_done = 0
            for p in range(2, 14):
                if p % 2 and 1 <= p // 2 <= 4:
                    norm_qk(p // 2)
                for j in SSM_AT.get(p, []):
                    state_tile(j)
                    if j % 4 == 1 and j > 4:
                        ssm_out(y_done)
                        y_done += 1
            ssm_out(3)
            V.tensor_scalar(lam_sum, lam_sum, 1.0, None, ALU.mult).then_inc(nmax, 1)
            dve.wait_ge(act_step, 3)
            step(V.tensor_tensor(neg_lam, lam_exp[:, 1:2], lam_exp[:, 0:1], ALU.subtract))
            step(V.tensor_scalar(neg_lam, neg_lam, LAMBDA_INIT, None, ALU.subtract))
            dve.wait_ge(t_ps, 10)
            dve.wait_ge(y_read, 4)
            yf = yT.rearrange("p c n -> p (c n)")
            step(mul(glu_a, yf, yf))
            step(V.tensor_scalar(glu_a, glu_a, 0.044715, 1.0, ALU.mult, ALU.add))
            mul(glu_a, glu_a, yf).then_inc(gel_in, 1)

            for h in range(HEADS):
                dve.wait_ge(s_ps, h + 1)
                for m in range(2):
                    for qt in range(2):
                        cs = slice(0, 128) if qt == 0 else slice(128, 384)
                        cf = causal[:, :, :].rearrange("p b n -> p (b n)")
                        ins = V.tensor_tensor_reduce(out=masked[:, m, cs], in0=pair[:, m, cs], in1=cf[:, cs], scale=1.0,
                                                     scalar=-3e38, op0=ALU.add, op1=ALU.max,
                                                     accum_out=s_max[:, 2 * m + qt:2 * m + qt + 1])
                        ins.then_inc(s_read, 1)
                dve.wait_ge(s_read, 4 * h + 4)
                V.tensor_scalar(n_bias, s_max, -SCALE, None, ALU.mult).then_inc(nmax, 1)
                dve.wait_ge(p_ready, 4 * h + 4)
                step(V.reciprocal(p_rs, p_sum))
                step(V.tensor_scalar(p_c1, p_rs[:, 2:4], neg_lam, None, ALU.mult))
                if h >= 1:
                    dve.wait_ge(aT_ps, h)
                for qt in range(2):
                    cs = slice(0, 128) if qt == 0 else slice(128, 384)
                    mark(V.tensor_scalar(a_mix[:, cs], probs[:, 1, cs], p_c1[:, qt:qt + 1], None, ALU.mult))
                sync()
                for qt in range(2):
                    cs = slice(0, 128) if qt == 0 else slice(128, 384)
                    V.scalar_tensor_tensor(a_mix[:, cs], probs[:, 0, cs], p_rs[:, qt:qt + 1], a_mix[:, cs], ALU.mult,
                                           ALU.add).then_inc(a_ready, 1)
            dve.wait_ge(o_std, 1)
            step(V.reciprocal(o_rs, o_rs))
            for tt in range(TT):
                o3 = o_tok[:, tt, :].rearrange("p (h n) -> p h n", h=HEADS)
                mul(o3, o3, o_rs[:, 8 * tt:8 * tt + 8].unsqueeze(2).to_broadcast([P, HEADS, P])).then_inc(o_norm, 1)
            dve.wait_ge(gel_sig, 1)
            mul(zT[:, :, :].rearrange("p c n -> p (c n)"), yf, glu_g).then_inc(z_ready, 1)
            dve.wait_ge(glu_sig, 4)
            zf = zT[:, :, :].rearrange("p c n -> p (c n)")
            mul(zf, zf, glu_g).then_inc(sout_ready, 1)
            dve.wait_ge(gates_sig, 1)
            for a, first in ((0, P_PSSM), (1, P_PATT)):
                for n in range(2):
                    dve.wait_ge(piece_used, first + (a + 1) * (n + 1))
                    for tt in range(TT):
                        g = sg[:, a, tt, N * n:N * n + N]
                        ins = mul(g, g, bank[2 * n + tt])
                        ins.then_inc(merged_s, 1)
            dve.wait_ge(merged_s, 8)
            for tt in range(TT):
                V.tensor_tensor(merged[:, tt, :], sg[:, 0, tt, :], sg[:, 1, tt, :], ALU.add).then_inc(merged_s, 1)
            for n in range(2):
                dve.wait_ge(piece_used, P_WOUT + 2 * (n + 1))
                for tt in range(TT):
                    ps = pair[:, tt, :] if n == 0 else bank[tt]
                    xs = x_acc[:, tt, N * n:N * n + N]
                    V.tensor_tensor(xs, xs, ps, ALU.add).then_inc(x1_ready, 1)
            dve.wait_ge(x1_std, 1)
            step(V.reciprocal(x_rs, x_std))
            for tt in range(TT):
                V.tensor_scalar(h2[:, tt, :], x_acc[:, tt, :], x_rs[:, tt:tt + 1], None, ALU.mult).then_inc(h2_ready, 1)
            logit, ex, gt, eq, cum, pick, misc = [route[:, i, :, :] for i in range(7)]
            rank_m, gate = gt, ex
            dve.wait_ge(logit_ps, 1)
            mark(V.tensor_tensor(logit[:, 1, :], t_bank[:, E:2 * E], misc[:, 0, :], ALU.add))
            step(V.tensor_tensor(logit[:, 0, :], t_bank[:, 0:E], misc[:, 0, :], ALU.add))
            for tt in range(TT):
                mark(V.max(top8[:, tt, :], logit[:, tt, :]))
            sync()
            for tt in range(TT):
                V.tensor_scalar(neg_top[:, tt:tt + 1], top8[:, tt, 0:1], -1.0, None, ALU.mult).then_inc(top_ready, 1)
            for tt in range(TT):
                least = top8[:, tt, 3:4]
                mark(V.tensor_scalar(gt[:, tt, :], logit[:, tt, :], least, 0.0, ALU.is_gt, ALU.add,
                                     accum_out=over[:, tt:tt + 1]))
                mark(V.tensor_scalar(eq[:, tt, :], logit[:, tt, :], least, None, ALU.is_equal))
            sync()
            mark(V.tensor_scalar(need, over, -1.0, 4.0, ALU.mult, ALU.add))
            for tt in range(TT):
                mark(V.tensor_tensor_scan(cum[:, tt, :], ones[:, 0:E], eq[:, tt, :], 0.0, ALU.mult, ALU.add))
            sync()
            for tt in range(TT):
                mark(V.scalar_tensor_tensor(pick[:, tt, :], cum[:, tt, :], need[:, tt:tt + 1], eq[:, tt, :], ALU.is_le, ALU.mult))
            sync()
            V.tensor_tensor(pick, pick, gt, ALU.add).then_inc(picked, 1)
            dve.wait_ge(picked, 1)
            dve.wait_ge(gexp, 2)
            for tt in range(TT):
                mark(V.tensor_tensor_reduce(out=ex[:, tt, :], in0=ex[:, tt, :], in1=pick[:, tt, :], scale=1.0, scalar=0.0,
                                            op0=ALU.mult, op1=ALU.add, accum_out=g_sum[:, tt:tt + 1]))
            sync()
            step(V.reciprocal(g_rs, g_sum))
            for tt in range(TT):
                V.tensor_scalar(gate[:, tt, :], ex[:, tt, :], g_rs[:, tt:tt + 1], None, ALU.mult).then_inc(gates_ready, 1)
            dve.wait_ge(gates_ready, 2)
            dve.wait_ge(rank_ps, 1)
            step(V.scalar_tensor_tensor(rank_m, y_bank[:, 0:2 * E].rearrange("p (t e) -> p t e", t=TT), 1.0, pick, ALU.add,
                                        ALU.mult))
            mark(V.tensor_scalar(rank_m, rank_m, 1.0, None, ALU.subtract))
            counts = cum[:, 0, :]
            V.tensor_copy(counts, y_bank[:, 2 * E:3 * E]).then_inc(picked, 1)
            dve.wait_ge(picked, 2)
            sync()

            def slots(e, base):
                return [(iota[:, bass.ds(base, SLOT)], rank_m[:, tt, bass.ds(e, 1)], gate[:, tt, bass.ds(e, 1)])
                        for tt in range(TT)]

            def select(i, e, base):
                if not (isinstance(i, int) and i == 0):
                    dve.wait_ge(xg_ps, i)
                for tt, (at, rank, _) in enumerate(slots(e, base)):
                    V.tensor_scalar(sel[:, tt, :], at, rank, None, ALU.is_equal).then_inc(sel_ready, 1)

            def take_x(i):
                dve.wait_ge(xg_ps, i + 1)
                mul(xT, ps_xg.rearrange("p (k n) -> p k n", k=KT),
                    pcol[:, G2:G2 + KT].unsqueeze(2).to_broadcast([P, KT, SLOT])).then_inc(xT_ready, 1)

            def add_block(i, tt):
                dve.wait_ge(comb_ps, 2 * i + tt + 1)
                acc = x_acc[:, tt, :].rearrange("p (b n) -> p b n", b=2)
                V.tensor_tensor(acc, acc, pair[:, :, :], ALU.add).then_inc(added, 1)

            select(0, 0, 0)
            for tt in range(TT):
                dve.wait_ge(bias2_ps, tt + 1)
                acc = x_acc[:, tt, :].rearrange("p (b n) -> p b n", b=2)
                V.tensor_tensor(acc, acc, pair[:, :, :], ALU.add).then_inc(added, 1)
            dve.wait_ge(added, 2)
            take_x(0)

            def block_work(i, e, base, first, last):
                if not last:
                    select(i + 1, i + 1, 0)
                if not (isinstance(i, int) and i == 0):
                    dve.wait_ge(put_ps, i)
                for tt, (at, rank, g) in enumerate(slots(e, base)):
                    for c in range(2):
                        V.tensor_scalar(sel_g[:, tt, SLOT * c:SLOT * c + SLOT], at, rank, g, ALU.is_equal,
                                        ALU.mult).then_inc(selg_ready, 1)
                dve.wait_ge(hid_ps, i + 1)
                hid = bank01[:, :, :].rearrange("p b (n w) -> p b n w", w=2)
                ga, ua = (v.rearrange("p (b n) -> p b n", b=2) for v in (g_act, u_act))
                V.tensor_scalar(ga, hid[:, :, :, 0], 7.0, None, ALU.min).then_inc(g_ready, 1)
                V.tensor_scalar(ua, hid[:, :, :, 1], 7.0, -7.0, ALU.min, ALU.max).then_inc(hid_read, 1)
                dve.wait_ge(g_ready, i + 1)
                dve.wait_ge(hid_read, i + 1)
                V.scalar_tensor_tensor(u_act, u_act, 1.0, g_act, ALU.add, ALU.mult).then_inc(um_ready, 1)
                dve.wait_ge(um_ready, i + 1)
                dve.wait_ge(sig_ready, i + 1)
                mul(u_act, u_act, s_act).then_inc(act_ready, 1)
                if not last:
                    take_x(i + 1)
                if not first:
                    add_block(i - 1, 0)
                    add_block(i - 1, 1)

            block_work(0, 0, 0, True, False)
            for c in range(3):
                mark(V.tensor_scalar(flag[:, E * c:E * c + E], counts[0:1, :], float(SLOT * (c + 1)), None, ALU.is_gt))
                mark(V.memset(flag_b[:, E * c:E * c + E], float(SLOT * (c + 1))))
            sync()
            step(V.tensor_tensor_scan(flag_pos, ones[0:1, 0:96], flag, 0.0, ALU.mult, ALU.add))
            mark(V.tensor_copy(table_f[:, 0:1], flag_pos[:, 95:96]))
            mark(V.tensor_copy(table_f[:, 1:2], flag_pos[:, 95:96]))
            mark(mul(flag_e.rearrange("p (c e) -> p c e", c=3), flag.rearrange("p (c e) -> p c e", c=3),
                     iota[0:1, 0:E].unsqueeze(1).to_broadcast([1, 3, E])))
            mark(mul(flag_b, flag_b, flag))
            sync()
            step(V.tensor_tensor(flag_pos, flag_pos, flag, ALU.subtract))
            for w_, at in ((flag_e, 2), (flag_b, 2 + MAX_EXTRA)):
                step(V.tensor_tensor(big, flag_pos.unsqueeze(1).to_broadcast([1, MAX_EXTRA, 96]),
                                     iota[0:1, 0:MAX_EXTRA].unsqueeze(2).to_broadcast([1, MAX_EXTRA, 96]), ALU.is_equal))
                step(mul(big, big, w_.unsqueeze(1).to_broadcast([1, MAX_EXTRA, 96])))
                step(V.tensor_reduce(table_f[:, at:at + MAX_EXTRA], big, AX.X, ALU.add))
            V.tensor_copy(table[:, :], table_f).then_inc(table_ready, 1)

            with dve.Fori(1, E - 1) as i:
                block_work(i, i, 0, False, False)
            block_work(E - 1, E - 1, 0, False, True)
            add_block(E - 1, 0)
            add_block(E - 1, 1)
            dve.wait_ge(table_ready, 1)
            extra = dve.value_load(table[0:1, 0:1], min_val=0, max_val=MAX_EXTRA)
            with dve.If(extra > 0):
                with dve.Fori(0, extra) as j:
                    e = dve.value_load(table[0:1, bass.ds(j + 2, 1)], min_val=0, max_val=E - 1)
                    base = dve.value_load(table[0:1, bass.ds(j + 2 + MAX_EXTRA, 1)], min_val=0, max_val=3 * SLOT)
                    i = j + E
                    select(i, e, base)
                    take_x(i)
                    block_work(i, e, base, True, True)
                    add_block(i, 0)
                    add_block(i, 1)

        @block.tensor
        def _(pe):
            T = nc.tensor
            pe.wait_ge(consts, 1)
            pe.wait_ge(h_ready, 2)
            for b in range(4):
                for k in (2 * b, 2 * b + 1):
                    for tt in range(TT):
                        ins = T.transpose(bank[b][:, S * (k % 2) + P * tt:S * (k % 2) + P * tt + P],
                                          h_tok[:, tt, P * k:P * k + P], ident[:, :])
                ins.then_inc(hT_ps, 1)
            pe.wait_ge(prow_ready, 1)
            T.transpose(t_bank[:, 0:P], prow[:, :], ident[:, :]).then_inc(pcol_ps, 1)
            pe.wait_ge(bc_in, 16 * 20)
            for r in range(2):
                for ct in range(CT):
                    ins = T.transpose(pair[:, r, P * ct:P * ct + P],
                                      b_raw[:, r, 4 * ct:4 * ct + 4, :].rearrange("p j c -> p (j c)"), ident[:, :])
                ins.then_inc(b_ps, 1)
            pe.wait_ge(pcol_ready, 1)
            for r, ps in enumerate((t_bank, y_bank)):
                for ct in range(CT):
                    ins = T.transpose(ps[:, P * ct:P * ct + P], c_raw[:, r, ct, :], ident[:, :])
                ins.then_inc(c_ps, 1)

            def piece(i):
                pe.wait_ge(piece_in[i % 4], 16 * (i // 4 + 1))
                return stream[:, i % 4, :].rearrange("p (k n) -> p k n", k=4)

            def products(i, lhs, k0, outs, start, stop):
                w_ = piece(i)
                for tt in range(TT):
                    for k in range(4):
                        ins = T.matmul(outs[tt], lhs[:, k0 + k, P * tt:P * tt + P], w_[:, k, :], start=start and k == 0,
                                       stop=stop and k == 3)
                ins.then_inc(piece_used, 1)

            def in_piece(i):
                c = i // 2
                if i % 2 == 0:
                    if c == 2:
                        pe.wait_ge(chunk_read, 2)
                        pe.wait_ge(hT_act, 4)
                    elif c in (3, 4, 5, 6):
                        pe.wait_ge(qk_n, 2 * (c - 2))
                    elif c > 6:
                        pe.wait_ge(chunk_read, 2 + 2 * (c - 6))
                products(i, hT, 4 * (i % 2), bank[2 * (c % 2):2 * (c % 2) + 2], i % 2 == 0, i % 2 == 1)

            def transposes(c):
                pe.wait_ge(qk_n, 2 * c)
                for r in range(2):
                    pe.wait_ge(t_read, 2 * c + r)
                    for hh in range(2):
                        for tt in range(TT):
                            ins = T.transpose(t_bank[:, S * hh + P * tt:S * hh + P * tt + P],
                                              qn[:, tt, P * (2 * r + hh):P * (2 * r + hh) + P], ident[:, :])
                    ins.then_inc(t_ps, 1)

            def inputs(j):
                ct, jj = j // 4, j % 4
                if j >= 2:
                    pe.wait_ge(bu_read, j - 1)
                if j == 0:
                    pe.wait_ge(bT_ready, 2)
                    pe.wait_ge(t_read, 2)
                for r in range(2):
                    ins = T.matmul(pair[:, j % 2, S * r:S * r + S], bT[32 * jj:32 * jj + 32, ct, r, :],
                                   uT[32 * jj:32 * jj + 32, ct, :], start=True, stop=True, tile_position=(32 * jj, 0))
                ins.then_inc(bu_ps, 1)

            def outputs(j):
                ct, jj = j // 4, j % 4
                pe.wait_ge(xs_ready, j + 1)
                if jj == 0 and ct >= 1:
                    pe.wait_ge(y_read, ct)
                for r in range(2):
                    ins = T.matmul(y_bank[32 * jj:32 * jj + 32, S * (ct % 2):S * (ct % 2) + S], cT[:, r, j, :],
                                   x_state[:, j % 2, r, :], start=(r == 0), stop=(r == 1), tile_position=(0, 32 * jj))
                ins.then_inc(y_ps, 1)

            pe.wait_ge(hT_dve, 4)
            pe.wait_ge(hT_act, 4)
            for p in range(14):
                in_piece(p)
                if p == 2:
                    pe.wait_ge(chunk_read, 2)
                    pe.wait_ge(cT_ready, 2)
                    for ps, c0 in ((t_bank, 0), (y_bank, 2)):
                        for ct in (c0, c0 + 1):
                            for tt in range(TT):
                                ins = T.transpose(ps[:, S * (ct - c0) + P * tt:S * (ct - c0) + P * tt + P],
                                                  u_tok[:, tt, P * ct:P * ct + P], ident[:, :])
                        ins.then_inc(t_ps, 1)
                if p % 2 == 0 and 2 <= p // 2 <= 5:
                    transposes(p // 2 - 1)
                for j in SSM_AT.get(p, []):
                    inputs(j)
                    if j >= 2:
                        outputs(j - 2)
            outputs(NST - 2)
            outputs(NST - 1)

            def scores(h):
                if h == 0:
                    pe.wait_ge(t_read, 10)
                    pe.wait_ge(bu_read, NST)
                else:
                    pe.wait_ge(s_read, 4 * h)
                for qt in range(2):
                    for m in range(2):
                        a = slice(64 * m, 64 * m + 64)
                        ins = T.matmul(pair[:, m, 128 * qt:128 * qt + 128 * (qt + 1)], qT[a, h, P * qt:P * qt + P],
                                       kT[a, h, 0:P * (qt + 1)], start=(qt == 0), stop=True, tile_position=(64 * m, 0),
                                       skip_group_check=True)
                ins.then_inc(s_ps, 1)

            def mix(h):
                pe.wait_ge(a_ready, 2 * h + 2)
                if h >= 1:
                    pe.wait_ge(aT_ready, h)
                for b in range(3):
                    ins = T.transpose(t_bank[:, P * b:P * b + P], a_mix[:, P * b:P * b + P], ident[:, :])
                ins.then_inc(aT_ps, 1)

            def values(h):
                pe.wait_ge(aT_ready, h + 1)
                if h == 0:
                    pe.wait_ge(y_read, 4)
                    pe.wait_ge(chunk_read, 6)
                else:
                    pe.wait_ge(o_read, 4 * h)
                hs = slice(P * h, P * h + P)
                T.matmul(y_bank[:, 0:P], aT[:, 0, :], v_tok[:, 0, hs], start=True, stop=True)
                T.matmul(y_bank[:, P:2 * P], aT[:, 1, :], v_tok[:, 0, hs], start=True, stop=False)
                T.matmul(y_bank[:, P:2 * P], aT[:, 2, :], v_tok[:, 1, hs], start=False, stop=True).then_inc(o_ps, 1)

            scores(0)
            for h in range(HEADS):
                in_piece(14 + h)
                mix(h)
                if h + 1 < HEADS:
                    scores(h + 1)
                values(h)
            pe.wait_ge(o_norm, 2)
            pe.wait_ge(chunk_read, 14)
            for b in range(4):
                for h in (2 * b, 2 * b + 1):
                    for tt in range(TT):
                        ins = T.transpose(bank[b][:, S * (h % 2) + P * tt:S * (h % 2) + P * tt + P],
                                          o_tok[:, tt, P * h:P * h + P], ident[:, :])
                ins.then_inc(oT_ps, 1)
            pe.wait_ge(z_ready, 1)
            w_ = piece(P_GLU)
            for co in range(CT):
                for k in range(CT):
                    ins = T.matmul(pair[:, co // 2, S * (co % 2):S * (co % 2) + S], w_[:, k, P * co:P * co + P], zT[:, k, :],
                                   start=(k == 0), stop=(k == 3))
                if co == 1:
                    ins.then_inc(glu_ps, 1)
            ins.then_inc(piece_used, 1)
            pe.wait_ge(sout_ready, 1)
            pe.wait_ge(oT_ready, 4)
            for n in range(2):
                products(P_PSSM + n, zT, 0, bank[2 * n:2 * n + 2], True, True)
            for n in range(2):
                pe.wait_ge(merged_s, 2 * n + 2)
                for kh in range(2):
                    products(P_PATT + 2 * n + kh, oT, 4 * kh, bank[2 * n:2 * n + 2], kh == 0, kh == 1)
            pe.wait_ge(merged_s, 10)
            for b in range(4):
                for k in (2 * b, 2 * b + 1):
                    for tt in range(TT):
                        ins = T.transpose(bank[b][:, S * (k % 2) + P * tt:S * (k % 2) + P * tt + P],
                                          merged[:, tt, P * k:P * k + P], ident[:, :])
                ins.then_inc(mT_ps, 1)
            pe.wait_ge(mT_ready, 4)
            for n in range(2):
                for kh in range(2):
                    outs = [pair[:, 0, :], pair[:, 1, :]] if n == 0 else bank[0:2]
                    products(P_WOUT + 2 * n + kh, hT, 4 * kh, outs, kh == 0, kh == 1)
            pe.wait_ge(h2_ready, 2)
            for b in range(4):
                for k in (2 * b, 2 * b + 1):
                    for tt in range(TT):
                        ins = T.transpose(bank[b][:, S * (k % 2) + P * tt:S * (k % 2) + P * tt + P],
                                          h2[:, tt, P * k:P * k + P], ident[:, :])
                ins.then_inc(h2T_ps, 1)
            pe.wait_ge(h2T_ready, KT)
            for tt in range(TT):
                for k in range(KT):
                    ins = T.matmul(t_bank[:, E * tt:E * tt + E], hT[:, k, P * tt:P * tt + P], w_r[:, k, :], start=(k == 0),
                                   stop=(k == KT - 1))
            ins.then_inc(logit_ps, 1)
            pe.wait_ge(picked, 1)
            pick = route[:, 5, :, :]
            T.matmul(y_bank[:, 0:E], before[:, :], pick[:, 0, :], start=True, stop=True)
            T.matmul(y_bank[:, E:2 * E], ones[:, :], pick[:, 0, :], start=True, stop=False)
            T.matmul(y_bank[:, E:2 * E], before[:, :], pick[:, 1, :], start=False, stop=True)
            T.matmul(y_bank[:, 2 * E:3 * E], ones[:, :], pick[:, 0, :], start=True, stop=False)
            T.matmul(y_bank[:, 2 * E:3 * E], ones[:, :], pick[:, 1, :], start=False, stop=True).then_inc(rank_ps, 1)
            pe.wait_ge(gates_ready, 2)
            for tt in range(TT):
                ins = T.transpose(t_bank[0:E, P * tt:P * tt + P], route[:, 1, tt, :], ident[:, :])
            ins.then_inc(gT_ps, 1)

            def gather(i):
                pe.wait_ge(sel_ready, 2 * i + 2)
                for k in range(KT):
                    for tt in range(TT):
                        ins = T.matmul(ps_xg[:, SLOT * k:SLOT * k + SLOT], h2[:, tt, P * k:P * k + P], sel[:, tt, :],
                                       start=(tt == 0), stop=(tt == 1))
                ins.then_inc(xg_ps, 1)

            def combine(i, tt):
                if tt == 0:
                    pe.wait_ge(y_ready, i + 1)
                    pe.wait_ge(put_ready, i + 1)
                pe.wait_ge(added, 2 * i + tt + 2)
                for c in range(2):
                    h = slice(SLOT * c, SLOT * c + SLOT)
                    ins = T.matmul(pair[:, c, :], put[h, P * tt:P * tt + P], y_sb[h, :], start=True, stop=True,
                                   tile_position=(SLOT * c, 0))
                ins.then_inc(comb_ps, 1)

            gather(0)
            pe.wait_ge(gT_ready, 1)
            pe.wait_ge(b2_in, 16)
            for tt in range(TT):
                if tt:
                    pe.wait_ge(added, 1)
                for c in range(2):
                    ins = T.matmul(pair[:, c, :], gateT[:, P * tt:P * tt + P], b2_sb[:, N * c:N * c + N], start=True, stop=True)
                ins.then_inc(bias2_ps, 1)
            def block_work(i, first, last):
                later = not (isinstance(i, int) and i == 0)
                pe.wait_ge(xT_ready, i + 1)
                if later:
                    pe.wait_ge(hid_read, i)
                order = (0, 2, 1, 3)
                for k in range(W1P):
                    pe.wait_ge(w1_in[k], (i + 1) * 16)
                    for n in order:
                        h = SLOT * (n // 2)
                        ins = T.matmul(bank01[h:h + SLOT, n % 2, :], xT[:, k, :], ring[:, k, N * n:N * n + N], start=(k == 0),
                                       stop=False)
                    ins.then_inc(w1_used, 1)
                pe.wait_ge(b1_in, (i + 1) * 16)
                for n in order:
                    h = SLOT * (n // 2)
                    ins = T.matmul(bank01[h:h + SLOT, n % 2, :], ones[0:1, 0:SLOT], b1_row[:, N * n:N * n + N], start=False,
                                   stop=True)
                ins.then_inc(hid_ps, 1)
                if not last:
                    gather(i + 1)
                if not first:
                    combine(i - 1, 0)
                pe.wait_ge(act_ready, i + 1)
                for j in range(4):
                    ins = T.transpose(ps_act[:, P * j:P * j + P], u_act[:, P * j:P * j + P], ident[:, :])
                ins.then_inc(actT_ps, 1)
                if not first:
                    combine(i - 1, 1)
                pe.wait_ge(selg_ready, 4 * i + 4)
                if later:
                    pe.wait_ge(put_ready, i)
                for tt in range(TT):
                    ins = T.transpose(ps_put[:, P * tt:P * tt + P], sel_g[:, tt, :], ident[:, :])
                ins.then_inc(put_ps, 1)
                pe.wait_ge(actT_ready, i + 1)
                if later:
                    pe.wait_ge(y_ready, i)
                for m in range(W2P):
                    pe.wait_ge(w2_in[m], (i + 1) * 16)
                    for f in (2 * m, 2 * m + 1):
                        for c in range(2):
                            h = SLOT * c
                            ins = T.matmul(ps_y[h:h + SLOT, :], actT[:, f % 4, SLOT * (f // 4):SLOT * (f // 4) + SLOT],
                                           ring_w2(m)[:, f % 2, N * c:N * c + N], start=(f == 0), stop=(f == KT - 1))
                    ins.then_inc(w2_used, 1)

            block_work(0, True, False)
            with pe.Fori(1, E - 1) as i:
                block_work(i, False, False)
            block_work(E - 1, False, True)
            combine(E - 1, 0)
            combine(E - 1, 1)
            pe.wait_ge(table_ready, 1)
            extra = pe.value_load(table[0:1, 0:1], min_val=0, max_val=MAX_EXTRA)
            with pe.If(extra > 0):
                with pe.Fori(0, extra) as j:
                    i = j + E
                    gather(i)
                    block_work(i, True, True)
                    combine(i, 0)
                    combine(i, 1)


_INS = ["x", "norm1_gain", "w_in", "lambda_re", "lambda_im", "log_dt", "ssm_b_re", "ssm_b_im", "ssm_c_re", "ssm_c_im",
        "ssm_d", "w_glu", "b_glu", "q_norm_gain", "k_norm_gain", "lambda_q1", "lambda_k1", "lambda_q2", "lambda_k2",
        "subln_gain", "w_proj_ssm", "w_proj_attn", "w_out", "norm2_gain", "w_router", "b_router", "w_exp1", "b_exp1",
        "w_exp2", "b_exp2"]


def kernel(**inputs):
    import numpy as _np
    import concourse.bacc as _bacc
    from concourse import mybir as _mybir
    from concourse.bass_utils import run_bass_kernel_spmd as _run

    nc = _bacc.Bacc("TRN2", target_bir_lowering=False, num_devices=1)
    arrays, tensors = {}, {}
    for name in _INS:
        a = _np.ascontiguousarray(inputs[name])
        arrays[f"in_{name}"] = a
        tensors[name] = nc.dram_tensor(f"in_{name}", a.shape, _mybir.dt.from_np(a.dtype), kind="ExternalInput").ap()
    out = nc.dram_tensor("out", (1, S, D), _mybir.dt.from_np(_np.dtype("float32")), kind="ExternalOutput").ap()
    hybrid_block(nc, tensors, out)
    r = _run(nc, [arrays], core_ids=[0])
    return r.results[0]["out"]
```

```python
import math
from contextlib import ExitStack

import concourse.bass as bass
from concourse import mybir

ALU = mybir.AluOpType
ACT = mybir.ActivationFunctionType
AX = mybir.AxisListType
F32 = mybir.dt.float32
I32 = mybir.dt.int32

P = 128
D = 1024
S = 256
TT = S // P
KT = D // P
SW = 512
CT = SW // P
NST = 16
HEADS = 8
E = 32
FF = 1024
SLOT = 64
NB = E // 2
N = 512
EPS = 1e-5
LAMBDA_INIT = 0.8 - 0.6 * math.exp(-0.3 * 0)
SCALE = 0.125
MASKED = -1e30
MAGIC = 1.5 * 2.0 ** 23
LOG2E = 1.4426950408889634
LN2_HI, LN2_LO = 0.693359375, -2.12194440e-4
INV_2PI = 0.15915494309189535
TWO_PI_1 = 6.28125
TWO_PI_2 = 0.0019350051879882812
TWO_PI_3 = 2 * math.pi - TWO_PI_1 - TWO_PI_2
NO_SLOT = 4 * SLOT
MAX_EXTRA = 16
W1P, W2P = 8, 4
RING = 16
STREAM = 12

LRE, LIM, LDT, G1, BG, DS, SG, QG, KG, G2 = 0, 32, 64, 96, 104, 108, 112, 113, 114, 115

P_GLU, P_PSSM, P_PATT, P_WOUT, N_PIECES = 22, 23, 25, 29, 33
SSM_AT = {4 + j: j for j in range(NST)}


def hybrid_block(nc, t, out):
    x_d, w_in_d = t["x"], t["w_in"]
    ctx = ExitStack()
    with ctx:
        def sb(name, shape, dt=F32):
            return ctx.enter_context(nc.sbuf_tensor(name, shape, dt))

        def sem(name):
            return ctx.enter_context(nc.semaphore(name))

        bank01 = ctx.enter_context(nc.psum_tensor("bank01", [P, 2, N], F32))
        bank23 = ctx.enter_context(nc.psum_tensor("bank23", [P, 2, N], F32))
        bank = [bank01[:, 0, :], bank01[:, 1, :], bank23[:, 0, :], bank23[:, 1, :]]
        t_bank = ctx.enter_context(nc.psum_tensor("t_bank", [P, N], F32))
        y_bank = ctx.enter_context(nc.psum_tensor("y_bank", [P, N], F32))
        pair = ctx.enter_context(nc.psum_tensor("pair", [P, 2, N], F32))

        ring = sb("ring", [P, RING, 2048])
        x_acc = sb("x_acc", [P, TT, D])
        hT = sb("hT", [P, KT, S])
        uu = sb("uu", [P, 2048])
        qs = sb("qs", [P, 2048])
        zT = sb("zT", [P, CT, S])
        sg = sb("sg", [P, 2, TT, D])
        tmp = sb("tmp", [P, 3, 2, S])
        ident = sb("ident", [P, P])
        ones = sb("ones", [P, P])
        before = sb("before", [P, P])
        causal = sb("causal", [P, 3, P])
        iota = sb("iota", [P, 5 * SLOT])
        prow = sb("prow", [P, P])
        pcol = sb("pcol", [P, P])
        bT = sb("bT", [P, CT, 2, P])
        cT = sb("cT", [P, 2, NST, 32])
        lq = sb("lq", [P, 4, 64])
        w_r = sb("w_r", [P, KT, E])
        small = sb("small", [P, 26, NST])
        stat = sb("stat", [P, 160])
        ldt2 = sb("ldt2", [P, 2])
        route = sb("route", [P, 7, TT, E])
        gateT = sb("gateT", [E, S])
        table = sb("table", [1, 2 + 2 * MAX_EXTRA], I32)

        v_tok = ring[:, 2, :].rearrange("p (t n) -> p t n", t=TT)
        o_tok = ring[:, 3, :].rearrange("p (t n) -> p t n", t=TT)
        att = ring[:, 4:6, :].rearrange("p a n -> p (a n)")
        masked = att[:, 0:768].rearrange("p (m n) -> p m n", m=2)
        probs = att[:, 768:1536].rearrange("p (m n) -> p m n", m=2)
        a_mix = att[:, 1536:1920]
        aT = att[:, 1920:2304].rearrange("p (b n) -> p b n", b=3)
        o_sq = att[:, 2304:2560].rearrange("p (t n) -> p t n", t=TT)
        b_raw = att[:, 0:1024].rearrange("p (r j c) -> p r j c", r=2, j=NST)
        c_raw = att[:, 1024:2048].rearrange("p (r c n) -> p r c n", r=2, c=CT)
        glu_a = qs[:, 0:1024]
        glu_g = qs[:, 1024:2048]
        x_state = att[:, 3072:4096].rearrange("p (b r n) -> p b r n", b=2, r=2)
        qT = ring[:, 6, :].rearrange("p (h n) -> p h n", h=HEADS)
        kT = ring[:, 7, :].rearrange("p (h n) -> p h n", h=HEADS)
        turn = ring[:, 8:12, :].rearrange("p a n -> p (a n)").rearrange("p (j r n) -> p j r n", j=NST, r=2)
        u_tok = uu[:, 0:1024].rearrange("p (t n) -> p t n", t=TT)
        yT = uu[:, 0:1024].rearrange("p (c n) -> p c n", c=CT)
        uT = uu[:, 1024:2048].rearrange("p (c n) -> p c n", c=CT)
        merged = uu[:, :].rearrange("p (t n) -> p t n", t=TT)
        qn = qs[:, 0:1024].rearrange("p (t n) -> p t n", t=TT)
        sq = qs[:, 1024:2048].rearrange("p (t n) -> p t n", t=TT)
        oT = qs[:, :].rearrange("p (h n) -> p h n", h=HEADS)
        h2 = qs[:, :].rearrange("p (t n) -> p t n", t=TT)
        sgf = sg[:, :, :, :].rearrange("p a t n -> p (a t n)")
        h_tok = sgf[:, 0:2048].rearrange("p (t n) -> p t n", t=TT)
        sq_x = sgf[:, 2048:4096].rearrange("p (t n) -> p t n", t=TT)
        turn_t = sgf[:, 0:4096].rearrange("p (a j n) -> p a j n", a=2, j=NST)
        glu_t = sgf[:, 0:1024]
        xT = zT[:, :, :].rearrange("p c n -> p (c n)").rearrange("p (k n) -> p k n", k=KT)
        g_act = uu[:, 0:1024]
        u_act = uu[:, 1024:2048]
        s_act = sgf[:, 0:1024]
        actT = sgf[:, 1024:2048].rearrange("p (f n) -> p f n", f=KT)
        y_sb = sgf[:, 2048:3072]
        sel = sgf[:, 3072:3328].rearrange("p (t n) -> p t n", t=TT)
        sel_g = sgf[:, 3328:3584].rearrange("p (t n) -> p t n", t=TT)
        put = sgf[:, 3584:3840]
        b2_sb = tmp[0:E, 0:2, :, :].rearrange("p a b n -> p (a b n)")
        b1_rows = hT[:, :, :].rearrange("p k n -> p (k n)")
        big = tmp[0:1, :, :, :].rearrange("p a b n -> p (a b n)").rearrange("p (a b) -> p a b", a=MAX_EXTRA)
        smf = small[0:1, :, :].rearrange("p a n -> p (a n)")
        flag, flag_e, flag_b, flag_pos = (smf[:, 96 * i:96 * i + 96] for i in range(4))
        table_f = lq[0:1, 0, 0:2 + 2 * MAX_EXTRA]

        x_in = sem("x_in")
        prow_in = sem("prow_in")
        bc_in = sem("bc_in")
        misc_in = sem("misc_in")
        b2_in = sem("b2_in")
        piece_in = [sem(f"piece_in{i}") for i in range(4)]
        w1_in = [sem(f"w1_in{i}") for i in range(W1P)]
        w2_in = [sem(f"w2_in{i}") for i in range(W2P)]
        b1_in = sem("b1_in")
        out_in = sem("out_in")
        zeroed = sem("zeroed")
        consts = sem("consts")
        pool_step = sem("pool_step")
        turns_ready = sem("turns_ready")
        dve_step = sem("dve_step")
        act_step = sem("act_step")
        prow_ready = sem("prow_ready")
        x_sq = sem("x_sq")
        h_ready = sem("h_ready")
        pcol_ps = sem("pcol_ps")
        pcol_ready = sem("pcol_ready")
        hT_ps = sem("hT_ps")
        hT_dve = sem("hT_dve")
        hT_act = sem("hT_act")
        b_ps = sem("b_ps")
        c_ps = sem("c_ps")
        c_read = sem("c_read")
        bT_ready = sem("bT_ready")
        cT_ready = sem("cT_ready")
        sin_in = sem("sin_in")
        sin_ready = sem("sin_ready")
        turn_base = sem("turn_base")
        piece_used = sem("piece_used")
        chunk_read = sem("chunk_read")
        qk_sq = sem("qk_sq")
        qk_ss = sem("qk_ss")
        qk_std = sem("qk_std")
        qk_n = sem("qk_n")
        t_ps = sem("t_ps")
        t_read = sem("t_read")
        bu_ps = sem("bu_ps")
        bu_read = sem("bu_read")
        xs_ready = sem("xs_ready")
        y_ps = sem("y_ps")
        y_read = sem("y_read")
        s_ps = sem("s_ps")
        s_read = sem("s_read")
        nmax = sem("nmax")
        p_ready = sem("p_ready")
        a_ready = sem("a_ready")
        aT_ps = sem("aT_ps")
        aT_ready = sem("aT_ready")
        o_ps = sem("o_ps")
        o_read = sem("o_read")
        o_std = sem("o_std")
        o_norm = sem("o_norm")
        oT_ps = sem("oT_ps")
        oT_ready = sem("oT_ready")
        gel_in = sem("gel_in")
        gel_sig = sem("gel_sig")
        z_ready = sem("z_ready")
        glu_ps = sem("glu_ps")
        glu_sig = sem("glu_sig")
        sout_ready = sem("sout_ready")
        gates_sig = sem("gates_sig")
        merged_s = sem("merged_s")
        mT_ps = sem("mT_ps")
        mT_ready = sem("mT_ready")
        x1_ready = sem("x1_ready")
        x1_std = sem("x1_std")
        x1_sq = sem("x1_sq")
        x1_ss = sem("x1_ss")
        h2_ready = sem("h2_ready")
        h2T_ps = sem("h2T_ps")
        h2T_ready = sem("h2T_ready")
        logit_ps = sem("logit_ps")
        top_ready = sem("top_ready")
        gexp = sem("gexp")
        picked = sem("picked")
        rank_ps = sem("rank_ps")
        gates_ready = sem("gates_ready")
        gT_ps = sem("gT_ps")
        gT_ready = sem("gT_ready")
        table_ready = sem("table_ready")
        w1_used = sem("w1_used")
        w2_used = sem("w2_used")
        sel_ready = sem("sel_ready")
        selg_ready = sem("selg_ready")
        xg_ps = sem("xg_ps")
        xT_ready = sem("xT_ready")
        hid_ps = sem("hid_ps")
        g_ready = sem("g_ready")
        hid_read = sem("hid_read")
        um_ready = sem("um_ready")
        sig_ready = sem("sig_ready")
        act_ready = sem("act_ready")
        actT_ps = sem("actT_ps")
        actT_ready = sem("actT_ready")
        put_ps = sem("put_ps")
        put_ready = sem("put_ready")
        y_ready = sem("y_ready")
        comb_ps = sem("comb_ps")
        added_half = sem("added_half")
        added = sem("added")

        ps_xg = [t_bank, y_bank]
        ps_act, ps_put = bank01, bank[2]
        ps_y = pair
        bu_bank, yo_bank = bank[2], bank[3]

        def col(a, n=1):
            return stat[:, a:a + n]
        x_ss, x_std, x_rs = col(0, 2), col(2, 2), col(4, 2)
        n_ss, n_std, n_rs = col(6, 16), col(22, 16), col(38, 16)
        lam_sum, lam_exp, neg_lam = col(54, 2), col(56, 2), col(58)
        s_max, n_bias, p_sum, p_rs = col(60, 4), col(64, 4), col(68, 4), col(72, 4)
        p_c1 = col(76, 2)
        o_ss, o_rs = col(80, 16), col(96, 16)
        top8 = stat[:, 112:128].rearrange("p (t n) -> p t n", t=TT)
        neg_top, over, need, g_sum, g_rs = col(128, 2), col(130, 2), col(132, 2), col(134, 2), col(136, 2)
        x1_parts = col(138, 4)
        sub_gain, half_pi, eps = col(157), col(158), col(159)
        names = ["ldt", "lr", "li", "k", "r", "q", "pw", "dt", "a", "em1", "mag", "th", "thk", "thr", "sh", "ch",
                 "cos", "sin", "vers", "nr", "ai", "den", "t1", "t2", "cr", "ci"]
        sm = {n: small[:, i, :] for i, n in enumerate(names)}

        block = ctx.enter_context(nc.Block())

        def is_first(i):
            return isinstance(i, int) and i == 0

        def chunk_bank(c):
            return pair if c in (1, 3, 5) else bank01

        def stream_source(i):
            def cut(w, kh, n):
                return w[512 * kh:512 * kh + 512, N * n:N * n + N].rearrange("(k p) n -> p k n", p=P)
            if i < P_GLU:
                return cut(w_in_d[0], i % 2, i // 2)
            if i == P_GLU:
                return cut(t["w_glu"][0], 0, 0)
            if i < P_PATT:
                return cut(t["w_proj_ssm"][0], 0, i - P_PSSM)
            if i < P_WOUT:
                return cut(t["w_proj_attn"][0], (i - P_PATT) % 2, (i - P_PATT) // 2)
            return cut(t["w_out"][0], (i - P_WOUT) // 2, (i - P_WOUT) % 2)

        def w1_slot(odd, k, x):
            return (2 * k + x + W1P * odd) % RING

        def w2_slot(odd, m, x):
            return 2 * m + x + W1P * odd

        def w1_load(eng, e, k, x, odd):
            src = t["w_exp1"][0, bass.ds(e, 1), P * k:P * k + P, :].rearrange("e p n -> p (e n)")
            eng.dma_start(ring[:, w1_slot(odd, k, x), :], src).then_inc(w1_in[k], 16)

        def w2_load(eng, e, m, x, odd):
            src = t["w_exp2"][0, bass.ds(e, 1), 2 * P * m:2 * P * m + 2 * P, :].rearrange("e (k p) n -> p (e k) n", p=P)
            eng.dma_start(ring_w2(m, x, odd), src).then_inc(w2_in[m], 16)

        def ring_w2(m, x, odd):
            return ring[:, w2_slot(odd, m, x), :].rearrange("p (k n) -> p k n", k=2)

        prow_loads = [
            (prow[LRE:LRE + NST, :], t["lambda_re"][0].rearrange("(j g) p -> j (g p)", g=2)),
            (prow[LIM:LIM + NST, :], t["lambda_im"][0].rearrange("(j g) p -> j (g p)", g=2)),
            (ldt2[LDT:LDT + NST, :], t["log_dt"][0].rearrange("(j g) -> j g", g=2)),
            (prow[G1:G1 + KT, :], t["norm1_gain"][0].rearrange("(k p) -> k p", p=P)),
            (prow[BG:BG + CT, :], t["b_glu"][0].rearrange("(k p) -> k p", p=P)),
            (prow[DS:DS + CT, :], t["ssm_d"][0].rearrange("(c g) h -> c (g h)", c=CT)),
            (prow[G2:G2 + KT, :], t["norm2_gain"][0].rearrange("(k p) -> k p", p=P)),
            (prow[SG:SG + 1, :], t["subln_gain"]),
        ] + [(prow[r:r + 1, 64 * m:64 * m + 64], t[name]) for r, name in ((QG, "q_norm_gain"), (KG, "k_norm_gain"))
             for m in range(2)]

        @block.sync
        def _(sp):
            sp.dma_start(x_acc[:, :, :], x_d[0].rearrange("(t p) n -> p t n", p=P)).then_inc(x_in, 16)
            sp.wait_ge(zeroed, 1)
            for row, src in prow_loads[1::2]:
                sp.dma_start(row, src).then_inc(prow_in, 16)

            def stream_piece(i):
                if i >= 4:
                    sp.wait_ge(piece_used, i - 3)
                sp.dma_start(ring[:, STREAM + i % 4, :].rearrange("p (k n) -> p k n", k=4),
                             stream_source(i)).then_inc(piece_in[i % 4], 16)

            for i in range(5):
                stream_piece(i)
            for x in range(2):
                w1_load(sp, x, 0, x, 0)
            for i in range(5, P_PSSM):
                stream_piece(i)
            sp.wait_ge(xs_ready, NST)
            for k in (4, 5):
                for x in range(2):
                    w1_load(sp, x, k, x, 0)
            sp.dma_start(b2_sb, t["b_exp2"][0]).then_inc(b2_in, 16)
            for i in range(P_PSSM, P_PATT):
                stream_piece(i)
            sp.wait_ge(oT_ps, 4)
            stream_piece(P_PATT)
            stream_piece(P_PATT + 1)
            for k in (1, 2, 3):
                for x in range(2):
                    w1_load(sp, x, k, x, 0)
            for i in range(P_PATT + 2, N_PIECES):
                stream_piece(i)
            for i, (k, x) in zip(range(P_WOUT, N_PIECES), ((6, 1), (7, 0), (7, 1), (6, 0))):
                sp.wait_ge(piece_used, i + 1)
                w1_load(sp, x, k, x, 0)
            sp.wait_ge(logit_ps, 1)
            for x in range(2):
                sp.dma_start(b1_rows[32 * x:32 * x + 1, :], t["b_exp1"][0, x:x + 1, :]).then_inc(b1_in, 16)

            def load_w2(i, es, odd):
                for m in range(W2P):
                    sp.wait_ge(w1_used, i * W1P + m + 1)
                    for x in range(2):
                        w2_load(sp, es[x], m, x, odd)

            def load_block(i, es, odd, after_odd):
                for k in range(W1P):
                    if k < W1P // 2 and after_odd != odd:
                        sp.wait_ge(w1_used, (i - 1) * W1P + W1P // 2 + k + 1)
                    else:
                        sp.wait_ge(w2_used, (i - 1) * W2P + k % W2P + 1)
                    if k == 0:
                        for x in range(2):
                            sp.dma_start(b1_rows[32 * x:32 * x + 1, :],
                                         t["b_exp1"][0, bass.ds(es[x], 1), :]).then_inc(b1_in, 16)
                    for x in range(2):
                        w1_load(sp, es[x], k, x, odd)
                load_w2(i, es, odd)

            load_w2(0, (0, 1), 0)
            with sp.Fori(1, NB - 1, 2) as i:
                load_block(i, (2 * i, 2 * i + 1), 1, 0)
                load_block(i + 1, (2 * i + 2, 2 * i + 3), 0, 1)
            load_block(NB - 1, (E - 2, E - 1), 1, 0)
            sp.wait_ge(table_ready, 1)
            extra = sp.value_load(table[0:1, 0:1], min_val=0, max_val=MAX_EXTRA // 2)
            with sp.If(extra > 0):
                with sp.Fori(0, extra) as j:
                    es = [sp.value_load(table[0:1, bass.ds(2 * j + 2 + x, 1)], min_val=0, max_val=E - 1) for x in range(2)]
                    load_block(j + NB, es, 0, 0)
            sp.wait_ge(added, (extra + NB + 1) * 2)
            sp.dma_start(out[0].rearrange("(t p) n -> p t n", p=P), x_acc[:, :, :]).then_inc(out_in, 16)
            sp.wait_ge(out_in, 16)

        @block.gpsimd
        def _(pool):
            n_step = [0]

            def step(ins):
                n_step[0] += 1
                ins.then_inc(pool_step, 1)
                pool.wait_ge(pool_step, n_step[0])

            nc.gpsimd.memset(prow[:, :], 0.0).then_inc(zeroed, 1)
            nc.gpsimd.memset(att[:, 0:2048], 0.0).then_inc(zeroed, 1)
            pool.wait_ge(zeroed, 2)
            step(nc.gpsimd.memset(ones[:, :], 1.0))
            step(nc.gpsimd.memset(ident[:, :], 0.0))
            nc.gpsimd.affine_select(out=ident[:, :], in_=ident[:, :], compare_op=ALU.not_equal, fill=1.0, base=0,
                                    pattern=[[-1, P]], channel_multiplier=1).then_inc(consts, 1)
            nc.gpsimd.affine_select(out=before[:, :], in_=ones[:, :], compare_op=ALU.is_gt, fill=0.0, base=0,
                                    pattern=[[1, P]], channel_multiplier=-1).then_inc(consts, 1)
            for r, name in enumerate(("ssm_b_re", "ssm_b_im")):
                src = t[name][0].rearrange("(j g) p h -> g p j h", g=2)
                for g in range(2):
                    pool.dma_start(b_raw[64 * g:64 * g + 64, r, :, 16 * g:16 * g + 16], src[g]).then_inc(bc_in, 16)
            for r, name in enumerate(("ssm_c_re", "ssm_c_im")):
                src = t[name][0].rearrange("(c b) h p -> b h c p", c=CT)
                for b in range(8):
                    g = b % 2
                    pool.dma_start(c_raw[16 * b:16 * b + 16, r, :, 64 * g:64 * g + 64], src[b]).then_inc(bc_in, 16)
            for i, name in enumerate(("lambda_q1", "lambda_k1", "lambda_q2", "lambda_k2")):
                pool.dma_start(lq[:, i, :], t[name][0].partition_broadcast(P)).then_inc(misc_in, 16)
            pool.dma_start(w_r[:, :, :], t["w_router"][0].rearrange("(k p) e -> p k e", p=P)).then_inc(misc_in, 16)
            pool.dma_start(route[:, 6, 0, :], t["b_router"][0].partition_broadcast(P)).then_inc(misc_in, 16)
            step(nc.gpsimd.memset(causal[:, :, :], 0.0))
            for b in (0, 2):
                nc.gpsimd.affine_select(out=causal[:, b, :], in_=causal[:, b, :], compare_op=ALU.is_ge, fill=MASKED,
                                        base=0, pattern=[[-1, P]], channel_multiplier=1).then_inc(consts, 1)
            nc.gpsimd.iota(iota[:, :], pattern=[[1, 5 * SLOT]], base=0, channel_multiplier=0,
                           allow_small_or_imprecise_dtypes=True).then_inc(consts, 1)
            pool.wait_ge(turn_base, 1)
            for half in range(2):
                js = slice(8 * half, 8 * half + 8)
                for n, pr, pi in ((64, "t1", "t2"), (128, "th", "thk")):
                    def wide(name):
                        return sm[name][:, js].unsqueeze(2).to_broadcast([P, 8, n])
                    c0, s0 = turn[:, js, 0, 0:n], turn[:, js, 1, 0:n]
                    a, b = turn_t[:, 0, js, 0:n], turn_t[:, 1, js, 0:n]
                    step(nc.gpsimd.tensor_tensor(a, c0, wide(pr), ALU.mult))
                    step(nc.gpsimd.tensor_tensor(b, s0, wide(pi), ALU.mult))
                    step(nc.gpsimd.tensor_tensor(turn[:, js, 0, n:2 * n], a, b, ALU.subtract))
                    step(nc.gpsimd.tensor_tensor(a, c0, wide(pi), ALU.mult))
                    step(nc.gpsimd.tensor_tensor(b, s0, wide(pr), ALU.mult))
                    if n == 64:
                        step(nc.gpsimd.tensor_tensor(turn[:, js, 1, n:2 * n], a, b, ALU.add))
                    else:
                        nc.gpsimd.tensor_tensor(turn[:, js, 1, n:2 * n], a, b, ALU.add).then_inc(turns_ready, 1)

        @block.scalar
        def _(act):
            act.wait_ge(zeroed, 1)
            for row, src in prow_loads[0::2]:
                act.dma_start(row, src).then_inc(prow_in, 16)
            act.wait_ge(dve_step, 2)
            nc.scalar.activation(x_std, eps.to_broadcast([P, TT]), ACT.Sqrt).then_inc(act_step, 1)
            act.wait_ge(x_in, 16)
            nc.scalar.activation(sq_x[:, 0, :], x_acc[:, 0, :], ACT.Square, accum_out=x_ss[:, 0:1]).then_inc(act_step, 1)
            act.wait_ge(act_step, 2)
            act.wait_ge(dve_step, 3)
            nc.scalar.activation(x_std, x_ss, ACT.Sqrt, bias=eps, scale=1.0 / D).then_inc(x_sq, 1)
            for b in (1, 3):
                act.wait_ge(pcol_ready, 1)
                act.wait_ge(hT_ps, b + 1)
                for k in (2 * b, 2 * b + 1):
                    nc.scalar.activation(hT[:, k, :], bank[b][:, 256 * (k % 2):256 * (k % 2) + 256], ACT.Identity,
                                         scale=pcol[:, G1 + k:G1 + k + 1]).then_inc(hT_act, 1)
            act.wait_ge(sin_in, 1)
            nc.scalar.activation(sm["sh"], sm["thr"], ACT.Sin, scale=0.5).then_inc(sin_ready, 1)
            nc.scalar.activation(sm["ch"], sm["thr"], ACT.Sin, scale=0.5, bias=half_pi).then_inc(sin_ready, 1)
            act.wait_ge(b_ps, 2)
            for r in range(2):
                nc.scalar.copy(bT[:, :, r, :], bank23[:, r, :].rearrange("p (c n) -> p c n", c=CT)).then_inc(bT_ready, 1)
            for r, ps in enumerate((t_bank, y_bank)):
                act.wait_ge(c_ps, r + 1)
                nc.scalar.copy(cT[:, r, :, :], ps[:, :].rearrange("p (j n) -> p j n", j=NST)).then_inc(c_read, 1)

            def copy_t(dst, ps, gain=None, view=None):
                if gain is None:
                    nc.scalar.copy(dst, ps).then_inc(t_read, 1)
                else:
                    nc.scalar.activation(dst, ps, ACT.Identity, scale=gain).then_inc(t_read, 1)

            for c in range(7):
                act.wait_ge(piece_used, 2 * c + 2)
                ps = chunk_bank(c)
                if c == 0:
                    for tt in range(TT):
                        nc.scalar.copy(u_tok[:, tt, :], ps[:, tt, :]).then_inc(chunk_read, 1)
                    act.wait_ge(t_ps, 1)
                    copy_t(uT[:, 0:2, :], t_bank[:, :].rearrange("p (c n) -> p c n", c=2))
                    act.wait_ge(t_ps, 2)
                    copy_t(uT[:, 2:4, :], y_bank[:, :].rearrange("p (c n) -> p c n", c=2))
                elif c < 5:
                    if c >= 2:
                        act.wait_ge(qk_ss, c - 1)
                    for tt in range(TT):
                        nc.scalar.activation(sq[:, tt, :], ps[:, tt, :], ACT.Square).then_inc(qk_sq, 1)
                    act.wait_ge(qk_ss, c)
                    nc.scalar.activation(n_std, n_ss, ACT.Sqrt, bias=eps,
                                         scale=1.0 / 64).then_inc(qk_std, 1)
                    dst, gain = (qT, QG) if c < 3 else (kT, KG)
                    for r in range(2):
                        h = 4 * ((c - 1) % 2) + 2 * r
                        act.wait_ge(t_ps, 2 * c + r + 1)
                        copy_t(dst[:, h:h + 2, :], (t_bank, y_bank)[r][:, :].rearrange("p (h n) -> p h n", h=2), pcol[:, gain:gain + 1])
                else:
                    for tt in range(TT):
                        nc.scalar.copy(v_tok[:, tt, N * (c - 5):N * (c - 5) + N], ps[:, tt, :]).then_inc(chunk_read, 1)

            act.wait_ge(nmax, 1)
            nc.scalar.activation(lam_exp, lam_sum, ACT.Exp).then_inc(act_step, 1)

            def gate_chunk(g):
                act.wait_ge(piece_used, 2 * (7 + g) + 2)
                for tt in range(TT):
                    nc.scalar.copy(sg[:, g // 2, tt, N * (g % 2):N * (g % 2) + N], bank01[:, tt, :]).then_inc(chunk_read, 1)

            for h in range(HEADS):
                act.wait_ge(nmax, h + 2)
                for m in range(2):
                    for qt in range(2):
                        cs = slice(0, 128) if qt == 0 else slice(128, 384)
                        i = 2 * m + qt
                        nc.scalar.activation(probs[:, m, cs], masked[:, m, cs], ACT.Exp, bias=n_bias[:, i:i + 1],
                                             scale=SCALE, accum_out=p_sum[:, i:i + 1]).then_inc(p_ready, 1)
                if h == 1:
                    act.wait_ge(turns_ready, 2)
                if h % 2 and h < HEADS - 1:
                    gate_chunk(h // 2)
                if h == HEADS - 1:
                    act.wait_ge(gel_in, 1)
                    nc.scalar.activation(glu_g, glu_a, ACT.Sigmoid, scale=2 * 0.7978845608028654).then_inc(gel_sig, 1)
                act.wait_ge(aT_ps, h + 1)
                nc.scalar.copy(aT, t_bank[:, 0:384].rearrange("p (b n) -> p b n", b=3)).then_inc(aT_ready, 1)
                act.wait_ge(o_ps, h + 1)
                for qt in range(2):
                    ps = y_bank[:, 128 * qt:128 * qt + 128]
                    nc.scalar.activation(o_sq[:, qt, :], ps, ACT.Square,
                                         accum_out=o_ss[:, 8 * qt + h:8 * qt + h + 1]).then_inc(o_read, 1)
                    nc.scalar.copy(o_tok[:, qt, 128 * h:128 * h + 128], ps).then_inc(o_read, 1)
            gate_chunk(HEADS // 2 - 1)
            act.wait_ge(o_read, 4 * HEADS)
            nc.scalar.activation(o_rs, o_ss, ACT.Sqrt, bias=eps, scale=1.0 / P).then_inc(o_std, 1)
            act.wait_ge(chunk_read, 14)
            nc.scalar.activation(sgf[:, :], sgf[:, :], ACT.Sigmoid).then_inc(gates_sig, 1)
            for ct in range(CT):
                if ct < 2:
                    act.wait_ge(glu_ps, 1)
                else:
                    act.wait_ge(piece_used, P_GLU + 1)
                nc.scalar.activation(glu_g[:, S * ct:S * ct + S], pair[:, ct // 2, S * (ct % 2):S * (ct % 2) + S], ACT.Sigmoid,
                                     bias=pcol[:, BG + ct:BG + ct + 1]).then_inc(glu_sig, 1)
            act.wait_ge(sout_ready, 1)
            for b in range(4):
                act.wait_ge(oT_ps, b + 1)
                nc.scalar.activation(oT[:, 2 * b:2 * b + 2, :], bank[b][:, :].rearrange("p (h n) -> p h n", h=2), ACT.Identity,
                                     scale=sub_gain).then_inc(oT_ready, 1)
            for b in range(4):
                act.wait_ge(mT_ps, b + 1)
                nc.scalar.copy(hT[:, 2 * b:2 * b + 2, :],
                               bank[b][:, :].rearrange("p (h n) -> p h n", h=2)).then_inc(mT_ready, 1)
            def squares(n):
                act.wait_ge(x1_ready, 2 * n + 2)
                for tt in range(TT):
                    nc.scalar.activation(sg[:, 0, tt, N * n:N * n + N], x_acc[:, tt, N * n:N * n + N], ACT.Square,
                                         accum_out=x1_parts[:, 2 * n + tt:2 * n + tt + 1]).then_inc(x1_sq, 1)

            squares(0)
            for half in range(2):
                for b in range(2):
                    act.wait_ge(h2T_ps, 2 * half + b + 1)
                    for kk in range(2):
                        k = 4 * half + 2 * b + kk
                        ps = (bank23[:, b, :] if half == 0 else (t_bank, y_bank)[b])[:, S * kk:S * kk + S]
                        nc.scalar.activation(hT[:, k, :], ps, ACT.Identity, scale=pcol[:, G2 + k:G2 + k + 1]).then_inc(h2T_ready, 1)
            squares(1)
            act.wait_ge(x1_ss, 1)
            nc.scalar.activation(x_std, x_ss, ACT.Sqrt, bias=eps, scale=1.0 / D).then_inc(x1_std, 1)
            for tt in range(TT):
                act.wait_ge(top_ready, tt + 1)
                nc.scalar.activation(route[:, 1, tt, :], route[:, 0, tt, :], ACT.Exp,
                                     bias=neg_top[:, tt:tt + 1]).then_inc(gexp, 1)
            act.wait_ge(gT_ps, 1)
            nc.scalar.copy(gateT[:, :], pair[0:E, 0, 0:S]).then_inc(gT_ready, 1)

            def block_work(i):
                for b in range(2):
                    act.wait_ge(g_ready, 2 * i + b + 1)
                    nc.scalar.activation(s_act[:, N * b:N * b + N], g_act[:, N * b:N * b + N], ACT.Sigmoid,
                                         scale=1.702).then_inc(sig_ready, 1)
                for b in range(2):
                    act.wait_ge(actT_ps, 2 * i + b + 1)
                    nc.scalar.copy(actT[:, 4 * b:4 * b + 4, :],
                                   ps_act[:, b, :].rearrange("p (f n) -> p f n", f=4)).then_inc(actT_ready, 1)
                act.wait_ge(put_ps, i + 1)
                act.wait_ge(comb_ps, 2 * i + 2)
                nc.scalar.copy(put, ps_put[:, 0:S]).then_inc(put_ready, 1)
                act.wait_ge(w2_used, (i + 1) * W2P)
                nc.scalar.copy(y_sb, ps_y[:, :, :].rearrange("p c n -> p (c n)")).then_inc(y_ready, 1)

            block_work(0)
            with act.Fori(1, NB) as i:
                block_work(i)
            act.wait_ge(table_ready, 1)
            extra = act.value_load(table[0:1, 0:1], min_val=0, max_val=MAX_EXTRA // 2)
            with act.If(extra > 0):
                with act.Fori(0, extra) as j:
                    block_work(j + NB)

        @block.vector
        def _(dve):
            V = nc.vector
            n_step = [0]

            def mark(ins):
                n_step[0] += 1
                ins.then_inc(dve_step, 1)

            def sync():
                dve.wait_ge(dve_step, n_step[0])

            def step(ins):
                mark(ins)
                sync()

            def mul(out, a, b):
                return V.tensor_tensor(out, a, b, ALU.mult)

            mark(V.memset(half_pi, math.pi / 2))
            step(V.memset(eps, EPS))
            dve.wait_ge(x_in, 16)
            mark(V.tensor_tensor_reduce(out=sq_x[:, 1, :], in0=x_acc[:, 1, :], in1=x_acc[:, 1, :], scale=1.0, scalar=0.0,
                                        op0=ALU.mult, op1=ALU.add, accum_out=x_ss[:, 1:2]))
            dve.wait_ge(x_sq, 1)
            step(V.reciprocal(x_rs, x_std))
            for tt in range(TT):
                V.tensor_scalar(h_tok[:, tt, :], x_acc[:, tt, :], x_rs[:, tt:tt + 1], None, ALU.mult).then_inc(h_ready, 1)
            dve.wait_ge(prow_in, 16 * 12)
            V.tensor_copy(prow[LDT:LDT + NST, :].rearrange("j (g p) -> j g p", g=2),
                          ldt2[LDT:LDT + NST, :].unsqueeze(2).to_broadcast([NST, 2, 64])).then_inc(prow_ready, 1)
            dve.wait_ge(pcol_ps, 1)
            V.tensor_copy(pcol[:, :], t_bank[:, 0:P]).then_inc(pcol_ready, 1)
            dve.wait_ge(pcol_ready, 1)
            for b in (0, 2):
                dve.wait_ge(hT_ps, b + 1)
                for k in (2 * b, 2 * b + 1):
                    V.tensor_scalar(hT[:, k, :], bank[b][:, S * (k % 2):S * (k % 2) + S], pcol[:, G1 + k:G1 + k + 1], None,
                                    ALU.mult).then_inc(hT_dve, 1)

            step(V.tensor_scalar(sub_gain, pcol[:, SG:SG + 1], 1.0 - LAMBDA_INIT, None, ALU.mult))

            def exponential(x):
                step(V.tensor_scalar(sm[x], sm[x], -100.0, 88.0, ALU.max, ALU.min))
                step(V.tensor_scalar(sm["k"], sm[x], LOG2E, MAGIC, ALU.mult, ALU.add))
                step(V.tensor_scalar(sm["k"], sm["k"], MAGIC, -127.0, ALU.subtract, ALU.max))
                step(V.scalar_tensor_tensor(sm["r"], sm["k"], -LN2_HI, sm[x], ALU.mult, ALU.add))
                step(V.scalar_tensor_tensor(sm["r"], sm["k"], -LN2_LO, sm["r"], ALU.mult, ALU.add))
                mark(V.tensor_scalar(sm["pw"].bitcast(I32), sm["k"], 127.0, 2.0 ** 23, ALU.add, ALU.mult))
                step(V.tensor_scalar(sm["q"], sm["r"], 1.0 / 8, 1.0, ALU.mult, ALU.add))
                for n in (7, 6, 5, 4, 3, 2):
                    step(mul(sm["q"], sm["q"], sm["r"]))
                    step(V.tensor_scalar(sm["q"], sm["q"], 1.0 / n, 1.0, ALU.mult, ALU.add))
                step(mul(sm["q"], sm["q"], sm["r"]))

            step(V.tensor_copy(sm["ldt"], pcol[:, LDT:LDT + NST]))
            exponential("ldt")
            step(V.scalar_tensor_tensor(sm["dt"], sm["q"], 1.0, sm["pw"], ALU.add, ALU.mult))
            mark(V.tensor_scalar(sm["lr"], pcol[:, LRE:LRE + NST], -1e-4, None, ALU.min))
            mark(V.tensor_copy(sm["li"], pcol[:, LIM:LIM + NST]))
            step(mul(sm["th"], pcol[:, LIM:LIM + NST], sm["dt"]))
            step(V.tensor_scalar(sm["thk"], sm["th"], INV_2PI, MAGIC, ALU.mult, ALU.add))
            step(V.tensor_scalar(sm["thk"], sm["thk"], MAGIC, None, ALU.subtract))
            step(V.scalar_tensor_tensor(sm["thr"], sm["thk"], -TWO_PI_1, sm["th"], ALU.mult, ALU.add))
            step(V.scalar_tensor_tensor(sm["thr"], sm["thk"], -TWO_PI_2, sm["thr"], ALU.mult, ALU.add))
            step(V.scalar_tensor_tensor(sm["thr"], sm["thk"], -TWO_PI_3, sm["thr"], ALU.mult, ALU.add))
            V.tensor_scalar(sm["thr"], sm["thr"], -3.14159, 3.14159, ALU.max, ALU.min).then_inc(sin_in, 1)
            step(mul(sm["a"], sm["lr"], sm["dt"]))
            exponential("a")
            mark(V.scalar_tensor_tensor(sm["mag"], sm["q"], 1.0, sm["pw"], ALU.add, ALU.mult))
            mark(V.tensor_scalar(sm["t2"], sm["pw"], 1.0, None, ALU.subtract))
            step(mul(sm["t1"], sm["q"], sm["pw"]))
            step(V.tensor_tensor(sm["em1"], sm["t1"], sm["t2"], ALU.add))
            dve.wait_ge(sin_ready, 2)
            mark(V.scalar_tensor_tensor(sm["sin"], sm["sh"], 2.0, sm["ch"], ALU.mult, ALU.mult))
            step(V.scalar_tensor_tensor(sm["vers"], sm["sh"], 2.0, sm["sh"], ALU.mult, ALU.mult))
            step(V.tensor_scalar(sm["cos"], sm["vers"], -1.0, 1.0, ALU.mult, ALU.add))
            mark(mul(sm["ai"], sm["mag"], sm["sin"]))
            step(mul(sm["nr"], sm["em1"], sm["cos"]))
            step(V.tensor_tensor(sm["nr"], sm["nr"], sm["vers"], ALU.subtract))
            mark(mul(sm["t1"], sm["lr"], sm["lr"]))
            step(mul(sm["t2"], sm["li"], sm["li"]))
            step(V.tensor_tensor(sm["den"], sm["t1"], sm["t2"], ALU.add))
            step(V.reciprocal(sm["den"], sm["den"]))
            mark(mul(sm["t1"], sm["nr"], sm["lr"]))
            step(mul(sm["t2"], sm["ai"], sm["li"]))
            step(V.tensor_tensor(sm["t1"], sm["t1"], sm["t2"], ALU.add))
            step(mul(sm["cr"], sm["t1"], sm["den"]))
            mark(mul(sm["t1"], sm["ai"], sm["lr"]))
            step(mul(sm["t2"], sm["nr"], sm["li"]))
            step(V.tensor_tensor(sm["t1"], sm["t1"], sm["t2"], ALU.subtract))
            step(mul(sm["ci"], sm["t1"], sm["den"]))
            dve.wait_ge(c_read, 2)
            cre, cim = cT[:, 0, :, :], cT[:, 1, :, :]
            w = [tmp[:, i, :, :].rearrange("p a n -> p (a n)").rearrange("p (j n) -> p j n", j=NST) for i in range(3)]
            cr_w = sm["cr"].unsqueeze(2).to_broadcast([P, NST, 32])
            ci_w = sm["ci"].unsqueeze(2).to_broadcast([P, NST, 32])
            mark(mul(w[0], cre, cr_w))
            mark(mul(w[1], cim, ci_w))
            step(mul(w[2], cre, ci_w))
            V.tensor_tensor(cT[:, 0, :, :], w[0], w[1], ALU.subtract).then_inc(cT_ready, 1)
            dve.wait_ge(cT_ready, 1)
            step(mul(w[0], cim, cr_w))
            V.scalar_tensor_tensor(cT[:, 1, :, :], w[2], -1.0, w[0], ALU.mult, ALU.subtract).then_inc(cT_ready, 1)
            dve.wait_ge(cT_ready, 2)
            powers = {1: ("cos", "sin"), 2: ("ldt", "q"), 4: ("k", "r"), 8: ("a", "em1"), 16: ("nr", "ai"),
                      32: ("sh", "ch"), 64: ("t1", "t2"), 128: ("th", "thk")}
            for n in (1, 2, 4, 8, 16, 32, 64):
                (pr, pi), (qr, qi) = powers[n], powers[2 * n]
                mark(mul(sm["den"], sm[pr], sm[pr]))
                mark(mul(sm["dt"], sm[pi], sm[pi]))
                step(V.scalar_tensor_tensor(sm[qi], sm[pr], 2.0, sm[pi], ALU.mult, ALU.mult))
                step(V.tensor_tensor(sm[qr], sm["den"], sm["dt"], ALU.subtract))
            dve.wait_ge(hT_ps, 4)
            mark(V.memset(turn[:, :, 0, 0:1], 1.0))
            step(V.memset(turn[:, :, 1, 0:1], 0.0))
            for n in (1, 2, 4, 8, 16, 32):
                def wide(name):
                    return sm[name].unsqueeze(2).to_broadcast([P, NST, n])
                pr, pi = powers[n]
                c0, s0 = turn[:, :, 0, 0:n], turn[:, :, 1, 0:n]
                c1, s1 = turn[:, :, 0, n:2 * n], turn[:, :, 1, n:2 * n]
                a, b = turn_t[:, 0, :, 0:n], turn_t[:, 1, :, 0:n]
                mark(mul(a, c0, wide(pr)))
                mark(mul(b, s0, wide(pi)))
                mark(mul(c1, c0, wide(pi)))
                step(mul(s1, s0, wide(pr)))
                step(V.tensor_tensor(s1, s1, c1, ALU.add))
                ins = V.tensor_tensor(c1, a, b, ALU.subtract)
                if n < 32:
                    step(ins)
                else:
                    ins.then_inc(turn_base, 1)
            dve.wait_ge(misc_in, 16 * 6)
            for i in range(2):
                mark(V.tensor_tensor_reduce(out=tmp[:, 0, i, 0:64], in0=lq[:, 2 * i, :], in1=lq[:, 2 * i + 1, :], scale=1.0,
                                            scalar=0.0, op0=ALU.mult, op1=ALU.add, accum_out=lam_sum[:, i:i + 1]))
            sync()

            def state_tile(j):
                if j == 0:
                    dve.wait_ge(turns_ready, 1)
                if j == 8:
                    dve.wait_ge(turns_ready, 2)
                rot = turn[:, j, :, :]
                src = bu_bank.rearrange("p (r n) -> p r n", r=2)
                a, b, v = tmp[:, 0, :, :], tmp[:, 1, :, :], tmp[:, 2, :, :]
                decay = sm["mag"][:, j:j + 1].to_broadcast([P, S])
                dve.wait_ge(bu_ps, j + 1)
                mark(mul(a, rot, src))
                mul(b, rot, src[:, ::-1, :]).then_inc(bu_read, 1)
                dve.wait_ge(bu_read, j + 1)
                sync()
                mark(V.tensor_tensor(v[:, 0, :], a[:, 0, :], a[:, 1, :], ALU.add))
                mark(V.tensor_tensor(v[:, 1, :], b[:, 0, :], b[:, 1, :], ALU.subtract))
                sync()
                for r in range(2):
                    mark(V.tensor_tensor_scan(a[:, r, :], decay, v[:, r, :], 0.0, ALU.mult, ALU.add))
                sync()
                mark(mul(b, rot, a))
                mark(mul(v, rot, a[:, ::-1, :]))
                sync()
                if j >= 2:
                    dve.wait_ge(y_ps, j - 1)
                mark(V.tensor_tensor(x_state[:, j % 2, 0, :], b[:, 0, :], b[:, 1, :], ALU.subtract))
                V.tensor_tensor(x_state[:, j % 2, 1, :], v[:, 0, :], v[:, 1, :], ALU.add).then_inc(xs_ready, 1)
                dve.wait_ge(xs_ready, j + 1)
                sync()

            def ssm_out(ct):
                dve.wait_ge(y_ps, 4 * ct + 4)
                if ct == 0:
                    dve.wait_ge(t_read, 2)
                V.scalar_tensor_tensor(yT[:, ct, :], uT[:, ct, :], pcol[:, DS + ct:DS + ct + 1],
                                       yo_bank[:, S * (ct % 2):S * (ct % 2) + S], ALU.mult, ALU.add).then_inc(y_read, 1)

            def norm_qk(c):
                dve.wait_ge(qk_sq, 2 * c)
                V.tensor_reduce(n_ss, sq.rearrange("p t (g d) -> p (t g) d", d=64), AX.X, ALU.add).then_inc(qk_ss, 1)
                dve.wait_ge(qk_std, c)
                step(V.reciprocal(n_rs, n_std))
                if c >= 2:
                    dve.wait_ge(t_ps, 2 * c)
                for tt in range(TT):
                    mul(qn[:, tt, :].rearrange("p (g d) -> p g d", d=64),
                        chunk_bank(c)[:, tt, :].rearrange("p (g d) -> p g d", d=64),
                        n_rs[:, 8 * tt:8 * tt + 8].unsqueeze(2).to_broadcast([P, 8, 64])).then_inc(qk_n, 1)

            def ssm_slot(p):
                if p in SSM_AT:
                    j = SSM_AT[p]
                    state_tile(j)
                    if j % 4 == 1 and j > 4:
                        ssm_out(j // 4 - 1)

            for p in range(2, 14):
                if p % 2 and 1 <= p // 2 <= 4:
                    norm_qk(p // 2)
                ssm_slot(p)
            V.tensor_scalar(lam_sum, lam_sum, 1.0, None, ALU.mult).then_inc(nmax, 1)
            dve.wait_ge(act_step, 3)
            step(V.tensor_tensor(neg_lam, lam_exp[:, 1:2], lam_exp[:, 0:1], ALU.subtract))
            step(V.tensor_scalar(neg_lam, neg_lam, LAMBDA_INIT, None, ALU.subtract))
            yf = yT.rearrange("p c n -> p (c n)")

            def maxima(h):
                dve.wait_ge(s_ps, h + 1)
                for m in range(2):
                    for qt in range(2):
                        cs = slice(0, 128) if qt == 0 else slice(128, 384)
                        cf = causal[:, :, :].rearrange("p b n -> p (b n)")
                        ins = V.tensor_tensor_reduce(out=masked[:, m, cs], in0=pair[:, m, cs], in1=cf[:, cs], scale=1.0,
                                                     scalar=-3e38, op0=ALU.add, op1=ALU.max,
                                                     accum_out=s_max[:, 2 * m + qt:2 * m + qt + 1])
                        ins.then_inc(s_read, 1)
                dve.wait_ge(s_read, 4 * h + 4)
                V.tensor_scalar(n_bias, s_max, -SCALE, None, ALU.mult).then_inc(nmax, 1)

            maxima(0)
            for h in range(HEADS):
                dve.wait_ge(p_ready, 4 * h + 4)
                step(V.reciprocal(p_rs, p_sum))
                step(V.tensor_scalar(p_c1, p_rs[:, 2:4], neg_lam, None, ALU.mult))
                if h >= 1:
                    dve.wait_ge(aT_ps, h)
                for qt in range(2):
                    cs = slice(0, 128) if qt == 0 else slice(128, 384)
                    mark(V.tensor_scalar(a_mix[:, cs], probs[:, 1, cs], p_c1[:, qt:qt + 1], None, ALU.mult))
                sync()
                for qt in range(2):
                    cs = slice(0, 128) if qt == 0 else slice(128, 384)
                    V.scalar_tensor_tensor(a_mix[:, cs], probs[:, 0, cs], p_rs[:, qt:qt + 1], a_mix[:, cs], ALU.mult,
                                           ALU.add).then_inc(a_ready, 1)
                if h + 1 < HEADS:
                    maxima(h + 1)
                ssm_slot(14 + h)
                if h == HEADS - 2:
                    ssm_out(3)
                    dve.wait_ge(y_read, 4)
                    step(mul(glu_a, yf, yf))
                    step(V.tensor_scalar(glu_a, glu_a, 0.044715, 1.0, ALU.mult, ALU.add))
                    mul(glu_a, glu_a, yf).then_inc(gel_in, 1)
            dve.wait_ge(gel_sig, 1)
            mul(zT[:, :, :].rearrange("p c n -> p (c n)"), yf, glu_g).then_inc(z_ready, 1)
            dve.wait_ge(o_std, 1)
            step(V.reciprocal(o_rs, o_rs))
            for tt in range(TT):
                o3 = o_tok[:, tt, :].rearrange("p (h n) -> p h n", h=HEADS)
                mul(o3, o3, o_rs[:, 8 * tt:8 * tt + 8].unsqueeze(2).to_broadcast([P, HEADS, P])).then_inc(o_norm, 1)
            dve.wait_ge(glu_sig, 4)
            zf = zT[:, :, :].rearrange("p c n -> p (c n)")
            mul(zf, zf, glu_g).then_inc(sout_ready, 1)
            dve.wait_ge(gates_sig, 1)
            for a, first in ((0, P_PSSM), (1, P_PATT)):
                for n in range(2):
                    cols = slice(N * n, N * n + N)
                    dve.wait_ge(piece_used, first + (a + 1) * (n + 1))
                    for tt in range(TT):
                        g = sg[:, a, tt, cols]
                        mul(g, g, bank[2 * n + tt]).then_inc(merged_s, 1)
                    if a == 1:
                        dve.wait_ge(merged_s, 6 + 4 * n)
                        for tt in range(TT):
                            V.tensor_tensor(merged[:, tt, cols], sg[:, 0, tt, cols], sg[:, 1, tt, cols],
                                            ALU.add).then_inc(merged_s, 1)
            for n in range(2):
                dve.wait_ge(piece_used, P_WOUT + 3 + n)
                for tt in range(TT):
                    ps = (pair, bank01)[n][:, tt, :]
                    xs = x_acc[:, tt, N * n:N * n + N]
                    V.tensor_tensor(xs, xs, ps, ALU.add).then_inc(x1_ready, 1)
            dve.wait_ge(x1_sq, 4)
            V.tensor_tensor(x_ss, x1_parts[:, 0:2], x1_parts[:, 2:4], ALU.add).then_inc(x1_ss, 1)
            dve.wait_ge(x1_std, 1)
            step(V.reciprocal(x_rs, x_std))
            logit, ex, gt, eq, cum, pick, misc = [route[:, i, :, :] for i in range(7)]
            rank_m, gate = gt, ex
            dve.wait_ge(logit_ps, 1)
            for tt in range(TT):
                mark(V.scalar_tensor_tensor(logit[:, tt, :], pair[:, tt, 0:E], x_rs[:, tt:tt + 1], misc[:, 0, :], ALU.mult,
                                            ALU.add))
            sync()
            for tt in range(TT):
                mark(V.max(top8[:, tt, :], logit[:, tt, :]))
            sync()
            for tt in range(TT):
                V.tensor_scalar(neg_top[:, tt:tt + 1], top8[:, tt, 0:1], -1.0, None, ALU.mult).then_inc(top_ready, 1)
            for tt in range(TT):
                least = top8[:, tt, 3:4]
                mark(V.tensor_scalar(gt[:, tt, :], logit[:, tt, :], least, 0.0, ALU.is_gt, ALU.add,
                                     accum_out=over[:, tt:tt + 1]))
                mark(V.tensor_scalar(eq[:, tt, :], logit[:, tt, :], least, None, ALU.is_equal))
            sync()
            mark(V.tensor_scalar(need, over, -1.0, 4.0, ALU.mult, ALU.add))
            for tt in range(TT):
                mark(V.tensor_tensor_scan(cum[:, tt, :], ones[:, 0:E], eq[:, tt, :], 0.0, ALU.mult, ALU.add))
            sync()
            for tt in range(TT):
                mark(V.scalar_tensor_tensor(pick[:, tt, :], cum[:, tt, :], need[:, tt:tt + 1], eq[:, tt, :], ALU.is_le, ALU.mult))
            sync()
            V.tensor_tensor(pick, pick, gt, ALU.add).then_inc(picked, 1)
            for tt in range(TT):
                V.tensor_scalar(h2[:, tt, :], x_acc[:, tt, :], x_rs[:, tt:tt + 1], None, ALU.mult).then_inc(h2_ready, 1)
            dve.wait_ge(picked, 1)
            dve.wait_ge(gexp, 2)
            for tt in range(TT):
                mark(V.tensor_tensor_reduce(out=ex[:, tt, :], in0=ex[:, tt, :], in1=pick[:, tt, :], scale=1.0, scalar=0.0,
                                            op0=ALU.mult, op1=ALU.add, accum_out=g_sum[:, tt:tt + 1]))
            sync()
            step(V.reciprocal(g_rs, g_sum))
            for tt in range(TT):
                V.tensor_scalar(gate[:, tt, :], ex[:, tt, :], g_rs[:, tt:tt + 1], None, ALU.mult).then_inc(gates_ready, 1)
            dve.wait_ge(gates_ready, 2)
            dve.wait_ge(rank_ps, 1)
            step(V.scalar_tensor_tensor(rank_m, y_bank[:, 0:2 * E].rearrange("p (t e) -> p t e", t=TT), 1.0, pick, ALU.add,
                                        ALU.mult))
            mark(V.tensor_scalar(rank_m, rank_m, 1.0, None, ALU.subtract))
            counts = cum[:, 0, :]
            V.tensor_copy(counts, y_bank[:, 2 * E:3 * E]).then_inc(picked, 1)
            dve.wait_ge(picked, 2)
            sync()

            def slot_columns(es, bases):
                for x in range(2):
                    for tt in range(TT):
                        yield (tt, slice(SLOT * x, SLOT * x + SLOT), iota[:, bass.ds(bases[x], SLOT)],
                               rank_m[:, tt, bass.ds(es[x], 1)], gate[:, tt, bass.ds(es[x], 1)])

            def select(i, es, bases):
                if not is_first(i):
                    dve.wait_ge(xg_ps, i)
                for tt, cols, at, rank, _ in slot_columns(es, bases):
                    V.tensor_scalar(sel[:, tt, cols], at, rank, None, ALU.is_equal).then_inc(sel_ready, 1)

            def take_x(i):
                dve.wait_ge(xg_ps, i + 1)
                for b in range(2):
                    mul(xT[:, 4 * b:4 * b + 4, :], ps_xg[b][:, :].rearrange("p (k n) -> p k n", k=4),
                        pcol[:, G2 + 4 * b:G2 + 4 * b + 4].unsqueeze(2).to_broadcast([P, 4, P])).then_inc(xT_ready, 1)

            def add_block(i, tt):
                dve.wait_ge(comb_ps, 2 * i + tt + 3)
                for c in range(1 if tt == 0 else 2):
                    if tt == 0:
                        acc, ps = x_acc[:, tt, :].rearrange("p (b n) -> p b n", b=2), pair[:, :, :]
                    else:
                        acc, ps = x_acc[:, tt, N * c:N * c + N], ps_xg[c][:, :]
                    ins = V.tensor_tensor(acc, acc, ps, ALU.add)
                    if tt == 0 or c == 1:
                        ins.then_inc(added, 1)
                    else:
                        ins.then_inc(added_half, 1)
                if tt == 1:
                    dve.wait_ge(added_half, i + 2)

            def block_work(i, es, bases, first, last):
                if not last:
                    select(i + 1, (2 * i + 2, 2 * i + 3), (0, 0))
                if not is_first(i):
                    dve.wait_ge(put_ps, i)
                for tt, cols, at, rank, g in slot_columns(es, bases):
                    V.tensor_scalar(sel_g[:, tt, cols], at, rank, g, ALU.is_equal, ALU.mult).then_inc(selg_ready, 1)
                for b in range(2):
                    if b == 0:
                        dve.wait_ge(hid_ps, i + 1)
                    else:
                        dve.wait_ge(w1_used, (i + 1) * W1P)
                    hid = (bank01, bank23)[b][:, :, :].rearrange("p b (n w) -> p b n w", w=2)
                    ga, ua = (v[:, N * b:N * b + N].rearrange("p (b n) -> p b n", b=2) for v in (g_act, u_act))
                    V.tensor_scalar(ga, hid[:, :, :, 0], 7.0, None, ALU.min).then_inc(g_ready, 1)
                    V.tensor_scalar(ua, hid[:, :, :, 1], 7.0, -7.0, ALU.min, ALU.max).then_inc(hid_read, 1)
                for b in range(2):
                    cols = slice(N * b, N * b + N)
                    dve.wait_ge(g_ready, 2 * i + b + 1)
                    dve.wait_ge(hid_read, 2 * i + b + 1)
                    V.scalar_tensor_tensor(u_act[:, cols], u_act[:, cols], 1.0, g_act[:, cols], ALU.add,
                                           ALU.mult).then_inc(um_ready, 1)
                for b in range(2):
                    cols = slice(N * b, N * b + N)
                    dve.wait_ge(um_ready, 2 * i + b + 1)
                    dve.wait_ge(sig_ready, 2 * i + b + 1)
                    mul(u_act[:, cols], u_act[:, cols], s_act[:, cols]).then_inc(act_ready, 1)
                if not last:
                    take_x(i + 1)
                if not first:
                    add_block(i - 1, 0)
                    add_block(i - 1, 1)

            select(0, (0, 1), (0, 0))
            take_x(0)
            block_work(0, (0, 1), (0, 0), False, False)
            for c in range(3):
                mark(V.tensor_scalar(flag[:, E * c:E * c + E], counts[0:1, :], float(SLOT * (c + 1)), None, ALU.is_gt))
                mark(V.memset(flag_b[:, E * c:E * c + E], float(SLOT * (c + 1) - NO_SLOT)))
            sync()
            step(V.tensor_tensor_scan(flag_pos, ones[0:1, 0:96], flag, 0.0, ALU.mult, ALU.add))
            step(V.tensor_scalar(table_f[:, 0:1], flag_pos[:, 95:96], 0.5, 0.25, ALU.mult, ALU.add))
            step(V.tensor_scalar(table_f[:, 0:1], table_f[:, 0:1], MAGIC, None, ALU.add))
            mark(V.tensor_scalar(table_f[:, 0:1], table_f[:, 0:1], MAGIC, None, ALU.subtract))
            mark(V.tensor_copy(table_f[:, 1:2], flag_pos[:, 95:96]))
            mark(mul(flag_e.rearrange("p (c e) -> p c e", c=3), flag.rearrange("p (c e) -> p c e", c=3),
                     iota[0:1, 0:E].unsqueeze(1).to_broadcast([1, 3, E])))
            mark(mul(flag_b, flag_b, flag))
            sync()
            step(V.tensor_tensor(flag_pos, flag_pos, flag, ALU.subtract))
            for w_, at in ((flag_e, 2), (flag_b, 2 + MAX_EXTRA)):
                step(V.tensor_tensor(big, flag_pos.unsqueeze(1).to_broadcast([1, MAX_EXTRA, 96]),
                                     iota[0:1, 0:MAX_EXTRA].unsqueeze(2).to_broadcast([1, MAX_EXTRA, 96]), ALU.is_equal))
                step(mul(big, big, w_.unsqueeze(1).to_broadcast([1, MAX_EXTRA, 96])))
                step(V.tensor_reduce(table_f[:, at:at + MAX_EXTRA], big, AX.X, ALU.add))
            at = 2 + MAX_EXTRA
            step(V.tensor_scalar(table_f[:, at:at + MAX_EXTRA], table_f[:, at:at + MAX_EXTRA], float(NO_SLOT), None, ALU.add))
            V.tensor_copy(table[:, :], table_f).then_inc(table_ready, 1)

            with dve.Fori(1, NB - 1) as i:
                block_work(i, (2 * i, 2 * i + 1), (0, 0), False, False)
            block_work(NB - 1, (E - 2, E - 1), (0, 0), False, True)
            add_block(NB - 1, 0)
            add_block(NB - 1, 1)
            dve.wait_ge(table_ready, 1)
            extra = dve.value_load(table[0:1, 0:1], min_val=0, max_val=MAX_EXTRA // 2)
            with dve.If(extra > 0):
                with dve.Fori(0, extra) as j:
                    es = [dve.value_load(table[0:1, bass.ds(2 * j + 2 + x, 1)], min_val=0, max_val=E - 1) for x in range(2)]
                    bases = [dve.value_load(table[0:1, bass.ds(2 * j + 2 + MAX_EXTRA + x, 1)], min_val=0, max_val=NO_SLOT)
                             for x in range(2)]
                    i = j + NB
                    select(i, es, bases)
                    take_x(i)
                    block_work(i, es, bases, True, True)
                    add_block(i, 0)
                    add_block(i, 1)

        @block.tensor
        def _(pe):
            T = nc.tensor
            pe.wait_ge(consts, 1)
            pe.wait_ge(h_ready, 2)
            for b in range(4):
                for k in (2 * b, 2 * b + 1):
                    for tt in range(TT):
                        ins = T.transpose(bank[b][:, S * (k % 2) + P * tt:S * (k % 2) + P * tt + P],
                                          h_tok[:, tt, P * k:P * k + P], ident[:, :])
                ins.then_inc(hT_ps, 1)
                if b == 1:
                    pe.wait_ge(prow_ready, 1)
                    T.transpose(t_bank[:, 0:P], prow[:, :], ident[:, :]).then_inc(pcol_ps, 1)

            def ssm_matrices():
                pe.wait_ge(bc_in, 16 * 20)
                for r in range(2):
                    for ct in range(CT):
                        ins = T.transpose(bank23[:, r, P * ct:P * ct + P],
                                          b_raw[:, r, 4 * ct:4 * ct + 4, :].rearrange("p j c -> p (j c)"), ident[:, :])
                    ins.then_inc(b_ps, 1)
                pe.wait_ge(pcol_ready, 1)
                for r, ps in enumerate((t_bank, y_bank)):
                    for ct in range(CT):
                        ins = T.transpose(ps[:, P * ct:P * ct + P], c_raw[:, r, ct, :], ident[:, :])
                    ins.then_inc(c_ps, 1)

            def piece(i):
                pe.wait_ge(piece_in[i % 4], 16 * (i // 4 + 1))
                return ring[:, STREAM + i % 4, :].rearrange("p (k n) -> p k n", k=4)

            def products(i, lhs, k0, outs, start, stop):
                w_ = piece(i)
                for tt in range(TT):
                    for k in range(4):
                        ins = T.matmul(outs[tt], lhs[:, k0 + k, P * tt:P * tt + P], w_[:, k, :], start=start and k == 0,
                                       stop=stop and k == 3)
                ins.then_inc(piece_used, 1)

            def in_piece(i):
                c = i // 2
                if i % 2 == 0:
                    if c == 2:
                        pe.wait_ge(chunk_read, 2)
                    elif c in (3, 4, 5, 6):
                        pe.wait_ge(qk_n, 2 * (c - 2))
                    elif c > 6:
                        pe.wait_ge(chunk_read, 2 * (c - 4))
                ps = chunk_bank(c)
                products(i, hT, 4 * (i % 2), [ps[:, 0, :], ps[:, 1, :]], i % 2 == 0, i % 2 == 1)

            def transposes(c):
                pe.wait_ge(qk_n, 2 * c)
                for r in range(2):
                    pe.wait_ge(t_read, 2 * c + r - 1)
                    for hh in range(2):
                        for tt in range(TT):
                            ins = T.transpose((t_bank, y_bank)[r][:, S * hh + P * tt:S * hh + P * tt + P],
                                              qn[:, tt, P * (2 * r + hh):P * (2 * r + hh) + P], ident[:, :])
                    ins.then_inc(t_ps, 1)

            def inputs(j):
                ct, jj = j // 4, j % 4
                if j >= 1:
                    pe.wait_ge(bu_read, j)
                else:
                    pe.wait_ge(t_read, 2)
                    pe.wait_ge(bT_ready, 2)
                for r in range(2):
                    ins = T.matmul(bu_bank[:, S * r:S * r + S], bT[32 * jj:32 * jj + 32, ct, r, :],
                                   uT[32 * jj:32 * jj + 32, ct, :], start=True, stop=True, tile_position=(32 * jj, 0))
                ins.then_inc(bu_ps, 1)

            def outputs(j):
                ct, jj = j // 4, j % 4
                pe.wait_ge(xs_ready, j + 1)
                if j == 0:
                    pe.wait_ge(cT_ready, 2)
                if jj == 0 and ct >= 1:
                    pe.wait_ge(y_read, ct)
                for r in range(2):
                    ins = T.matmul(yo_bank[32 * jj:32 * jj + 32, S * (ct % 2):S * (ct % 2) + S], cT[:, r, j, :],
                                   x_state[:, j % 2, r, :], start=(r == 0), stop=(r == 1), tile_position=(0, 32 * jj))
                ins.then_inc(y_ps, 1)

            def ssm_slot(p):
                if p in SSM_AT:
                    j = SSM_AT[p]
                    inputs(j)
                    if j >= 2:
                        outputs(j - 2)

            for p in range(14):
                if p < 2:
                    pe.wait_ge(hT_dve, 2 * p + 2)
                    pe.wait_ge(hT_act, 2 * p + 2)
                in_piece(p)
                if p == 1:
                    ssm_matrices()
                if p == 2:
                    pe.wait_ge(chunk_read, 2)
                    pe.wait_ge(c_read, 2)
                    for ps, c0 in ((t_bank, 0), (y_bank, 2)):
                        for ct in (c0, c0 + 1):
                            for tt in range(TT):
                                ins = T.transpose(ps[:, S * (ct - c0) + P * tt:S * (ct - c0) + P * tt + P],
                                                  u_tok[:, tt, P * ct:P * ct + P], ident[:, :])
                        ins.then_inc(t_ps, 1)
                if p % 2 == 0 and 2 <= p // 2 <= 5:
                    transposes(p // 2 - 1)
                ssm_slot(p)

            def scores(h):
                if h == 0:
                    pe.wait_ge(t_read, 10)
                    pe.wait_ge(chunk_read, 4)
                else:
                    pe.wait_ge(s_read, 4 * h)
                for qt in range(2):
                    for m in range(2):
                        a = slice(64 * m, 64 * m + 64)
                        ins = T.matmul(pair[:, m, 128 * qt:128 * qt + 128 * (qt + 1)], qT[a, h, P * qt:P * qt + P],
                                       kT[a, h, 0:P * (qt + 1)], start=(qt == 0), stop=True, tile_position=(64 * m, 0),
                                       skip_group_check=True)
                ins.then_inc(s_ps, 1)

            def mix(h):
                pe.wait_ge(a_ready, 2 * h + 2)
                if h >= 1:
                    pe.wait_ge(aT_ready, h)
                for b in range(3):
                    ins = T.transpose(t_bank[:, P * b:P * b + P], a_mix[:, P * b:P * b + P], ident[:, :])
                ins.then_inc(aT_ps, 1)

            def values(h):
                pe.wait_ge(aT_ready, h + 1)
                if h == 0:
                    pe.wait_ge(chunk_read, 6)
                else:
                    pe.wait_ge(o_read, 4 * h)
                hs = slice(P * h, P * h + P)
                T.matmul(y_bank[:, 0:P], aT[:, 0, :], v_tok[:, 0, hs], start=True, stop=True)
                T.matmul(y_bank[:, P:2 * P], aT[:, 1, :], v_tok[:, 0, hs], start=True, stop=False)
                T.matmul(y_bank[:, P:2 * P], aT[:, 2, :], v_tok[:, 1, hs], start=False, stop=True).then_inc(o_ps, 1)

            scores(0)
            for h in range(HEADS):
                in_piece(14 + h)
                mix(h)
                if h + 1 < HEADS:
                    scores(h + 1)
                values(h)
                ssm_slot(14 + h)
                if h == HEADS - 2:
                    outputs(NST - 2)
                    outputs(NST - 1)
            pe.wait_ge(z_ready, 1)
            w_ = piece(P_GLU)
            for co in range(CT):
                for k in range(CT):
                    ins = T.matmul(pair[:, co // 2, S * (co % 2):S * (co % 2) + S], w_[:, k, P * co:P * co + P], zT[:, k, :],
                                   start=(k == 0), stop=(k == 3))
                if co == 1:
                    ins.then_inc(glu_ps, 1)
            ins.then_inc(piece_used, 1)
            pe.wait_ge(o_norm, 2)
            pe.wait_ge(y_read, 4)
            pe.wait_ge(chunk_read, 14)
            for b in range(4):
                for h in (2 * b, 2 * b + 1):
                    for tt in range(TT):
                        ins = T.transpose(bank[b][:, S * (h % 2) + P * tt:S * (h % 2) + P * tt + P],
                                          o_tok[:, tt, P * h:P * h + P], ident[:, :])
                ins.then_inc(oT_ps, 1)
            pe.wait_ge(sout_ready, 1)
            pe.wait_ge(oT_ready, 4)
            for n in range(2):
                products(P_PSSM + n, zT, 0, bank[2 * n:2 * n + 2], True, True)
            def turn_merged(half):
                pe.wait_ge(merged_s, 4 * half + 8)
                for b in (2 * half, 2 * half + 1):
                    for k in (2 * b, 2 * b + 1):
                        for tt in range(TT):
                            ins = T.transpose(bank[b][:, S * (k % 2) + P * tt:S * (k % 2) + P * tt + P],
                                              merged[:, tt, P * k:P * k + P], ident[:, :])
                    ins.then_inc(mT_ps, 1)

            for n in range(2):
                pe.wait_ge(merged_s, 2 * n + 2)
                for kh in range(2):
                    products(P_PATT + 2 * n + kh, oT, 4 * kh, bank[2 * n:2 * n + 2], kh == 0, kh == 1)
                    if (n, kh) == (1, 0):
                        turn_merged(0)
            for kh in range(2):
                pe.wait_ge(mT_ready, 2 * kh + 2)
                for n in range(2):
                    products(P_WOUT + 2 * kh + n, hT, 4 * kh, [(pair, bank01)[n][:, tt, :] for tt in range(TT)], kh == 0,
                             kh == 1)
                    if (kh, n) == (0, 0):
                        turn_merged(1)

            def turn_x1(half):
                pe.wait_ge(x1_ready, 2 * half + 2)
                for b in range(2):
                    for kk in range(2):
                        k = 4 * half + 2 * b + kk
                        for tt in range(TT):
                            ps = bank23[:, b, :] if half == 0 else (t_bank, y_bank)[b]
                            ins = T.transpose(ps[:, S * kk + P * tt:S * kk + P * tt + P], x_acc[:, tt, P * k:P * k + P],
                                              ident[:, :])
                    ins.then_inc(h2T_ps, 1)

            def router(half):
                pe.wait_ge(h2T_ready, 4 * half + 4)
                for tt in range(TT):
                    for k in range(4 * half, 4 * half + 4):
                        ins = T.matmul(pair[:, tt, 0:E], hT[:, k, P * tt:P * tt + P], w_r[:, k, :], start=(k == 0),
                                       stop=(k == KT - 1))
                return ins

            turn_x1(0)
            turn_x1(1)
            router(0)
            router(1).then_inc(logit_ps, 1)
            pe.wait_ge(picked, 1)
            pick = route[:, 5, :, :]
            T.matmul(y_bank[:, 0:E], before[:, :], pick[:, 0, :], start=True, stop=True)
            T.matmul(y_bank[:, E:2 * E], ones[:, :], pick[:, 0, :], start=True, stop=False)
            T.matmul(y_bank[:, E:2 * E], before[:, :], pick[:, 1, :], start=False, stop=True)
            T.matmul(y_bank[:, 2 * E:3 * E], ones[:, :], pick[:, 0, :], start=True, stop=False)
            T.matmul(y_bank[:, 2 * E:3 * E], ones[:, :], pick[:, 1, :], start=False, stop=True).then_inc(rank_ps, 1)
            pe.wait_ge(gates_ready, 2)
            for tt in range(TT):
                ins = T.transpose(pair[0:E, 0, P * tt:P * tt + P], route[:, 1, tt, :], ident[:, :])
            ins.then_inc(gT_ps, 1)

            def gather(i):
                pe.wait_ge(sel_ready, 4 * i + 4)
                for b in range(2):
                    for k in range(4):
                        for tt in range(TT):
                            ins = T.matmul(ps_xg[b][:, P * k:P * k + P], h2[:, tt, P * (4 * b + k):P * (4 * b + k) + P],
                                           sel[:, tt, :], start=(tt == 0), stop=(tt == 1))
                ins.then_inc(xg_ps, 1)

            def combine(i, tt):
                bias = isinstance(i, int) and i < 0
                if tt == 0 and bias:
                    pe.wait_ge(gT_ready, 1)
                    pe.wait_ge(b2_in, 16)
                elif tt == 0:
                    pe.wait_ge(y_ready, i + 1)
                    pe.wait_ge(put_ready, i + 1)
                for c in range(2):
                    ps = pair[:, c, :] if tt == 0 else ps_xg[c][:, :]
                    if bias:
                        ins = T.matmul(ps, gateT[:, P * tt:P * tt + P], b2_sb[:, N * c:N * c + N], start=True, stop=True)
                    else:
                        ins = T.matmul(ps, put[:, P * tt:P * tt + P], y_sb[:, N * c:N * c + N], start=True, stop=True)
                ins.then_inc(comb_ps, 1)

            pe.wait_ge(h2_ready, 2)
            gather(0)

            def block_work(i, odd, first, last):
                later = not is_first(i)
                pe.wait_ge(xT_ready, 2 * i + 2)
                if later:
                    pe.wait_ge(hid_read, 2 * i)
                    pe.wait_ge(actT_ready, 2 * i)
                    pe.wait_ge(put_ready, i)
                hid = [bank01[:, 0, :], bank01[:, 1, :], bank23[:, 0, :], bank23[:, 1, :]]
                halves = [slice(0, SLOT), slice(SLOT, 2 * SLOT)]
                pe.wait_ge(b1_in, (i + 1) * 32)
                for n in range(4):
                    for x, h in enumerate(halves):
                        row = slice(32 * x, 32 * x + 1)
                        T.matmul(hid[n][h, :], ones[row, 0:SLOT], b1_rows[row, N * n:N * n + N], start=True, stop=False,
                                 tile_position=(32 * x, SLOT * x))
                for k in range(W1P):
                    pe.wait_ge(w1_in[k], (i + 1) * 32)
                    for n in range(4):
                        for x, h in enumerate(halves):
                            ins = T.matmul(hid[n][h, :], xT[:, k, h], ring[:, w1_slot(odd, k, x), N * n:N * n + N],
                                           start=False, stop=(k == W1P - 1))
                        if k == W1P - 1 and n == 1:
                            ins.then_inc(hid_ps, 1)
                    ins.then_inc(w1_used, 1)
                if not last:
                    if later:
                        pe.wait_ge(added, 2 * i)
                    gather(i + 1)
                if not first:
                    combine(i - 1, 0)
                for b in range(2):
                    pe.wait_ge(act_ready, 2 * i + b + 1)
                    if b == 0:
                        pe.wait_ge(hid_read, 2 * i + 2)
                    for f in range(4):
                        cols = slice(N * b + P * f, N * b + P * f + P)
                        ins = T.transpose(ps_act[:, b, P * f:P * f + P], u_act[:, cols], ident[:, :])
                    ins.then_inc(actT_ps, 1)
                pe.wait_ge(selg_ready, 4 * i + 4)
                for tt in range(TT):
                    ins = T.transpose(ps_put[:, P * tt:P * tt + P], sel_g[:, tt, :], ident[:, :])
                ins.then_inc(put_ps, 1)
                if not first:
                    if last:
                        pe.wait_ge(added, 2 * i)
                    else:
                        pe.wait_ge(xT_ready, 2 * i + 4)
                    combine(i - 1, 1)
                pe.wait_ge(added, 2 * i + 1)
                for m in range(W2P):
                    if m % 2 == 0:
                        pe.wait_ge(actT_ready, 2 * i + m // 2 + 1)
                    pe.wait_ge(w2_in[m], (i + 1) * 32)
                    for f in (2 * m, 2 * m + 1):
                        for c in range(2):
                            for x, h in enumerate(halves):
                                ins = T.matmul(ps_y[h, c, :], actT[:, f, h], ring_w2(m, x, odd)[:, f % 2, N * c:N * c + N],
                                               start=(f == 0), stop=(f == KT - 1))
                    ins.then_inc(w2_used, 1)

            block_work(0, 0, False, False)
            with pe.Fori(1, NB - 1, 2) as i:
                block_work(i, 1, False, False)
                block_work(i + 1, 0, False, False)
            block_work(NB - 1, 1, False, True)
            combine(NB - 1, 0)
            pe.wait_ge(added, 2 * NB)
            combine(NB - 1, 1)
            pe.wait_ge(table_ready, 1)
            extra = pe.value_load(table[0:1, 0:1], min_val=0, max_val=MAX_EXTRA // 2)
            with pe.If(extra > 0):
                with pe.Fori(0, extra) as j:
                    i = j + NB
                    pe.wait_ge(added, 2 * i + 2)
                    gather(i)
                    block_work(i, 0, True, True)
                    combine(i, 0)
                    combine(i, 1)


_INS = ["x", "norm1_gain", "w_in", "lambda_re", "lambda_im", "log_dt", "ssm_b_re", "ssm_b_im", "ssm_c_re", "ssm_c_im",
        "ssm_d", "w_glu", "b_glu", "q_norm_gain", "k_norm_gain", "lambda_q1", "lambda_k1", "lambda_q2", "lambda_k2",
        "subln_gain", "w_proj_ssm", "w_proj_attn", "w_out", "norm2_gain", "w_router", "b_router", "w_exp1", "b_exp1",
        "w_exp2", "b_exp2"]


def kernel(**inputs):
    import numpy as _np
    import concourse.bacc as _bacc
    from concourse import mybir as _mybir
    from concourse.bass_utils import run_bass_kernel_spmd as _run

    nc = _bacc.Bacc("TRN2", target_bir_lowering=False, num_devices=1)
    arrays, tensors = {}, {}
    for name in _INS:
        a = _np.ascontiguousarray(inputs[name])
        arrays[f"in_{name}"] = a
        tensors[name] = nc.dram_tensor(f"in_{name}", a.shape, _mybir.dt.from_np(a.dtype), kind="ExternalInput").ap()
    out = nc.dram_tensor("out", (1, S, D), _mybir.dt.from_np(_np.dtype("float32")), kind="ExternalOutput").ap()
    hybrid_block(nc, tensors, out)
    r = _run(nc, [arrays], core_ids=[0])
    return r.results[0]["out"]
```

```python
import math
from contextlib import ExitStack

import concourse.bass as bass
from concourse import mybir

ALU = mybir.AluOpType
ACT = mybir.ActivationFunctionType
AX = mybir.AxisListType
F32 = mybir.dt.float32
I32 = mybir.dt.int32

P = 128
D = 1024
S = 256
TT = S // P
KT = D // P
SW = 512
CT = SW // P
NST = 16
HEADS = 8
E = 32
SLOT = 64
NB = E // 2
N = 512
EPS = 1e-5
LAMBDA_INIT = 0.8 - 0.6 * math.exp(-0.3 * 0)
SCALE = 0.125
MASKED = -1e30
MAGIC = 1.5 * 2.0 ** 23
LOG2E = 1.4426950408889634
LN2_HI, LN2_LO = 0.693359375, -2.12194440e-4
INV_2PI = 0.15915494309189535
TWO_PI_1 = 6.28125
TWO_PI_2 = 0.0019350051879882812
TWO_PI_3 = 2 * math.pi - TWO_PI_1 - TWO_PI_2
NO_SLOT = 4 * SLOT
MAX_EXTRA = 16
W1P, W2P = 8, 4
RING = 16
STREAM = 12

LRE, LIM, LDT, G1, BG, DS, SG, QG, KG, G2 = 0, 32, 64, 96, 104, 108, 112, 113, 114, 115

P_GLU, P_BRANCH, P_WOUT, N_PIECES = 22, 23, 29, 33
BRANCH = [(1, 0, 0), (1, 0, 1), (0, 0, 0), (1, 1, 0), (1, 1, 1), (0, 1, 0)]
SSM_AT = {4 + j: j for j in range(NST)}


def hybrid_block(nc, t, out):
    x_d, w_in_d = t["x"], t["w_in"]
    ctx = ExitStack()
    with ctx:
        def sb(name, shape, dt=F32):
            return ctx.enter_context(nc.sbuf_tensor(name, shape, dt))

        def sem(name):
            return ctx.enter_context(nc.semaphore(name))

        bank01 = ctx.enter_context(nc.psum_tensor("bank01", [P, 2, N], F32))
        bank23 = ctx.enter_context(nc.psum_tensor("bank23", [P, 2, N], F32))
        bank = [bank01[:, 0, :], bank01[:, 1, :], bank23[:, 0, :], bank23[:, 1, :]]
        t_bank = ctx.enter_context(nc.psum_tensor("t_bank", [P, N], F32))
        y_bank = ctx.enter_context(nc.psum_tensor("y_bank", [P, N], F32))
        pair = ctx.enter_context(nc.psum_tensor("pair", [P, 2, N], F32))

        ring = sb("ring", [P, RING, 2048])
        x_acc = sb("x_acc", [P, TT, D])
        hT = sb("hT", [P, KT, S])
        uu = sb("uu", [P, 2048])
        qs = sb("qs", [P, 2048])
        zT = sb("zT", [P, CT, S])
        sg = sb("sg", [P, 2, TT, D])
        tmp = sb("tmp", [P, 3, 2, S])
        ident = sb("ident", [P, P])
        ones = sb("ones", [P, P])
        before = sb("before", [P, P])
        causal = sb("causal", [P, 3, P])
        iota = sb("iota", [P, 5 * SLOT])
        prow = sb("prow", [P, P])
        pcol = sb("pcol", [P, P])
        mats = sb("mats", [P, 2048])
        lq = sb("lq", [P, 4, 64])
        w_r = sb("w_r", [P, KT, E])
        small = sb("small", [P, 26, NST])
        stat = sb("stat", [P, 160])
        ldt2 = sb("ldt2", [P, 2])
        route = sb("route", [P, 7, TT, E])
        gateT = sb("gateT", [E, S])
        table = sb("table", [1, 2 + 2 * MAX_EXTRA], I32)

        v_tok = ring[:, 2, :].rearrange("p (t n) -> p t n", t=TT)
        o_tok = ring[:, 3, :].rearrange("p (t n) -> p t n", t=TT)
        att = ring[:, 4:6, :].rearrange("p a n -> p (a n)")
        masked = att[:, 0:768].rearrange("p (m n) -> p m n", m=2)
        probs = att[:, 768:1536].rearrange("p (m n) -> p m n", m=2)
        a_mix = att[:, 1536:1920]
        aT = att[:, 1920:2304].rearrange("p (b n) -> p b n", b=3)
        o_sq = att[:, 2304:2560].rearrange("p (t n) -> p t n", t=TT)
        b_raw = att[:, 0:1024].rearrange("p (r j c) -> p r j c", r=2, j=NST)
        c_raw = att[:, 1024:2048].rearrange("p (r c n) -> p r c n", r=2, c=CT)
        glu_a = att[:, 3072:4096]
        glu_g = mats[:, 0:1024]
        bT = mats[:, 0:1024].rearrange("p (c r n) -> p c r n", c=CT, r=2)
        cT = mats[:, 1024:2048].rearrange("p (r j n) -> p r j n", r=2, j=NST)
        x_state = att[:, 3072:4096].rearrange("p (b r n) -> p b r n", b=2, r=2)
        qT = ring[:, 6, :].rearrange("p (h n) -> p h n", h=HEADS)
        kT = ring[:, 7, :].rearrange("p (h n) -> p h n", h=HEADS)
        turn = ring[:, 8:12, :].rearrange("p a n -> p (a n)").rearrange("p (j r n) -> p j r n", j=NST, r=2)
        u_tok = uu[:, 0:1024].rearrange("p (t n) -> p t n", t=TT)
        yT = uu[:, 0:1024].rearrange("p (c n) -> p c n", c=CT)
        uT = uu[:, 1024:2048].rearrange("p (c n) -> p c n", c=CT)
        merged = uu[:, :].rearrange("p (t n) -> p t n", t=TT)
        qn = qs[:, 0:1024].rearrange("p (t n) -> p t n", t=TT)
        sq = qs[:, 1024:2048].rearrange("p (t n) -> p t n", t=TT)
        oT = qs[:, :].rearrange("p (h n) -> p h n", h=HEADS)
        h2 = qs[:, :].rearrange("p (t n) -> p t n", t=TT)
        sgf = sg[:, :, :, :].rearrange("p a t n -> p (a t n)")
        h_tok = sgf[:, 0:2048].rearrange("p (t n) -> p t n", t=TT)
        sq_x = sgf[:, 2048:4096].rearrange("p (t n) -> p t n", t=TT)
        turn_t = sgf[:, 0:4096].rearrange("p (a j n) -> p a j n", a=2, j=NST)
        lam_prod = qs[:, 0:128].rearrange("p (i n) -> p i n", i=2)
        xT = zT[:, :, :].rearrange("p c n -> p (c n)").rearrange("p (k n) -> p k n", k=KT)
        g_act = uu[:, 0:1024]
        u_act = uu[:, 1024:2048]
        s_act = sgf[:, 0:1024]
        actT = sgf[:, 1024:2048].rearrange("p (f n) -> p f n", f=KT)
        y_sb = sgf[:, 2048:3072]
        sel = sgf[:, 3072:3328].rearrange("p (t n) -> p t n", t=TT)
        sel_g = sgf[:, 3328:3584].rearrange("p (t n) -> p t n", t=TT)
        put = sgf[:, 3584:3840]
        b2_sb = tmp[0:E, 0:2, :, :].rearrange("p a b n -> p (a b n)")
        b1_rows = mats
        big = tmp[0:1, :, :, :].rearrange("p a b n -> p (a b n)").rearrange("p (a b) -> p a b", a=MAX_EXTRA)
        smf = small[0:1, :, :].rearrange("p a n -> p (a n)")
        flag, flag_e, flag_b, flag_pos = (smf[:, 96 * i:96 * i + 96] for i in range(4))
        table_f = lq[0:1, 0, 0:2 + 2 * MAX_EXTRA]

        x_in = sem("x_in")
        prow_in = sem("prow_in")
        bc_in = sem("bc_in")
        c_im_in = sem("c_im_in")
        misc_in = sem("misc_in")
        b2_in = sem("b2_in")
        piece_in = [sem(f"piece_in{i}") for i in range(4)]
        w1_in = [sem(f"w1_in{i}") for i in range(W1P)]
        w2_in = [sem(f"w2_in{i}") for i in range(W2P)]
        b1_in = sem("b1_in")
        out_in = sem("out_in")
        zeroed = sem("zeroed")
        consts = sem("consts")
        pool_step = sem("pool_step")
        turns_ready = sem("turns_ready")
        coef_ready = sem("coef_ready")
        dve_step = sem("dve_step")
        act_step = sem("act_step")
        prow_ready = sem("prow_ready")
        x_sq = sem("x_sq")
        h_ready = sem("h_ready")
        pcol_ps = sem("pcol_ps")
        pcol_ready = sem("pcol_ready")
        hT_ps = sem("hT_ps")
        hT_dve = sem("hT_dve")
        hT_act = sem("hT_act")
        b_ps = sem("b_ps")
        c_ps = sem("c_ps")
        c_read = sem("c_read")
        bT_ready = sem("bT_ready")
        cT_ready = sem("cT_ready")
        sin_in = sem("sin_in")
        sin_ready = sem("sin_ready")
        turn_base = sem("turn_base")
        piece_used = sem("piece_used")
        chunk_read = sem("chunk_read")
        qk_sq = sem("qk_sq")
        qk_ss = sem("qk_ss")
        qk_std = sem("qk_std")
        qk_n = sem("qk_n")
        t_ps = sem("t_ps")
        t_read = sem("t_read")
        bu_ps = sem("bu_ps")
        bu_read = sem("bu_read")
        xs_ready = sem("xs_ready")
        y_ps = sem("y_ps")
        y_read = sem("y_read")
        s_ps = sem("s_ps")
        s_read = sem("s_read")
        nmax = sem("nmax")
        p_ready = sem("p_ready")
        a_ready = sem("a_ready")
        aT_ps = sem("aT_ps")
        aT_ready = sem("aT_ready")
        o_ps = sem("o_ps")
        o_read = sem("o_read")
        o_std = sem("o_std")
        o_norm = sem("o_norm")
        oT_ps = sem("oT_ps")
        oT_ready = sem("oT_ready")
        gel_in = sem("gel_in")
        gel_sig = sem("gel_sig")
        z_ready = sem("z_ready")
        glu_ps = sem("glu_ps")
        glu_sig = sem("glu_sig")
        sout_ready = sem("sout_ready")
        gates_sig = sem("gates_sig")
        merged_s = sem("merged_s")
        mT_ps = sem("mT_ps")
        mT_ready = sem("mT_ready")
        x1_ready = sem("x1_ready")
        x1_std = sem("x1_std")
        x1_sq = sem("x1_sq")
        x1_first = sem("x1_first")
        x1_ss = sem("x1_ss")
        h2_ready = sem("h2_ready")
        h2T_ps = sem("h2T_ps")
        h2T_ready = sem("h2T_ready")
        logit_ps = sem("logit_ps")
        top_ready = sem("top_ready")
        gexp = sem("gexp")
        picked = sem("picked")
        rank_ps = sem("rank_ps")
        gates_ready = sem("gates_ready")
        gT_ps = sem("gT_ps")
        gT_ready = sem("gT_ready")
        table_ready = sem("table_ready")
        w1_used = sem("w1_used")
        w2_used = sem("w2_used")
        sel_ready = sem("sel_ready")
        selg_ready = sem("selg_ready")
        xg_ps = sem("xg_ps")
        xT_ready = sem("xT_ready")
        hid_ps = sem("hid_ps")
        g_ready = sem("g_ready")
        hid_read = sem("hid_read")
        um_ready = sem("um_ready")
        sig_ready = sem("sig_ready")
        act_ready = sem("act_ready")
        out_ps = sem("out_ps")
        actT_ps = sem("actT_ps")
        actT_ready = sem("actT_ready")
        put_ps = sem("put_ps")
        put_ready = sem("put_ready")
        y_ready = sem("y_ready")
        comb_ps = sem("comb_ps")
        added_half = sem("added_half")
        added = sem("added")

        ps_xg = [t_bank, y_bank]
        ps_act, ps_put = bank01, bank[2]
        ps_y = pair
        bu_bank, yo_bank = bank[2], bank[3]

        def col(a, n=1):
            return stat[:, a:a + n]
        x_ss, x_std, x_rs = col(0, 2), col(2, 2), col(4, 2)
        n_ss, n_std, n_rs = col(6, 16), col(22, 16), col(38, 16)
        lam_sum, lam_exp, neg_lam = col(54, 2), col(56, 2), col(58)
        s_max, n_bias, p_sum, p_rs = col(60, 4), col(64, 4), col(68, 4), col(72, 4)
        p_c1 = col(76, 2)
        o_ss, o_rs = col(80, 16), col(96, 16)
        top8 = stat[:, 112:128].rearrange("p (t n) -> p t n", t=TT)
        neg_top, over, need, g_sum, g_rs = col(128, 2), col(130, 2), col(132, 2), col(134, 2), col(136, 2)
        x1_parts = col(138, 4)
        sub_gain, half_pi, eps = col(157), col(158), col(159)
        names = ["ldt", "lr", "li", "k", "r", "q", "pw", "dt", "a", "em1", "mag", "th", "thk", "thr", "sh", "ch",
                 "cos", "sin", "vers", "nr", "ai", "den", "t1", "t2", "cr", "ci"]
        sm = {n: small[:, i, :] for i, n in enumerate(names)}

        block = ctx.enter_context(nc.Block())

        def is_first(i):
            return isinstance(i, int) and i == 0

        def chunk_bank(c):
            return pair if c in (1, 3, 5) else bank01

        def branch_bank(attn, n):
            if attn:
                return bank[2 * n:2 * n + 2]
            return (pair[:, 0, :], pair[:, 1, :]) if n == 0 else (t_bank[:, :], y_bank[:, :])

        def stream_source(i):
            def cut(w, kh, n):
                return w[512 * kh:512 * kh + 512, N * n:N * n + N].rearrange("(k p) n -> p k n", p=P)
            if i < P_GLU:
                return cut(w_in_d[0], i % 2, i // 2)
            if i == P_GLU:
                return cut(t["w_glu"][0], 0, 0)
            if i < P_WOUT:
                attn, n, kh = BRANCH[i - P_BRANCH]
                return cut((t["w_proj_attn"] if attn else t["w_proj_ssm"])[0], kh, n)
            return cut(t["w_out"][0], (i - P_WOUT) // 2, (i - P_WOUT) % 2)

        def w1_slot(odd, k, x):
            return (2 * k + x + W1P * odd) % RING

        def w2_slot(odd, m, x):
            return 2 * m + x + W1P * odd

        def w1_load(eng, i, e, k, x, odd):
            src = t["w_exp1"][0, bass.ds(e, 1), P * k:P * k + P, :].rearrange("e p n -> p (e n)")
            eng.dma_start(w1_piece(i, k, x, odd), src).then_inc(w1_in[k], 16)

        def w2_load(eng, e, m, x, dst):
            src = t["w_exp2"][0, bass.ds(e, 1), 2 * P * m:2 * P * m + 2 * P, :].rearrange("e (k p) n -> p (e k) n", p=P)
            eng.dma_start(dst, src).then_inc(w2_in[m], 16)

        def w1_piece(i, k, x, odd):
            if is_first(i) and k == 3:
                return (uu[:, :], sgf[:, 0:2048])[x]
            return ring[:, w1_slot(odd, k, x), :]

        def w2_piece(i, m, x, odd):
            if is_first(i) and (m, x) == (0, 0):
                return hT[:, :, :].rearrange("p a b -> p (a b)").rearrange("p (k n) -> p k n", k=2)
            return ring[:, w2_slot(odd, m, x), :].rearrange("p (k n) -> p k n", k=2)

        def load_c(eng, r, name, loaded):
            src = t[name][0].rearrange("(c b) h p -> b h c p", c=CT)
            for b in range(8):
                g = b % 2
                eng.dma_start(c_raw[16 * b:16 * b + 16, r, :, 64 * g:64 * g + 64], src[b]).then_inc(loaded, 16)

        prow_loads = [
            (prow[LRE:LRE + NST, :], t["lambda_re"][0].rearrange("(j g) p -> j (g p)", g=2)),
            (prow[LIM:LIM + NST, :], t["lambda_im"][0].rearrange("(j g) p -> j (g p)", g=2)),
            (ldt2[LDT:LDT + NST, :], t["log_dt"][0].rearrange("(j g) -> j g", g=2)),
            (prow[G1:G1 + KT, :], t["norm1_gain"][0].rearrange("(k p) -> k p", p=P)),
            (prow[BG:BG + CT, :], t["b_glu"][0].rearrange("(k p) -> k p", p=P)),
            (prow[DS:DS + CT, :], t["ssm_d"][0].rearrange("(c g) h -> c (g h)", c=CT)),
            (prow[G2:G2 + KT, :], t["norm2_gain"][0].rearrange("(k p) -> k p", p=P)),
            (prow[SG:SG + 1, :], t["subln_gain"]),
        ] + [(prow[r:r + 1, 64 * m:64 * m + 64], t[name]) for r, name in ((QG, "q_norm_gain"), (KG, "k_norm_gain"))
             for m in range(2)]

        @block.sync
        def _(sp):
            sp.dma_start(x_acc[:, :, :], x_d[0].rearrange("(t p) n -> p t n", p=P)).then_inc(x_in, 16)
            sp.wait_ge(zeroed, 1)
            for row, src in prow_loads[5:9]:
                sp.dma_start(row, src).then_inc(prow_in, 16)

            def stream_piece(i):
                if i >= 4:
                    sp.wait_ge(piece_used, i - 3)
                sp.dma_start(ring[:, STREAM + i % 4, :].rearrange("p (k n) -> p k n", k=4),
                             stream_source(i)).then_inc(piece_in[i % 4], 16)

            stream_piece(0)
            for row, src in prow_loads[9:]:
                sp.dma_start(row, src).then_inc(prow_in, 16)
            for i in range(1, 5):
                stream_piece(i)
            for x in range(2):
                w1_load(sp, 0, x, 0, x, 0)
            for i in range(5, P_BRANCH):
                stream_piece(i)
            sp.wait_ge(xs_ready, NST)
            for k in (4, 5):
                for x in range(2):
                    w1_load(sp, 0, x, k, x, 0)
            sp.dma_start(b2_sb, t["b_exp2"][0]).then_inc(b2_in, 16)
            for i in range(P_BRANCH, P_BRANCH + 3):
                stream_piece(i)
            sp.wait_ge(oT_ps, 4)
            for k in (1, 2, 3):
                stream_piece(P_BRANCH + 2 + k)
                for x in range(2):
                    if k < 3:
                        w1_load(sp, 0, x, k, x, 0)
                    else:
                        w2_load(sp, x, 3, x, w2_piece(0, 3, x, 0))
            for i in range(P_WOUT, N_PIECES):
                stream_piece(i)
            for i, (k, x) in zip(range(P_WOUT, N_PIECES), ((6, 1), (7, 0), (7, 1), (6, 0))):
                sp.wait_ge(piece_used, i + 1)
                w1_load(sp, 0, x, k, x, 0)
                if i == P_WOUT:
                    sp.wait_ge(mT_ps, 4)
                    for x3 in range(2):
                        w1_load(sp, 0, x3, 3, x3, 0)
            sp.wait_ge(sout_ready, 1)
            for x in range(2):
                sp.dma_start(b1_rows[32 * x:32 * x + 1, :], t["b_exp1"][0, x:x + 1, :]).then_inc(b1_in, 16)
            sp.wait_ge(logit_ps, 1)
            w2_load(sp, 0, 0, 0, w2_piece(0, 0, 0, 0))

            def load_w2(i, es, odd):
                for m in range(W2P):
                    sp.wait_ge(w1_used, i * W1P + m + 1)
                    for x in range(2):
                        if not (is_first(i) and (m, x) in ((0, 0), (3, 0), (3, 1))):
                            w2_load(sp, es[x], m, x, w2_piece(i, m, x, odd))

            def load_block(i, es, odd, after_odd):
                for k in range(W1P):
                    if k < W1P // 2 and after_odd != odd:
                        sp.wait_ge(w1_used, (i - 1) * W1P + W1P // 2 + k + 1)
                    else:
                        sp.wait_ge(w2_used, (i - 1) * W2P + k % W2P + 1)
                    if k == 3:
                        for x in range(2):
                            sp.dma_start(b1_rows[32 * x:32 * x + 1, :],
                                         t["b_exp1"][0, bass.ds(es[x], 1), :]).then_inc(b1_in, 16)
                    for x in range(2):
                        w1_load(sp, i, es[x], k, x, odd)
                load_w2(i, es, odd)

            load_w2(0, (0, 1), 0)
            with sp.Fori(1, NB - 1, 2) as i:
                load_block(i, (2 * i, 2 * i + 1), 1, 0)
                load_block(i + 1, (2 * i + 2, 2 * i + 3), 0, 1)
            load_block(NB - 1, (E - 2, E - 1), 1, 0)
            sp.wait_ge(table_ready, 1)
            extra = sp.value_load(table[0:1, 0:1], min_val=0, max_val=MAX_EXTRA // 2)
            with sp.If(extra > 0):
                with sp.Fori(0, extra) as j:
                    es = [sp.value_load(table[0:1, bass.ds(2 * j + 2 + x, 1)], min_val=0, max_val=E - 1) for x in range(2)]
                    load_block(j + NB, es, 0, 0)
            for c in range(2):
                sp.wait_ge(added, (extra + NB) * 2 + 1 + c)
                cols = slice(N * c, N * c + N)
                sp.dma_start(out[0, :, cols].rearrange("(t p) n -> p t n", p=P), x_acc[:, :, cols]).then_inc(out_in, 16)
            sp.wait_ge(out_in, 32)

        @block.gpsimd
        def _(pool):
            n_step = [0]

            def step(ins):
                n_step[0] += 1
                ins.then_inc(pool_step, 1)
                pool.wait_ge(pool_step, n_step[0])

            nc.gpsimd.memset(prow[:, :], 0.0).then_inc(zeroed, 1)
            nc.gpsimd.memset(att[:, 0:2048], 0.0).then_inc(zeroed, 1)
            pool.wait_ge(zeroed, 2)
            step(nc.gpsimd.memset(ones[:, :], 1.0))
            step(nc.gpsimd.memset(ident[:, :], 0.0))
            nc.gpsimd.affine_select(out=ident[:, :], in_=ident[:, :], compare_op=ALU.not_equal, fill=1.0, base=0,
                                    pattern=[[-1, P]], channel_multiplier=1).then_inc(consts, 1)
            nc.gpsimd.affine_select(out=before[:, :], in_=ones[:, :], compare_op=ALU.is_gt, fill=0.0, base=0,
                                    pattern=[[1, P]], channel_multiplier=-1).then_inc(consts, 1)
            for r, name in enumerate(("ssm_b_re", "ssm_b_im")):
                src = t[name][0].rearrange("(j g) p h -> g p j h", g=2)
                for g in range(2):
                    pool.dma_start(b_raw[64 * g:64 * g + 64, r, :, 16 * g:16 * g + 16], src[g]).then_inc(bc_in, 16)
            load_c(pool, 0, "ssm_c_re", bc_in)
            for i, name in enumerate(("lambda_q1", "lambda_k1", "lambda_q2", "lambda_k2")):
                pool.dma_start(lq[:, i, :], t[name][0].partition_broadcast(P)).then_inc(misc_in, 16)
            pool.dma_start(w_r[:, :, :], t["w_router"][0].rearrange("(k p) e -> p k e", p=P)).then_inc(misc_in, 16)
            pool.dma_start(route[:, 6, 0, :], t["b_router"][0].partition_broadcast(P)).then_inc(misc_in, 16)
            step(nc.gpsimd.memset(causal[:, :, :], 0.0))
            for b in (0, 2):
                nc.gpsimd.affine_select(out=causal[:, b, :], in_=causal[:, b, :], compare_op=ALU.is_ge, fill=MASKED,
                                        base=0, pattern=[[-1, P]], channel_multiplier=1).then_inc(consts, 1)
            nc.gpsimd.iota(iota[:, :], pattern=[[1, 5 * SLOT]], base=0, channel_multiplier=0,
                           allow_small_or_imprecise_dtypes=True).then_inc(consts, 1)
            pool.wait_ge(coef_ready, 1)
            pool.wait_ge(c_read, 2)
            cre, cim = cT[:, 0, :, :], cT[:, 1, :, :]
            w = [tmp[:, i, :, :].rearrange("p a n -> p (a n)").rearrange("p (j n) -> p j n", j=NST) for i in range(3)]
            cr_w, ci_w, minus_ci_w = (sm[name].unsqueeze(2).to_broadcast([P, NST, 32]) for name in ("cr", "ci", "pw"))
            step(nc.gpsimd.tensor_tensor(w[0], cre, cr_w, ALU.mult))
            step(nc.gpsimd.tensor_tensor(w[1], cim, ci_w, ALU.mult))
            step(nc.gpsimd.tensor_tensor(w[2], cre, minus_ci_w, ALU.mult))
            nc.gpsimd.tensor_tensor(cT[:, 0, :, :], w[0], w[1], ALU.subtract).then_inc(cT_ready, 1)
            pool.wait_ge(cT_ready, 1)
            step(nc.gpsimd.tensor_tensor(w[0], cim, cr_w, ALU.mult))
            nc.gpsimd.tensor_tensor(cT[:, 1, :, :], w[2], w[0], ALU.subtract).then_inc(cT_ready, 1)
            pool.wait_ge(turn_base, 1)
            for j0, j1 in ((4, 8), (8, NST)):
                js = slice(j0, j1)
                for n, pr, pi in ((64, "t1", "t2"), (128, "th", "thk")):
                    def wide(name):
                        return sm[name][:, js].unsqueeze(2).to_broadcast([P, j1 - j0, n])
                    c0, s0 = turn[:, js, 0, 0:n], turn[:, js, 1, 0:n]
                    a, b = turn_t[:, 0, js, 0:n], turn_t[:, 1, js, 0:n]
                    step(nc.gpsimd.tensor_tensor(a, c0, wide(pr), ALU.mult))
                    step(nc.gpsimd.tensor_tensor(b, s0, wide(pi), ALU.mult))
                    step(nc.gpsimd.tensor_tensor(turn[:, js, 0, n:2 * n], a, b, ALU.subtract))
                    step(nc.gpsimd.tensor_tensor(a, c0, wide(pi), ALU.mult))
                    step(nc.gpsimd.tensor_tensor(b, s0, wide(pr), ALU.mult))
                    if n == 64:
                        step(nc.gpsimd.tensor_tensor(turn[:, js, 1, n:2 * n], a, b, ALU.add))
                    else:
                        nc.gpsimd.tensor_tensor(turn[:, js, 1, n:2 * n], a, b, ALU.add).then_inc(turns_ready, 1)

        @block.scalar
        def _(act):
            act.wait_ge(dve_step, 2)
            nc.scalar.activation(x_std, eps.to_broadcast([P, TT]), ACT.Sqrt).then_inc(act_step, 1)
            act.wait_ge(zeroed, 1)
            for row, src in prow_loads[0:5]:
                act.dma_start(row, src).then_inc(prow_in, 16)
            act.wait_ge(x_in, 16)
            nc.scalar.activation(sq_x[:, 0, :], x_acc[:, 0, :], ACT.Square, accum_out=x_ss[:, 0:1]).then_inc(act_step, 1)
            act.wait_ge(act_step, 2)
            act.wait_ge(dve_step, 3)
            nc.scalar.activation(x_std, x_ss, ACT.Sqrt, bias=eps, scale=1.0 / D).then_inc(x_sq, 1)
            for b in (1, 3):
                act.wait_ge(pcol_ready, 1)
                act.wait_ge(hT_ps, b + 1)
                for k in (2 * b, 2 * b + 1):
                    nc.scalar.activation(hT[:, k, :], bank[b][:, 256 * (k % 2):256 * (k % 2) + 256], ACT.Identity,
                                         scale=pcol[:, G1 + k:G1 + k + 1]).then_inc(hT_act, 1)
            act.wait_ge(zeroed, 2)
            load_c(act, 1, "ssm_c_im", c_im_in)
            act.wait_ge(sin_in, 1)
            nc.scalar.activation(sm["sh"], sm["thr"], ACT.Sin, scale=0.5).then_inc(sin_ready, 1)
            nc.scalar.activation(sm["ch"], sm["thr"], ACT.Sin, scale=0.5, bias=half_pi).then_inc(sin_ready, 1)
            act.wait_ge(b_ps, 2)
            for r in range(2):
                nc.scalar.copy(bT[:, :, r, :], bank23[:, r, :].rearrange("p (c n) -> p c n", c=CT)).then_inc(bT_ready, 1)
            for r, ps in enumerate((t_bank, y_bank)):
                act.wait_ge(c_ps, r + 1)
                nc.scalar.copy(cT[:, r, :, :], ps[:, :].rearrange("p (j n) -> p j n", j=NST)).then_inc(c_read, 1)

            def copy_t(dst, ps, gain=None):
                if gain is None:
                    nc.scalar.copy(dst, ps).then_inc(t_read, 1)
                else:
                    nc.scalar.activation(dst, ps, ACT.Identity, scale=gain).then_inc(t_read, 1)

            for c in range(7):
                act.wait_ge(piece_used, 2 * c + 2)
                ps = chunk_bank(c)
                if c == 0:
                    for tt in range(TT):
                        nc.scalar.copy(u_tok[:, tt, :], ps[:, tt, :]).then_inc(chunk_read, 1)
                    act.wait_ge(t_ps, 1)
                    copy_t(uT[:, 0:2, :], t_bank[:, :].rearrange("p (c n) -> p c n", c=2))
                    act.wait_ge(t_ps, 2)
                    copy_t(uT[:, 2:4, :], y_bank[:, :].rearrange("p (c n) -> p c n", c=2))
                elif c < 5:
                    if c >= 2:
                        act.wait_ge(qk_ss, c - 1)
                    for tt in range(TT):
                        nc.scalar.activation(sq[:, tt, :], ps[:, tt, :], ACT.Square).then_inc(qk_sq, 1)
                    act.wait_ge(qk_ss, c)
                    nc.scalar.activation(n_std, n_ss, ACT.Sqrt, bias=eps,
                                         scale=1.0 / 64).then_inc(qk_std, 1)
                    dst, gain = (qT, QG) if c < 3 else (kT, KG)
                    for r in range(2):
                        h = 4 * ((c - 1) % 2) + 2 * r
                        act.wait_ge(t_ps, 2 * c + r + 1)
                        copy_t(dst[:, h:h + 2, :], (t_bank, y_bank)[r][:, :].rearrange("p (h n) -> p h n", h=2),
                               pcol[:, gain:gain + 1])
                else:
                    for tt in range(TT):
                        nc.scalar.copy(v_tok[:, tt, N * (c - 5):N * (c - 5) + N], ps[:, tt, :]).then_inc(chunk_read, 1)

            act.wait_ge(nmax, 1)
            nc.scalar.activation(lam_exp, lam_sum, ACT.Exp).then_inc(act_step, 1)

            def gate_chunk(g):
                act.wait_ge(piece_used, 2 * (7 + g) + 2)
                for tt in range(TT):
                    nc.scalar.copy(sg[:, g // 2, tt, N * (g % 2):N * (g % 2) + N], bank01[:, tt, :]).then_inc(chunk_read, 1)

            for h in range(HEADS):
                act.wait_ge(nmax, h + 2)
                for m in range(2):
                    for qt in range(2):
                        cs = slice(0, 128) if qt == 0 else slice(128, 384)
                        i = 2 * m + qt
                        nc.scalar.activation(probs[:, m, cs], masked[:, m, cs], ACT.Exp, bias=n_bias[:, i:i + 1],
                                             scale=SCALE, accum_out=p_sum[:, i:i + 1]).then_inc(p_ready, 1)
                if h == 1:
                    act.wait_ge(turns_ready, 2)
                if h % 2 and h < HEADS - 1:
                    gate_chunk(h // 2)
                if h == HEADS - 1:
                    act.wait_ge(gel_in, 1)
                    nc.scalar.activation(glu_g, glu_a, ACT.Sigmoid, scale=2 * 0.7978845608028654).then_inc(gel_sig, 1)
                act.wait_ge(aT_ps, h + 1)
                nc.scalar.copy(aT, t_bank[:, 0:384].rearrange("p (b n) -> p b n", b=3)).then_inc(aT_ready, 1)
                act.wait_ge(o_ps, h + 1)
                for qt in range(2):
                    ps = y_bank[:, 128 * qt:128 * qt + 128]
                    nc.scalar.activation(o_sq[:, qt, :], ps, ACT.Square,
                                         accum_out=o_ss[:, 8 * qt + h:8 * qt + h + 1]).then_inc(o_read, 1)
                    nc.scalar.copy(o_tok[:, qt, 128 * h:128 * h + 128], ps).then_inc(o_read, 1)
            act.wait_ge(o_read, 4 * HEADS)
            nc.scalar.activation(o_rs, o_ss, ACT.Sqrt, bias=eps, scale=1.0 / P).then_inc(o_std, 1)
            gate_chunk(HEADS // 2 - 1)

            def gates(a):
                nc.scalar.activation(sg[:, a, :, :], sg[:, a, :, :], ACT.Sigmoid).then_inc(gates_sig, 1)

            act.wait_ge(chunk_read, 14)
            gates(1)
            for ct in range(CT):
                if ct < 2:
                    act.wait_ge(glu_ps, 1)
                else:
                    act.wait_ge(piece_used, P_GLU + 1)
                nc.scalar.activation(glu_g[:, S * ct:S * ct + S], pair[:, ct // 2, S * (ct % 2):S * (ct % 2) + S], ACT.Sigmoid,
                                     bias=pcol[:, BG + ct:BG + ct + 1]).then_inc(glu_sig, 1)
            for b in range(4):
                act.wait_ge(oT_ps, b + 1)
                nc.scalar.activation(oT[:, 2 * b:2 * b + 2, :], bank[b][:, :].rearrange("p (h n) -> p h n", h=2), ACT.Identity,
                                     scale=sub_gain).then_inc(oT_ready, 1)
            gates(0)
            for b in range(4):
                act.wait_ge(mT_ps, b + 1)
                nc.scalar.copy(hT[:, 2 * b:2 * b + 2, :],
                               bank[b][:, :].rearrange("p (h n) -> p h n", h=2)).then_inc(mT_ready, 1)
            act.wait_ge(o_norm, 2)
            nc.scalar.activation(o_rs, o_ss, ACT.Sqrt, bias=eps, scale=1.0 / P)
            act.wait_ge(x1_ready, 2)
            for tt in range(TT):
                nc.scalar.activation(sg[:, 1, tt, 0:N], x_acc[:, tt, 0:N], ACT.Square,
                                     accum_out=x1_parts[:, tt:tt + 1]).then_inc(x1_sq, 1)
            for half in range(2):
                for b in range(2):
                    act.wait_ge(h2T_ps, 2 * half + b + 1)
                    for kk in range(2):
                        k = 4 * half + 2 * b + kk
                        ps = (bank23[:, b, :] if half == 0 else (t_bank, y_bank)[b])[:, S * kk:S * kk + S]
                        nc.scalar.activation(hT[:, k, :], ps, ACT.Identity, scale=pcol[:, G2 + k:G2 + k + 1]).then_inc(h2T_ready, 1)
            act.wait_ge(x1_ss, 1)
            nc.scalar.activation(x_std, x_ss, ACT.Sqrt, bias=eps, scale=1.0 / D).then_inc(x1_std, 1)
            for tt in range(TT):
                act.wait_ge(top_ready, tt + 1)
                nc.scalar.activation(route[:, 1, tt, :], route[:, 0, tt, :], ACT.Exp,
                                     bias=neg_top[:, tt:tt + 1]).then_inc(gexp, 1)
            act.wait_ge(gT_ps, 1)
            nc.scalar.copy(gateT[:, :], pair[0:E, 0, 0:S]).then_inc(gT_ready, 1)

            def block_work(i):
                for b in range(2):
                    act.wait_ge(g_ready, 2 * i + b + 1)
                    nc.scalar.activation(s_act[:, N * b:N * b + N], g_act[:, N * b:N * b + N], ACT.Sigmoid,
                                         scale=1.702).then_inc(sig_ready, 1)
                for b in range(2):
                    act.wait_ge(actT_ps, 2 * i + b + 1)
                    nc.scalar.copy(actT[:, 4 * b:4 * b + 4, :],
                                   ps_act[:, b, :].rearrange("p (f n) -> p f n", f=4)).then_inc(actT_ready, 1)
                act.wait_ge(put_ps, i + 1)
                act.wait_ge(comb_ps, 2 * i + 2)
                nc.scalar.copy(put, ps_put[:, 0:S]).then_inc(put_ready, 1)
                for c in range(2):
                    if c == 0:
                        act.wait_ge(out_ps, i + 1)
                    else:
                        act.wait_ge(w2_used, (i + 1) * W2P)
                    nc.scalar.copy(y_sb[:, N * c:N * c + N], ps_y[:, c, :]).then_inc(y_ready, 1)

            block_work(0)
            with act.Fori(1, NB) as i:
                block_work(i)
            act.wait_ge(table_ready, 1)
            extra = act.value_load(table[0:1, 0:1], min_val=0, max_val=MAX_EXTRA // 2)
            with act.If(extra > 0):
                with act.Fori(0, extra) as j:
                    block_work(j + NB)

        @block.vector
        def _(dve):
            V = nc.vector
            n_step = [0]

            def mark(ins):
                n_step[0] += 1
                ins.then_inc(dve_step, 1)

            def sync():
                dve.wait_ge(dve_step, n_step[0])

            def step(ins):
                mark(ins)
                sync()

            def mul(out, a, b):
                return V.tensor_tensor(out, a, b, ALU.mult)

            mark(V.memset(half_pi, math.pi / 2))
            step(V.memset(eps, EPS))
            dve.wait_ge(x_in, 16)
            mark(V.tensor_tensor_reduce(out=sq_x[:, 1, :], in0=x_acc[:, 1, :], in1=x_acc[:, 1, :], scale=1.0, scalar=0.0,
                                        op0=ALU.mult, op1=ALU.add, accum_out=x_ss[:, 1:2]))
            dve.wait_ge(x_sq, 1)
            step(V.reciprocal(x_rs, x_std))
            for tt in range(TT):
                V.tensor_scalar(h_tok[:, tt, :], x_acc[:, tt, :], x_rs[:, tt:tt + 1], None, ALU.mult).then_inc(h_ready, 1)
            dve.wait_ge(prow_in, 16 * 12)
            V.tensor_copy(prow[LDT:LDT + NST, :].rearrange("j (g p) -> j g p", g=2),
                          ldt2[LDT:LDT + NST, :].unsqueeze(2).to_broadcast([NST, 2, 64])).then_inc(prow_ready, 1)
            dve.wait_ge(pcol_ps, 1)
            V.tensor_copy(pcol[:, :], t_bank[:, 0:P]).then_inc(pcol_ready, 1)
            dve.wait_ge(pcol_ready, 1)
            for b in (0, 2):
                dve.wait_ge(hT_ps, b + 1)
                for k in (2 * b, 2 * b + 1):
                    V.tensor_scalar(hT[:, k, :], bank[b][:, S * (k % 2):S * (k % 2) + S], pcol[:, G1 + k:G1 + k + 1], None,
                                    ALU.mult).then_inc(hT_dve, 1)

            step(V.tensor_scalar(sub_gain, pcol[:, SG:SG + 1], 1.0 - LAMBDA_INIT, None, ALU.mult))

            def exponential(x):
                step(V.tensor_scalar(sm[x], sm[x], -100.0, 88.0, ALU.max, ALU.min))
                step(V.tensor_scalar(sm["k"], sm[x], LOG2E, MAGIC, ALU.mult, ALU.add))
                step(V.tensor_scalar(sm["k"], sm["k"], MAGIC, -127.0, ALU.subtract, ALU.max))
                step(V.scalar_tensor_tensor(sm["r"], sm["k"], -LN2_HI, sm[x], ALU.mult, ALU.add))
                step(V.scalar_tensor_tensor(sm["r"], sm["k"], -LN2_LO, sm["r"], ALU.mult, ALU.add))
                mark(V.tensor_scalar(sm["pw"].bitcast(I32), sm["k"], 127.0, 2.0 ** 23, ALU.add, ALU.mult))
                step(V.tensor_scalar(sm["q"], sm["r"], 1.0 / 8, 1.0, ALU.mult, ALU.add))
                for n in (7, 6, 5, 4, 3, 2):
                    step(mul(sm["q"], sm["q"], sm["r"]))
                    step(V.tensor_scalar(sm["q"], sm["q"], 1.0 / n, 1.0, ALU.mult, ALU.add))
                step(mul(sm["q"], sm["q"], sm["r"]))

            step(V.tensor_copy(sm["ldt"], pcol[:, LDT:LDT + NST]))
            exponential("ldt")
            step(V.scalar_tensor_tensor(sm["dt"], sm["q"], 1.0, sm["pw"], ALU.add, ALU.mult))
            mark(V.tensor_scalar(sm["lr"], pcol[:, LRE:LRE + NST], -1e-4, None, ALU.min))
            mark(V.tensor_copy(sm["li"], pcol[:, LIM:LIM + NST]))
            step(mul(sm["th"], pcol[:, LIM:LIM + NST], sm["dt"]))
            step(V.tensor_scalar(sm["thk"], sm["th"], INV_2PI, MAGIC, ALU.mult, ALU.add))
            step(V.tensor_scalar(sm["thk"], sm["thk"], MAGIC, None, ALU.subtract))
            step(V.scalar_tensor_tensor(sm["thr"], sm["thk"], -TWO_PI_1, sm["th"], ALU.mult, ALU.add))
            step(V.scalar_tensor_tensor(sm["thr"], sm["thk"], -TWO_PI_2, sm["thr"], ALU.mult, ALU.add))
            step(V.scalar_tensor_tensor(sm["thr"], sm["thk"], -TWO_PI_3, sm["thr"], ALU.mult, ALU.add))
            V.tensor_scalar(sm["thr"], sm["thr"], -3.14159, 3.14159, ALU.max, ALU.min).then_inc(sin_in, 1)
            step(mul(sm["a"], sm["lr"], sm["dt"]))
            exponential("a")
            mark(V.scalar_tensor_tensor(sm["mag"], sm["q"], 1.0, sm["pw"], ALU.add, ALU.mult))
            mark(V.tensor_scalar(sm["t2"], sm["pw"], 1.0, None, ALU.subtract))
            step(mul(sm["t1"], sm["q"], sm["pw"]))
            step(V.tensor_tensor(sm["em1"], sm["t1"], sm["t2"], ALU.add))
            dve.wait_ge(sin_ready, 2)
            mark(V.scalar_tensor_tensor(sm["sin"], sm["sh"], 2.0, sm["ch"], ALU.mult, ALU.mult))
            step(V.scalar_tensor_tensor(sm["vers"], sm["sh"], 2.0, sm["sh"], ALU.mult, ALU.mult))
            step(V.tensor_scalar(sm["cos"], sm["vers"], -1.0, 1.0, ALU.mult, ALU.add))
            mark(mul(sm["ai"], sm["mag"], sm["sin"]))
            step(mul(sm["nr"], sm["em1"], sm["cos"]))
            step(V.tensor_tensor(sm["nr"], sm["nr"], sm["vers"], ALU.subtract))
            mark(mul(sm["t1"], sm["lr"], sm["lr"]))
            step(mul(sm["t2"], sm["li"], sm["li"]))
            step(V.tensor_tensor(sm["den"], sm["t1"], sm["t2"], ALU.add))
            step(V.reciprocal(sm["den"], sm["den"]))
            mark(mul(sm["t1"], sm["nr"], sm["lr"]))
            step(mul(sm["t2"], sm["ai"], sm["li"]))
            step(V.tensor_tensor(sm["t1"], sm["t1"], sm["t2"], ALU.add))
            step(mul(sm["cr"], sm["t1"], sm["den"]))
            mark(mul(sm["t1"], sm["ai"], sm["lr"]))
            step(mul(sm["t2"], sm["nr"], sm["li"]))
            step(V.tensor_tensor(sm["t1"], sm["t1"], sm["t2"], ALU.subtract))
            mark(mul(sm["ci"], sm["t1"], sm["den"]))
            step(V.tensor_scalar(sm["pw"], sm["t1"], -1.0, None, ALU.mult))
            mul(sm["pw"], sm["pw"], sm["den"]).then_inc(coef_ready, 1)
            dve.wait_ge(coef_ready, 1)
            def norm_qk(c):
                dve.wait_ge(qk_sq, 2 * c)
                V.tensor_reduce(n_ss, sq.rearrange("p t (g d) -> p (t g) d", d=64), AX.X, ALU.add).then_inc(qk_ss, 1)
                dve.wait_ge(qk_std, c)
                step(V.reciprocal(n_rs, n_std))
                if c >= 2:
                    dve.wait_ge(t_ps, 2 * c)
                for tt in range(TT):
                    mul(qn[:, tt, :].rearrange("p (g d) -> p g d", d=64),
                        chunk_bank(c)[:, tt, :].rearrange("p (g d) -> p g d", d=64),
                        n_rs[:, 8 * tt:8 * tt + 8].unsqueeze(2).to_broadcast([P, 8, 64])).then_inc(qk_n, 1)

            dve.wait_ge(misc_in, 16 * 6)
            for i in range(2):
                mark(V.tensor_tensor_reduce(out=lam_prod[:, i, :], in0=lq[:, 2 * i, :], in1=lq[:, 2 * i + 1, :], scale=1.0,
                                            scalar=0.0, op0=ALU.mult, op1=ALU.add, accum_out=lam_sum[:, i:i + 1]))
            sync()
            powers = {1: ("cos", "sin"), 2: ("ldt", "q"), 4: ("k", "r"), 8: ("a", "em1"), 16: ("nr", "ai"),
                      32: ("sh", "ch"), 64: ("t1", "t2"), 128: ("th", "thk")}
            for n in (1, 2, 4, 8, 16, 32, 64):
                (pr, pi), (qr, qi) = powers[n], powers[2 * n]
                mark(mul(sm["den"], sm[pr], sm[pr]))
                mark(mul(sm["dt"], sm[pi], sm[pi]))
                step(V.scalar_tensor_tensor(sm[qi], sm[pr], 2.0, sm[pi], ALU.mult, ALU.mult))
                step(V.tensor_tensor(sm[qr], sm["den"], sm["dt"], ALU.subtract))
            dve.wait_ge(hT_ps, 4)
            mark(V.memset(turn[:, :, 0, 0:1], 1.0))
            step(V.memset(turn[:, :, 1, 0:1], 0.0))
            for n in (1, 2, 4, 8, 16, 32, 64, 128):
                tiles = NST if n < 64 else 4
                if n == 64:
                    norm_qk(1)

                def wide(name):
                    return sm[name][:, 0:tiles].unsqueeze(2).to_broadcast([P, tiles, n])
                pr, pi = powers[n]
                c0, s0 = turn[:, 0:tiles, 0, 0:n], turn[:, 0:tiles, 1, 0:n]
                c1, s1 = turn[:, 0:tiles, 0, n:2 * n], turn[:, 0:tiles, 1, n:2 * n]
                a, b = turn_t[:, 0, 0:tiles, 0:n], turn_t[:, 1, 0:tiles, 0:n]
                mark(mul(a, c0, wide(pr)))
                mark(mul(b, s0, wide(pi)))
                mark(mul(c1, c0, wide(pi)))
                step(mul(s1, s0, wide(pr)))
                step(V.tensor_tensor(s1, s1, c1, ALU.add))
                ins = V.tensor_tensor(c1, a, b, ALU.subtract)
                if n == 32:
                    ins.then_inc(turn_base, 1)
                    dve.wait_ge(turn_base, 1)
                else:
                    step(ins)
            def state_tile(j):
                if j == 0:
                    dve.wait_ge(cT_ready, 2)
                if j == 4:
                    dve.wait_ge(turns_ready, 1)
                if j == 8:
                    dve.wait_ge(turns_ready, 2)
                rot = turn[:, j, :, :]
                src = bu_bank.rearrange("p (r n) -> p r n", r=2)
                a, b, v = tmp[:, 0, :, :], tmp[:, 1, :, :], tmp[:, 2, :, :]
                decay = sm["mag"][:, j:j + 1].to_broadcast([P, S])
                dve.wait_ge(bu_ps, j + 1)
                mark(mul(a, rot, src))
                mul(b, rot, src[:, ::-1, :]).then_inc(bu_read, 1)
                dve.wait_ge(bu_read, j + 1)
                sync()
                mark(V.tensor_tensor(v[:, 0, :], a[:, 0, :], a[:, 1, :], ALU.add))
                mark(V.tensor_tensor(v[:, 1, :], b[:, 0, :], b[:, 1, :], ALU.subtract))
                sync()
                for r in range(2):
                    mark(V.tensor_tensor_scan(a[:, r, :], decay, v[:, r, :], 0.0, ALU.mult, ALU.add))
                sync()
                mark(mul(b, rot, a))
                mark(mul(v, rot, a[:, ::-1, :]))
                sync()
                if j >= 2:
                    dve.wait_ge(y_ps, j - 1)
                mark(V.tensor_tensor(x_state[:, j % 2, 0, :], b[:, 0, :], b[:, 1, :], ALU.subtract))
                V.tensor_tensor(x_state[:, j % 2, 1, :], v[:, 0, :], v[:, 1, :], ALU.add).then_inc(xs_ready, 1)
                dve.wait_ge(xs_ready, j + 1)
                sync()

            def ssm_out(ct):
                dve.wait_ge(y_ps, 4 * ct + 4)
                if ct == 0:
                    dve.wait_ge(t_read, 2)
                V.scalar_tensor_tensor(yT[:, ct, :], uT[:, ct, :], pcol[:, DS + ct:DS + ct + 1],
                                       yo_bank[:, S * (ct % 2):S * (ct % 2) + S], ALU.mult, ALU.add).then_inc(y_read, 1)

            def ssm_slot(p):
                if p in SSM_AT:
                    j = SSM_AT[p]
                    state_tile(j)
                    if j % 4 == 1 and j > 4:
                        ssm_out(j // 4 - 1)

            def maxima(h):
                dve.wait_ge(s_ps, h + 1)
                for m in range(2):
                    for qt in range(2):
                        cs = slice(0, 128) if qt == 0 else slice(128, 384)
                        cf = causal[:, :, :].rearrange("p b n -> p (b n)")
                        ins = V.tensor_tensor_reduce(out=masked[:, m, cs], in0=pair[:, m, cs], in1=cf[:, cs], scale=1.0,
                                                     scalar=-3e38, op0=ALU.add, op1=ALU.max,
                                                     accum_out=s_max[:, 2 * m + qt:2 * m + qt + 1])
                        ins.then_inc(s_read, 1)
                dve.wait_ge(s_read, 4 * h + 4)
                V.tensor_scalar(n_bias, s_max, -SCALE, None, ALU.mult).then_inc(nmax, 1)

            for p in range(2, 14):
                if p == 13:
                    V.tensor_scalar(lam_sum, lam_sum, 1.0, None, ALU.mult).then_inc(nmax, 1)
                    maxima(0)
                if p % 2 and 2 <= p // 2 <= 4:
                    norm_qk(p // 2)
                ssm_slot(p)
            dve.wait_ge(act_step, 3)
            step(V.tensor_tensor(neg_lam, lam_exp[:, 1:2], lam_exp[:, 0:1], ALU.subtract))
            step(V.tensor_scalar(neg_lam, neg_lam, LAMBDA_INIT, None, ALU.subtract))
            yf = yT.rearrange("p c n -> p (c n)")

            for h in range(HEADS):
                dve.wait_ge(p_ready, 4 * h + 4)
                step(V.reciprocal(p_rs, p_sum))
                step(V.tensor_scalar(p_c1, p_rs[:, 2:4], neg_lam, None, ALU.mult))
                if h >= 1:
                    dve.wait_ge(aT_ps, h)
                for qt in range(2):
                    cs = slice(0, 128) if qt == 0 else slice(128, 384)
                    mark(V.tensor_scalar(a_mix[:, cs], probs[:, 1, cs], p_c1[:, qt:qt + 1], None, ALU.mult))
                sync()
                for qt in range(2):
                    cs = slice(0, 128) if qt == 0 else slice(128, 384)
                    V.scalar_tensor_tensor(a_mix[:, cs], probs[:, 0, cs], p_rs[:, qt:qt + 1], a_mix[:, cs], ALU.mult,
                                           ALU.add).then_inc(a_ready, 1)
                if h + 1 < HEADS:
                    maxima(h + 1)
                ssm_slot(14 + h)
                if h == HEADS - 2:
                    ssm_out(3)
                    dve.wait_ge(y_read, 4)
                    step(mul(glu_a, yf, yf))
                    step(V.tensor_scalar(glu_a, glu_a, 0.044715, 1.0, ALU.mult, ALU.add))
                    mul(glu_a, glu_a, yf).then_inc(gel_in, 1)
            dve.wait_ge(gel_sig, 1)
            mul(zT[:, :, :].rearrange("p c n -> p (c n)"), yf, glu_g).then_inc(z_ready, 1)
            dve.wait_ge(o_std, 1)
            step(V.reciprocal(o_rs, o_rs))
            for tt in range(TT):
                o3 = o_tok[:, tt, :].rearrange("p (h n) -> p h n", h=HEADS)
                mul(o3, o3, o_rs[:, 8 * tt:8 * tt + 8].unsqueeze(2).to_broadcast([P, HEADS, P])).then_inc(o_norm, 1)
            dve.wait_ge(glu_sig, 4)
            zf = zT[:, :, :].rearrange("p c n -> p (c n)")
            mul(zf, zf, glu_g).then_inc(sout_ready, 1)
            for i, (attn, n, kh) in enumerate(BRANCH):
                if attn and kh == 0:
                    continue
                cols = slice(N * n, N * n + N)
                dve.wait_ge(gates_sig, 2 - attn)
                dve.wait_ge(piece_used, P_BRANCH + i + 1)
                for tt in range(TT):
                    g = sg[:, attn, tt, cols]
                    mul(g, g, branch_bank(attn, n)[tt]).then_inc(merged_s, 1)
                if not attn:
                    dve.wait_ge(merged_s, 4 + 6 * n)
                    for tt in range(TT):
                        V.tensor_tensor(merged[:, tt, cols], sg[:, 0, tt, cols], sg[:, 1, tt, cols],
                                        ALU.add).then_inc(merged_s, 1)
            for n in range(2):
                for tt in range(TT):
                    if (n, tt) == (1, 0):
                        dve.wait_ge(x1_first, 1)
                    else:
                        dve.wait_ge(piece_used, P_WOUT + 3 + n)
                    ps = (pair, bank01)[n][:, tt, :]
                    xs = x_acc[:, tt, N * n:N * n + N]
                    V.tensor_tensor(xs, xs, ps, ALU.add).then_inc(x1_ready, 1)
            dve.wait_ge(x1_ready, 4)
            for tt in range(TT):
                mark(V.tensor_tensor_reduce(out=sg[:, 1, tt, N:2 * N], in0=x_acc[:, tt, N:2 * N],
                                            in1=x_acc[:, tt, N:2 * N], scale=1.0, scalar=0.0, op0=ALU.mult, op1=ALU.add,
                                            accum_out=x1_parts[:, 2 + tt:3 + tt]))
            sync()
            dve.wait_ge(x1_sq, 2)
            V.tensor_tensor(x_ss, x1_parts[:, 0:2], x1_parts[:, 2:4], ALU.add).then_inc(x1_ss, 1)
            dve.wait_ge(x1_std, 1)
            step(V.reciprocal(x_rs, x_std))
            logit, ex, gt, eq, cum, pick, misc = [route[:, i, :, :] for i in range(7)]
            rank_m, gate = gt, ex
            dve.wait_ge(logit_ps, 1)
            for tt in range(TT):
                mark(V.scalar_tensor_tensor(logit[:, tt, :], pair[:, tt, 0:E], x_rs[:, tt:tt + 1], misc[:, 0, :], ALU.mult,
                                            ALU.add))
            sync()
            for tt in range(TT):
                mark(V.max(top8[:, tt, :], logit[:, tt, :]))
            sync()
            for tt in range(TT):
                V.tensor_scalar(neg_top[:, tt:tt + 1], top8[:, tt, 0:1], -1.0, None, ALU.mult).then_inc(top_ready, 1)
            for tt in range(TT):
                least = top8[:, tt, 3:4]
                mark(V.tensor_scalar(gt[:, tt, :], logit[:, tt, :], least, 0.0, ALU.is_gt, ALU.add,
                                     accum_out=over[:, tt:tt + 1]))
                mark(V.tensor_scalar(eq[:, tt, :], logit[:, tt, :], least, None, ALU.is_equal))
            sync()
            mark(V.tensor_scalar(need, over, -1.0, 4.0, ALU.mult, ALU.add))
            for tt in range(TT):
                mark(V.tensor_tensor_scan(cum[:, tt, :], ones[:, 0:E], eq[:, tt, :], 0.0, ALU.mult, ALU.add))
            sync()
            for tt in range(TT):
                mark(V.scalar_tensor_tensor(pick[:, tt, :], cum[:, tt, :], need[:, tt:tt + 1], eq[:, tt, :], ALU.is_le, ALU.mult))
            sync()
            V.tensor_tensor(pick, pick, gt, ALU.add).then_inc(picked, 1)
            for tt in range(TT):
                V.tensor_scalar(h2[:, tt, :], x_acc[:, tt, :], x_rs[:, tt:tt + 1], None, ALU.mult).then_inc(h2_ready, 1)
            dve.wait_ge(picked, 1)
            dve.wait_ge(gexp, 2)
            for tt in range(TT):
                mark(V.tensor_tensor_reduce(out=ex[:, tt, :], in0=ex[:, tt, :], in1=pick[:, tt, :], scale=1.0, scalar=0.0,
                                            op0=ALU.mult, op1=ALU.add, accum_out=g_sum[:, tt:tt + 1]))
            sync()
            step(V.reciprocal(g_rs, g_sum))
            for tt in range(TT):
                V.tensor_scalar(gate[:, tt, :], ex[:, tt, :], g_rs[:, tt:tt + 1], None, ALU.mult).then_inc(gates_ready, 1)
            dve.wait_ge(gates_ready, 2)
            dve.wait_ge(rank_ps, 1)
            step(V.scalar_tensor_tensor(rank_m, y_bank[:, 0:2 * E].rearrange("p (t e) -> p t e", t=TT), 1.0, pick, ALU.add,
                                        ALU.mult))
            mark(V.tensor_scalar(rank_m, rank_m, 1.0, None, ALU.subtract))
            counts = cum[:, 0, :]
            V.tensor_copy(counts, y_bank[:, 2 * E:3 * E]).then_inc(picked, 1)
            dve.wait_ge(picked, 2)
            sync()

            def slot_columns(es, bases):
                for x in range(2):
                    for tt in range(TT):
                        yield (tt, slice(SLOT * x, SLOT * x + SLOT), iota[:, bass.ds(bases[x], SLOT)],
                               rank_m[:, tt, bass.ds(es[x], 1)], gate[:, tt, bass.ds(es[x], 1)])

            def select(i, es, bases):
                if not is_first(i):
                    dve.wait_ge(xg_ps, i)
                for tt, cols, at, rank, _ in slot_columns(es, bases):
                    V.tensor_scalar(sel[:, tt, cols], at, rank, None, ALU.is_equal).then_inc(sel_ready, 1)

            def take_x(i):
                for b in range(2):
                    dve.wait_ge(xg_ps, 2 * i + b + 1)
                    mul(xT[:, 4 * b:4 * b + 4, :], ps_xg[b][:, :].rearrange("p (k n) -> p k n", k=4),
                        pcol[:, G2 + 4 * b:G2 + 4 * b + 4].unsqueeze(2).to_broadcast([P, 4, P])).then_inc(xT_ready, 1)

            def add_block(i, c, turn):
                dve.wait_ge(comb_ps, 2 * i + turn + 3)
                acc = x_acc[:, :, N * c:N * c + N]
                if c == 1:
                    V.tensor_tensor(acc, acc, pair[:, :, :], ALU.add).then_inc(added, 1)
                    return
                V.tensor_tensor(acc[:, 0, :], acc[:, 0, :], ps_xg[0][:, :], ALU.add).then_inc(added_half, 1)
                V.tensor_tensor(acc[:, 1, :], acc[:, 1, :], ps_xg[1][:, :], ALU.add).then_inc(added, 1)
                dve.wait_ge(added_half, i + 2)

            def block_work(i, es, bases, first, last):
                if not last:
                    select(i + 1, (2 * i + 2, 2 * i + 3), (0, 0))
                if not is_first(i):
                    dve.wait_ge(put_ps, i)
                for tt, cols, at, rank, g in slot_columns(es, bases):
                    V.tensor_scalar(sel_g[:, tt, cols], at, rank, g, ALU.is_equal, ALU.mult).then_inc(selg_ready, 1)
                for b in range(2):
                    if b == 0:
                        dve.wait_ge(hid_ps, i + 1)
                    else:
                        dve.wait_ge(w1_used, (i + 1) * W1P)
                    hid = (bank01, bank23)[b][:, :, :].rearrange("p b (n w) -> p b n w", w=2)
                    ga, ua = (v[:, N * b:N * b + N].rearrange("p (b n) -> p b n", b=2) for v in (g_act, u_act))
                    V.tensor_scalar(ga, hid[:, :, :, 0], 7.0, None, ALU.min).then_inc(g_ready, 1)
                    V.tensor_scalar(ua, hid[:, :, :, 1], 7.0, -7.0, ALU.min, ALU.max).then_inc(hid_read, 1)
                for b in range(2):
                    cols = slice(N * b, N * b + N)
                    dve.wait_ge(g_ready, 2 * i + b + 1)
                    dve.wait_ge(hid_read, 2 * i + b + 1)
                    V.scalar_tensor_tensor(u_act[:, cols], u_act[:, cols], 1.0, g_act[:, cols], ALU.add,
                                           ALU.mult).then_inc(um_ready, 1)
                for b in range(2):
                    cols = slice(N * b, N * b + N)
                    dve.wait_ge(um_ready, 2 * i + b + 1)
                    dve.wait_ge(sig_ready, 2 * i + b + 1)
                    mul(u_act[:, cols], u_act[:, cols], s_act[:, cols]).then_inc(act_ready, 1)
                if not last:
                    take_x(i + 1)
                if not first:
                    add_block(i - 1, 1, 0)
                    add_block(i - 1, 0, 1)

            select(0, (0, 1), (0, 0))
            take_x(0)
            block_work(0, (0, 1), (0, 0), False, False)
            for c in range(3):
                mark(V.tensor_scalar(flag[:, E * c:E * c + E], counts[0:1, :], float(SLOT * (c + 1)), None, ALU.is_gt))
                mark(V.memset(flag_b[:, E * c:E * c + E], float(SLOT * (c + 1) - NO_SLOT)))
            sync()
            step(V.tensor_tensor_scan(flag_pos, ones[0:1, 0:96], flag, 0.0, ALU.mult, ALU.add))
            step(V.tensor_scalar(table_f[:, 0:1], flag_pos[:, 95:96], 0.5, 0.25, ALU.mult, ALU.add))
            step(V.tensor_scalar(table_f[:, 0:1], table_f[:, 0:1], MAGIC, None, ALU.add))
            mark(V.tensor_scalar(table_f[:, 0:1], table_f[:, 0:1], MAGIC, None, ALU.subtract))
            mark(V.tensor_copy(table_f[:, 1:2], flag_pos[:, 95:96]))
            mark(mul(flag_e.rearrange("p (c e) -> p c e", c=3), flag.rearrange("p (c e) -> p c e", c=3),
                     iota[0:1, 0:E].unsqueeze(1).to_broadcast([1, 3, E])))
            mark(mul(flag_b, flag_b, flag))
            sync()
            step(V.tensor_tensor(flag_pos, flag_pos, flag, ALU.subtract))
            for w_, at in ((flag_e, 2), (flag_b, 2 + MAX_EXTRA)):
                step(V.tensor_tensor(big, flag_pos.unsqueeze(1).to_broadcast([1, MAX_EXTRA, 96]),
                                     iota[0:1, 0:MAX_EXTRA].unsqueeze(2).to_broadcast([1, MAX_EXTRA, 96]), ALU.is_equal))
                step(mul(big, big, w_.unsqueeze(1).to_broadcast([1, MAX_EXTRA, 96])))
                step(V.tensor_reduce(table_f[:, at:at + MAX_EXTRA], big, AX.X, ALU.add))
            at = 2 + MAX_EXTRA
            step(V.tensor_scalar(table_f[:, at:at + MAX_EXTRA], table_f[:, at:at + MAX_EXTRA], float(NO_SLOT), None, ALU.add))
            V.tensor_copy(table[:, :], table_f).then_inc(table_ready, 1)

            with dve.Fori(1, NB - 1) as i:
                block_work(i, (2 * i, 2 * i + 1), (0, 0), False, False)
            block_work(NB - 1, (E - 2, E - 1), (0, 0), False, True)
            add_block(NB - 1, 0, 0)
            add_block(NB - 1, 1, 1)
            dve.wait_ge(table_ready, 1)
            extra = dve.value_load(table[0:1, 0:1], min_val=0, max_val=MAX_EXTRA // 2)
            with dve.If(extra > 0):
                with dve.Fori(0, extra) as j:
                    es = [dve.value_load(table[0:1, bass.ds(2 * j + 2 + x, 1)], min_val=0, max_val=E - 1) for x in range(2)]
                    bases = [dve.value_load(table[0:1, bass.ds(2 * j + 2 + MAX_EXTRA + x, 1)], min_val=0, max_val=NO_SLOT)
                             for x in range(2)]
                    i = j + NB
                    select(i, es, bases)
                    take_x(i)
                    block_work(i, es, bases, True, True)
                    add_block(i, 0, 0)
                    add_block(i, 1, 1)

        @block.tensor
        def _(pe):
            T = nc.tensor
            pe.wait_ge(consts, 1)
            pe.wait_ge(h_ready, 2)
            for b in range(4):
                for k in (2 * b, 2 * b + 1):
                    for tt in range(TT):
                        ins = T.transpose(bank[b][:, S * (k % 2) + P * tt:S * (k % 2) + P * tt + P],
                                          h_tok[:, tt, P * k:P * k + P], ident[:, :])
                ins.then_inc(hT_ps, 1)
                if b == 1:
                    pe.wait_ge(prow_ready, 1)
                    T.transpose(t_bank[:, 0:P], prow[:, :], ident[:, :]).then_inc(pcol_ps, 1)

            def ssm_matrices():
                pe.wait_ge(bc_in, 16 * 12)
                pe.wait_ge(c_im_in, 16 * 8)
                for r in range(2):
                    for ct in range(CT):
                        ins = T.transpose(bank23[:, r, P * ct:P * ct + P],
                                          b_raw[:, r, 4 * ct:4 * ct + 4, :].rearrange("p j c -> p (j c)"), ident[:, :])
                    ins.then_inc(b_ps, 1)
                pe.wait_ge(pcol_ready, 1)
                for r, ps in enumerate((t_bank, y_bank)):
                    for ct in range(CT):
                        ins = T.transpose(ps[:, P * ct:P * ct + P], c_raw[:, r, ct, :], ident[:, :])
                    ins.then_inc(c_ps, 1)

            def piece(i):
                pe.wait_ge(piece_in[i % 4], 16 * (i // 4 + 1))
                return ring[:, STREAM + i % 4, :].rearrange("p (k n) -> p k n", k=4)

            def products(i, lhs, k0, outs, start, stop, between=None):
                w_ = piece(i)
                for tt in range(TT):
                    if tt == 1 and between:
                        ins.then_inc(x1_first, 1)
                        between()
                    for k in range(4):
                        ins = T.matmul(outs[tt], lhs[:, k0 + k, P * tt:P * tt + P], w_[:, k, :], start=start and k == 0,
                                       stop=stop and k == 3)
                ins.then_inc(piece_used, 1)

            def in_piece(i):
                c = i // 2
                if i % 2 == 0:
                    if c == 2:
                        pe.wait_ge(chunk_read, 2)
                    elif c in (3, 4, 5, 6):
                        pe.wait_ge(qk_n, 2 * (c - 2))
                    elif c > 6:
                        pe.wait_ge(chunk_read, 2 * (c - 4))
                ps = chunk_bank(c)
                products(i, hT, 4 * (i % 2), [ps[:, 0, :], ps[:, 1, :]], i % 2 == 0, i % 2 == 1)

            def transposes(c):
                pe.wait_ge(qk_n, 2 * c)
                for r in range(2):
                    pe.wait_ge(t_read, 2 * c + r - 1)
                    for hh in range(2):
                        for tt in range(TT):
                            ins = T.transpose((t_bank, y_bank)[r][:, S * hh + P * tt:S * hh + P * tt + P],
                                              qn[:, tt, P * (2 * r + hh):P * (2 * r + hh) + P], ident[:, :])
                    ins.then_inc(t_ps, 1)

            def inputs(j):
                ct, jj = j // 4, j % 4
                if j >= 1:
                    pe.wait_ge(bu_read, j)
                else:
                    pe.wait_ge(t_read, 2)
                    pe.wait_ge(bT_ready, 2)
                for r in range(2):
                    ins = T.matmul(bu_bank[:, S * r:S * r + S], bT[32 * jj:32 * jj + 32, ct, r, :],
                                   uT[32 * jj:32 * jj + 32, ct, :], start=True, stop=True, tile_position=(32 * jj, 0))
                ins.then_inc(bu_ps, 1)

            def outputs(j):
                ct, jj = j // 4, j % 4
                pe.wait_ge(xs_ready, j + 1)
                if j == 0:
                    pe.wait_ge(cT_ready, 2)
                if jj == 0 and ct >= 1:
                    pe.wait_ge(y_read, ct)
                for r in range(2):
                    ins = T.matmul(yo_bank[32 * jj:32 * jj + 32, S * (ct % 2):S * (ct % 2) + S], cT[:, r, j, :],
                                   x_state[:, j % 2, r, :], start=(r == 0), stop=(r == 1), tile_position=(0, 32 * jj))
                ins.then_inc(y_ps, 1)

            def ssm_slot(p):
                if p in SSM_AT:
                    j = SSM_AT[p]
                    inputs(j)
                    if j >= 2:
                        outputs(j - 2)

            def scores(h):
                if h == 0:
                    pe.wait_ge(t_read, 10)
                    pe.wait_ge(chunk_read, 4)
                else:
                    pe.wait_ge(s_read, 4 * h)
                for qt in range(2):
                    for m in range(2):
                        a = slice(64 * m, 64 * m + 64)
                        ins = T.matmul(pair[:, m, 128 * qt:128 * qt + 128 * (qt + 1)], qT[a, h, P * qt:P * qt + P],
                                       kT[a, h, 0:P * (qt + 1)], start=(qt == 0), stop=True, tile_position=(64 * m, 0),
                                       skip_group_check=True)
                ins.then_inc(s_ps, 1)

            for p in range(14):
                if p < 2:
                    pe.wait_ge(hT_dve, 2 * p + 2)
                    pe.wait_ge(hT_act, 2 * p + 2)
                in_piece(p)
                if p == 1:
                    ssm_matrices()
                if p == 2:
                    pe.wait_ge(chunk_read, 2)
                    pe.wait_ge(c_read, 2)
                    for ps, c0 in ((t_bank, 0), (y_bank, 2)):
                        for ct in (c0, c0 + 1):
                            for tt in range(TT):
                                ins = T.transpose(ps[:, S * (ct - c0) + P * tt:S * (ct - c0) + P * tt + P],
                                                  u_tok[:, tt, P * ct:P * ct + P], ident[:, :])
                        ins.then_inc(t_ps, 1)
                if p % 2 == 0 and 2 <= p // 2 <= 5:
                    transposes(p // 2 - 1)
                ssm_slot(p)
                if p == 12:
                    scores(0)

            def mix(h):
                pe.wait_ge(a_ready, 2 * h + 2)
                if h >= 1:
                    pe.wait_ge(aT_ready, h)
                for b in range(3):
                    ins = T.transpose(t_bank[:, P * b:P * b + P], a_mix[:, P * b:P * b + P], ident[:, :])
                ins.then_inc(aT_ps, 1)

            def values(h):
                pe.wait_ge(aT_ready, h + 1)
                if h == 0:
                    pe.wait_ge(chunk_read, 6)
                else:
                    pe.wait_ge(o_read, 4 * h)
                hs = slice(P * h, P * h + P)
                T.matmul(y_bank[:, 0:P], aT[:, 0, :], v_tok[:, 0, hs], start=True, stop=True)
                T.matmul(y_bank[:, P:2 * P], aT[:, 1, :], v_tok[:, 0, hs], start=True, stop=False)
                T.matmul(y_bank[:, P:2 * P], aT[:, 2, :], v_tok[:, 1, hs], start=False, stop=True).then_inc(o_ps, 1)

            for h in range(HEADS):
                in_piece(14 + h)
                mix(h)
                if h + 1 < HEADS:
                    scores(h + 1)
                values(h)
                ssm_slot(14 + h)
                if h == HEADS - 2:
                    outputs(NST - 2)
                    outputs(NST - 1)
            pe.wait_ge(z_ready, 1)
            w_ = piece(P_GLU)
            for co in range(CT):
                for k in range(CT):
                    ins = T.matmul(pair[:, co // 2, S * (co % 2):S * (co % 2) + S], w_[:, k, P * co:P * co + P], zT[:, k, :],
                                   start=(k == 0), stop=(k == 3))
                if co == 1:
                    ins.then_inc(glu_ps, 1)
            ins.then_inc(piece_used, 1)
            pe.wait_ge(o_norm, 2)
            pe.wait_ge(y_read, 4)
            pe.wait_ge(chunk_read, 14)
            for b in range(4):
                for h in (2 * b, 2 * b + 1):
                    for tt in range(TT):
                        ins = T.transpose(bank[b][:, S * (h % 2) + P * tt:S * (h % 2) + P * tt + P],
                                          o_tok[:, tt, P * h:P * h + P], ident[:, :])
                ins.then_inc(oT_ps, 1)

            def turn_merged(half):
                pe.wait_ge(merged_s, 6 * half + 6)
                for b in (2 * half, 2 * half + 1):
                    for k in (2 * b, 2 * b + 1):
                        for tt in range(TT):
                            ins = T.transpose(bank[b][:, S * (k % 2) + P * tt:S * (k % 2) + P * tt + P],
                                              merged[:, tt, P * k:P * k + P], ident[:, :])
                    ins.then_inc(mT_ps, 1)

            for i, (attn, n, kh) in enumerate(BRANCH):
                if attn:
                    pe.wait_ge(oT_ready, 2 * kh + 2 if n == 0 else 4)
                else:
                    pe.wait_ge(sout_ready, 1)
                products(P_BRANCH + i, oT if attn else zT, 4 * kh, branch_bank(attn, n), kh == 0, kh == 1 or not attn)
                if i == 3:
                    turn_merged(0)

            def turn_x1(half):
                pe.wait_ge(x1_ready, 2 * half + 2)
                for b in range(2):
                    for kk in range(2):
                        k = 4 * half + 2 * b + kk
                        for tt in range(TT):
                            ps = bank23[:, b, :] if half == 0 else (t_bank, y_bank)[b]
                            ins = T.transpose(ps[:, S * kk + P * tt:S * kk + P * tt + P], x_acc[:, tt, P * k:P * k + P],
                                              ident[:, :])
                    ins.then_inc(h2T_ps, 1)

            def router(half):
                pe.wait_ge(h2T_ready, 4 * half + 4)
                for tt in range(TT):
                    for k in range(4 * half, 4 * half + 4):
                        ins = T.matmul(pair[:, tt, 0:E], hT[:, k, P * tt:P * tt + P], w_r[:, k, :], start=(k == 0),
                                       stop=(k == KT - 1))
                return ins

            def w_out_products(kh, n, turn=None):
                products(P_WOUT + 2 * kh + n, hT, 4 * kh, [(pair, bank01)[n][:, tt, :] for tt in range(TT)], kh == 0, kh == 1,
                         turn)

            pe.wait_ge(mT_ready, 2)
            w_out_products(0, 0)
            turn_merged(1)
            w_out_products(0, 1)
            pe.wait_ge(mT_ready, 4)
            w_out_products(1, 0)
            w_out_products(1, 1, lambda: turn_x1(0))
            router(0)
            turn_x1(1)
            router(1).then_inc(logit_ps, 1)
            pe.wait_ge(picked, 1)
            pick = route[:, 5, :, :]
            T.matmul(y_bank[:, 0:E], before[:, :], pick[:, 0, :], start=True, stop=True)
            T.matmul(y_bank[:, E:2 * E], ones[:, :], pick[:, 0, :], start=True, stop=False)
            T.matmul(y_bank[:, E:2 * E], before[:, :], pick[:, 1, :], start=False, stop=True)
            T.matmul(y_bank[:, 2 * E:3 * E], ones[:, :], pick[:, 0, :], start=True, stop=False)
            T.matmul(y_bank[:, 2 * E:3 * E], ones[:, :], pick[:, 1, :], start=False, stop=True).then_inc(rank_ps, 1)
            pe.wait_ge(gates_ready, 2)
            for tt in range(TT):
                ins = T.transpose(pair[0:E, 0, P * tt:P * tt + P], route[:, 1, tt, :], ident[:, :])
            ins.then_inc(gT_ps, 1)

            def gather(i):
                pe.wait_ge(sel_ready, 4 * i + 4)
                for b in range(2):
                    for k in range(4):
                        for tt in range(TT):
                            ins = T.matmul(ps_xg[b][:, P * k:P * k + P], h2[:, tt, P * (4 * b + k):P * (4 * b + k) + P],
                                           sel[:, tt, :], start=(tt == 0), stop=(tt == 1))
                    ins.then_inc(xg_ps, 1)

            def combine(i, c):
                bias = isinstance(i, int) and i < 0
                if bias:
                    pe.wait_ge(gT_ready, 1)
                    pe.wait_ge(b2_in, 16)
                else:
                    pe.wait_ge(y_ready, 2 * i + 1 + c)
                    pe.wait_ge(put_ready, i + 1)
                for tt in range(TT):
                    ps = ps_xg[tt][:, :] if c == 0 else pair[:, tt, :]
                    tokens, cols = slice(P * tt, P * tt + P), slice(N * c, N * c + N)
                    if bias:
                        ins = T.matmul(ps, gateT[:, tokens], b2_sb[:, cols], start=True, stop=True)
                    else:
                        ins = T.matmul(ps, put[:, tokens], y_sb[:, cols], start=True, stop=True)
                ins.then_inc(comb_ps, 1)

            pe.wait_ge(h2_ready, 2)
            gather(0)

            def block_work(i, odd, first, last):
                later = not is_first(i)
                pe.wait_ge(xT_ready, 2 * i + 1)
                if later:
                    pe.wait_ge(hid_read, 2 * i)
                    pe.wait_ge(actT_ready, 2 * i)
                    pe.wait_ge(put_ready, i)
                hid = [bank01[:, 0, :], bank01[:, 1, :], bank23[:, 0, :], bank23[:, 1, :]]
                halves = [slice(0, SLOT), slice(SLOT, 2 * SLOT)]
                for k in range(W1P):
                    if k == (W1P // 2 if later else W1P - 1):
                        pe.wait_ge(b1_in, (i + 1) * 32)
                        for n in range(4):
                            for x, h in enumerate(halves):
                                row = slice(32 * x, 32 * x + 1)
                                T.matmul(hid[n][h, :], ones[row, 0:SLOT], b1_rows[row, N * n:N * n + N], start=False, stop=False,
                                         tile_position=(32 * x, SLOT * x))
                    if k == W1P // 2:
                        pe.wait_ge(xT_ready, 2 * i + 2)
                    pe.wait_ge(w1_in[k], (i + 1) * 32)
                    for n in range(4):
                        for x, h in enumerate(halves):
                            ins = T.matmul(hid[n][h, :], xT[:, k, h], w1_piece(i, k, x, odd)[:, N * n:N * n + N],
                                           start=(k == 0), stop=(k == W1P - 1))
                        if k == W1P - 1 and n == 1:
                            ins.then_inc(hid_ps, 1)
                    ins.then_inc(w1_used, 1)
                if not last:
                    if later:
                        pe.wait_ge(added, 2 * i)
                    gather(i + 1)
                if not first:
                    combine(i - 1, 1)
                for b in range(2):
                    pe.wait_ge(act_ready, 2 * i + b + 1)
                    if b == 0:
                        pe.wait_ge(hid_read, 2 * i + 2)
                    for f in range(4):
                        cols = slice(N * b + P * f, N * b + P * f + P)
                        ins = T.transpose(ps_act[:, b, P * f:P * f + P], u_act[:, cols], ident[:, :])
                    ins.then_inc(actT_ps, 1)
                pe.wait_ge(selg_ready, 4 * i + 4)
                for tt in range(TT):
                    ins = T.transpose(ps_put[:, P * tt:P * tt + P], sel_g[:, tt, :], ident[:, :])
                ins.then_inc(put_ps, 1)
                if not first:
                    if last:
                        pe.wait_ge(added, 2 * i)
                    else:
                        pe.wait_ge(xT_ready, 2 * i + 4)
                    combine(i - 1, 0)
                pe.wait_ge(added, 2 * i + 1)
                for m in range(W2P):
                    if m % 2 == 0:
                        pe.wait_ge(actT_ready, 2 * i + m // 2 + 1)
                    pe.wait_ge(w2_in[m], (i + 1) * 32)
                    for c in range(2):
                        for f in (2 * m, 2 * m + 1):
                            for x, h in enumerate(halves):
                                ins = T.matmul(ps_y[h, c, :], actT[:, f, h], w2_piece(i, m, x, odd)[:, f % 2, N * c:N * c + N],
                                               start=(f == 0), stop=(f == KT - 1))
                        if (m, c) == (W2P - 1, 0):
                            ins.then_inc(out_ps, 1)
                    ins.then_inc(w2_used, 1)

            block_work(0, 0, False, False)
            with pe.Fori(1, NB - 1, 2) as i:
                block_work(i, 1, False, False)
                block_work(i + 1, 0, False, False)
            block_work(NB - 1, 1, False, True)
            pe.wait_ge(added, 2 * NB)
            combine(NB - 1, 0)
            combine(NB - 1, 1)
            pe.wait_ge(table_ready, 1)
            extra = pe.value_load(table[0:1, 0:1], min_val=0, max_val=MAX_EXTRA // 2)
            with pe.If(extra > 0):
                with pe.Fori(0, extra) as j:
                    i = j + NB
                    pe.wait_ge(added, 2 * i + 2)
                    gather(i)
                    block_work(i, 0, True, True)
                    combine(i, 0)
                    combine(i, 1)


_INS = ["x", "norm1_gain", "w_in", "lambda_re", "lambda_im", "log_dt", "ssm_b_re", "ssm_b_im", "ssm_c_re", "ssm_c_im",
        "ssm_d", "w_glu", "b_glu", "q_norm_gain", "k_norm_gain", "lambda_q1", "lambda_k1", "lambda_q2", "lambda_k2",
        "subln_gain", "w_proj_ssm", "w_proj_attn", "w_out", "norm2_gain", "w_router", "b_router", "w_exp1", "b_exp1",
        "w_exp2", "b_exp2"]


def kernel(**inputs):
    import numpy as _np
    import concourse.bacc as _bacc
    from concourse import mybir as _mybir
    from concourse.bass_utils import run_bass_kernel_spmd as _run

    nc = _bacc.Bacc("TRN2", target_bir_lowering=False, num_devices=1)
    arrays, tensors = {}, {}
    for name in _INS:
        a = _np.ascontiguousarray(inputs[name])
        arrays[f"in_{name}"] = a
        tensors[name] = nc.dram_tensor(f"in_{name}", a.shape, _mybir.dt.from_np(a.dtype), kind="ExternalInput").ap()
    out = nc.dram_tensor("out", (1, S, D), _mybir.dt.from_np(_np.dtype("float32")), kind="ExternalOutput").ap()
    hybrid_block(nc, tensors, out)
    r = _run(nc, [arrays], core_ids=[0])
    return r.results[0]["out"]
```
